# Optimizing a Trainium2 kernel written in Bass

```python
import math
import jax
import jax.numpy as jnp
from jax import lax
import numpy as np

D_MODEL = 1024
BATCH = 1
SEQ = 256
DEPTH = 2

GRID_W = 64
CTX_LEN = 256

BRANCH_WIDTH = D_MODEL // 2
N_BRANCH = 3
HEAD_DIM = 64
NA_HEADS = BRANCH_WIDTH // HEAD_DIM
NA_KH_MAX = 8
NA_KW = 16
ROPE_THETA = 10000.0
NEG_INF = -1e30
POOL_WINDOWS = (2, 4, 8, 16)
POOL_GROUPS = len(POOL_WINDOWS)
POOL_GROUP_DIM = BRANCH_WIDTH // POOL_GROUPS
HY_ORDER = 2
HY_SHORT = 3
HY_EMB_DIM = 33
HY_FILTER_HIDDEN = 64
HY_MIN_DECAY = math.log(1e-2) / 0.3
HY_MAX_DECAY = math.log(1e-2) / 1.5
N_EXPERTS = 16
N_GROUPS = 4
EXPERTS_PER_GROUP = N_EXPERTS // N_GROUPS
TOP_K = 2
EXPERT_FF = D_MODEL // 2
N_MOD = 6
RMS_EPS = 1e-6
POOL_OFF = 3 * BRANCH_WIDTH
HY_OFF = POOL_OFF + BRANCH_WIDTH
GATE_OFF = HY_OFF + (HY_ORDER + 1) * BRANCH_WIDTH
IN_WIDTH = GATE_OFF + N_BRANCH * D_MODEL

kernel_name = 'hybrid_natten_pool_hyena_moe_dit'

def rms_norm(x, g):
    xf = x.astype(jnp.float32)
    y = xf * lax.rsqrt(jnp.mean(xf * xf, axis=-1, keepdims=True) + RMS_EPS)
    return (y * g.astype(jnp.float32)).astype(x.dtype)

def modulate(h, shift, scale):
    return h * (1.0 + scale) + shift

def split_heads(t):
    b, n, _ = t.shape
    return t.reshape(b, n, NA_HEADS, HEAD_DIM).transpose(0, 2, 1, 3)

def merge_heads(t):
    b, h, n, d = t.shape
    return t.transpose(0, 2, 1, 3).reshape(b, n, h * d)

def axial_rope_tables(n_tokens):
    t = jnp.arange(n_tokens)
    row = (t // GRID_W).astype(jnp.float32)
    col = (t % GRID_W).astype(jnp.float32)
    n_freq = HEAD_DIM // 4
    inv = ROPE_THETA ** (-jnp.arange(n_freq, dtype=jnp.float32) / n_freq)
    ang = jnp.concatenate([row[:, None] * inv, col[:, None] * inv], axis=-1)
    return jnp.cos(ang), jnp.sin(ang)

def apply_rope(x, cos, sin):
    xf = x.astype(jnp.float32)
    x1, x2 = jnp.split(xf, 2, axis=-1)
    return jnp.concatenate([x1 * cos - x2 * sin, x1 * sin + x2 * cos], axis=-1).astype(x.dtype)

def neighbourhood_attention(q_rot, q_plain, k_rot, v, k_ctx, v_ctx, rpb):
    b, h, s, dh = q_rot.shape
    rows = s // GRID_W
    kh = min(NA_KH_MAX, rows)
    r = jnp.arange(rows)
    row_start = jnp.clip(r - kh // 2, 0, rows - kh)
    key_rows = row_start[:, None] + jnp.arange(kh)[None, :]
    j = jnp.arange(GRID_W)
    col_start = jnp.clip(j - NA_KW // 2, 0, GRID_W - NA_KW)
    col_mask = (j[None, :] >= col_start[:, None]) & (j[None, :] < col_start[:, None] + NA_KW)
    dr = key_rows - r[:, None] + NA_KH_MAX - 1
    dc = jnp.clip(j[None, :] - j[:, None], -(NA_KW - 1), NA_KW - 1) + NA_KW - 1
    bias = rpb.astype(jnp.float32)[:, dr[:, None, :, None], dc[None, :, None, :]]
    bias = jnp.where(col_mask[None, None, :, None, :], bias, NEG_INF)
    q_g = q_rot.reshape(b, h, rows, GRID_W, dh)
    qp_g = q_plain.reshape(b, h, rows, GRID_W, dh)
    k_g = k_rot.reshape(b, h, rows, GRID_W, dh)[:, :, key_rows]
    v_g = v.reshape(b, h, rows, GRID_W, dh)[:, :, key_rows]
    scale = dh ** -0.5
    s_lat = jnp.einsum('bhrqd,bhrikd->bhrqik', q_g, k_g, preferred_element_type=jnp.float32) * scale + bias
    s_ctx = jnp.einsum('bhrqd,bhcd->bhrqc', qp_g, k_ctx, preferred_element_type=jnp.float32) * scale
    n_lat = kh * GRID_W
    scores = jnp.concatenate([s_lat.reshape(b, h, rows, GRID_W, n_lat), s_ctx], axis=-1)
    p = jax.nn.softmax(scores, axis=-1).astype(v.dtype)
    p_lat = p[..., :n_lat].reshape(b, h, rows, GRID_W, kh, GRID_W)
    out = jnp.einsum('bhrqik,bhrikd->bhrqd', p_lat, v_g) + jnp.einsum('bhrqc,bhcd->bhrqd', p[..., n_lat:], v_ctx)
    return out.reshape(b, h, s, dh)

def context_attention(q, k, v):
    s = jnp.einsum('bhqd,bhkd->bhqk', q, k, preferred_element_type=jnp.float32) * (HEAD_DIM ** -0.5)
    p = jax.nn.softmax(s, axis=-1).astype(v.dtype)
    return jnp.einsum('bhqk,bhkd->bhqd', p, v)

def multiscale_pool(u, pool_w, pool_scale):
    b, n, _ = u.shape
    uf = u.astype(jnp.float32)
    csum = jnp.concatenate([jnp.zeros((b, 1, BRANCH_WIDTH), jnp.float32), jnp.cumsum(uf, axis=1)], axis=1)
    t = jnp.arange(n)
    groups = []
    for g, w in enumerate(POOL_WINDOWS):
        lo = jnp.maximum(t - w // 2, 0)
        hi = jnp.minimum(t + w - w // 2, n)
        sl = slice(g * POOL_GROUP_DIM, (g + 1) * POOL_GROUP_DIM)
        cs = csum[..., sl]
        mean = (cs[:, hi] - cs[:, lo]) / (hi - lo).astype(jnp.float32)[None, :, None]
        groups.append(mean - uf[..., sl])
    y = jnp.stack(groups, axis=2)
    y = jnp.einsum('blgc,gcd->blgd', y, pool_w.astype(jnp.float32)).reshape(b, n, BRANCH_WIDTH)
    return (y * pool_scale.astype(jnp.float32)).astype(u.dtype)

def depthwise_conv3(u, w, bias):
    y = lax.conv_general_dilated(u, w[:, None, :].astype(u.dtype), window_strides=(1,),
                                 padding=((HY_SHORT // 2, HY_SHORT // 2),),
                                 dimension_numbers=('NWC', 'WIO', 'NWC'),
                                 feature_group_count=u.shape[-1])
    return y + bias.astype(u.dtype)

def hyena_filter_spectrum(n, w1, b1, freq, w2, b2, w3):
    f32 = jnp.float32
    t = jnp.linspace(0.0, 1.0, n, dtype=f32)[:, None]
    bands = (HY_EMB_DIM - 1) // 2
    ang = (2.0 * math.pi / n) * jnp.arange(n, dtype=f32)[:, None]
    f = jnp.linspace(1e-4, bands - 1, bands, dtype=f32)[None, :]
    z = jnp.concatenate([t, jnp.cos(f * ang), -jnp.sin(f * ang)], axis=-1)
    fr = freq.astype(f32)
    hh = jnp.sin(fr * (z @ w1.astype(f32) + b1.astype(f32)))
    hh = jnp.sin(fr * (hh @ w2.astype(f32) + b2.astype(f32)))
    hh = (hh @ w3.astype(f32)).reshape(n, HY_ORDER, 2, BRANCH_WIDTH)
    deltas = jnp.abs(jnp.linspace(HY_MIN_DECAY, HY_MAX_DECAY, BRANCH_WIDTH, dtype=f32))
    hh = hh * jnp.exp(-t * deltas)[:, None, None, :]
    fwd, bwd = hh[:, :, 0], hh[:, :, 1]
    buf = jnp.concatenate([fwd, jnp.zeros((1, HY_ORDER, BRANCH_WIDTH), f32), bwd[:0:-1]], axis=0)
    buf = buf / jnp.sum(jnp.abs(buf), axis=0, keepdims=True)
    return jnp.fft.rfft(buf, axis=0)

def bidirectional_long_conv(u, h_spec, skip):
    n = u.shape[1]
    y = jnp.fft.irfft(jnp.fft.rfft(u, n=2 * n, axis=1) * h_spec[None], n=2 * n, axis=1)[:, :n]
    return y + u * skip

def hyena_mixer(u, short_w, short_b, w1, b1, freq, w2, b2, w3, skip):
    n = u.shape[1]
    uc = depthwise_conv3(u, short_w, short_b).astype(jnp.float32)
    v, x1, x2 = jnp.split(uc, HY_ORDER + 1, axis=-1)
    h_spec = hyena_filter_spectrum(n, w1, b1, freq, w2, b2, w3)
    z = v
    for o, gate in enumerate((x1, x2)):
        z = gate * bidirectional_long_conv(z, h_spec[:, o], skip[o].astype(jnp.float32))
    return z.astype(u.dtype)

def merge_branches(p, y_attn, pool_w, pool_scale, hy_params, w_branch, w_out):
    b, n, _ = p.shape
    y_pool = multiscale_pool(p[..., POOL_OFF:HY_OFF], pool_w, pool_scale)
    y_hy = hyena_mixer(p[..., HY_OFF:GATE_OFF], *hy_params)
    gates = jax.nn.sigmoid(p[..., GATE_OFF:].astype(jnp.float32)).reshape(b, n, N_BRANCH, D_MODEL)
    ys = jnp.stack([y_attn.astype(p.dtype), y_pool, y_hy], axis=2)
    br = jnp.einsum('blnc,ncd->blnd', ys, w_branch, preferred_element_type=jnp.float32)
    merged = jnp.sum(gates * br, axis=2).astype(p.dtype)
    return merged @ w_out

def token_mixers(hl, hc, w_in, rpb, pool_w, pool_scale, hy_params, w_branch, w_out, cos, sin, need_ctx):
    pl = hl @ w_in
    pc = hc @ w_in
    ql, kl, vl = [split_heads(t) for t in jnp.split(pl[..., :POOL_OFF], 3, axis=-1)]
    qc, kc, vc = [split_heads(t) for t in jnp.split(pc[..., :POOL_OFF], 3, axis=-1)]
    ya_l = neighbourhood_attention(apply_rope(ql, cos, sin), ql, apply_rope(kl, cos, sin), vl, kc, vc, rpb)
    out_l = merge_branches(pl, merge_heads(ya_l), pool_w, pool_scale, hy_params, w_branch, w_out)
    out_c = None
    if need_ctx:
        ya_c = context_attention(qc, kc, vc)
        out_c = merge_branches(pc, merge_heads(ya_c), pool_w, pool_scale, hy_params, w_branch, w_out)
    return out_l, out_c

def grouped_moe(h, w_router, router_bias, w_gate, w_up, w_down):
    aff = jax.nn.sigmoid((h @ w_router).astype(jnp.float32))
    biased = (aff + router_bias.astype(jnp.float32)).reshape(-1, N_GROUPS, EXPERTS_PER_GROUP)
    group_score = jnp.sum(lax.top_k(biased, TOP_K)[0], axis=-1)
    group = jnp.argmax(group_score, axis=-1)
    in_group = jnp.take_along_axis(biased, group[:, None, None], axis=1)[:, 0]
    local = lax.top_k(in_group, TOP_K)[1]
    expert = group[:, None] * EXPERTS_PER_GROUP + local
    wsel = jnp.take_along_axis(aff, expert, axis=-1)
    wsel = wsel / jnp.sum(wsel, axis=-1, keepdims=True)
    gates = jnp.einsum('tk,tke->te', wsel, jax.nn.one_hot(expert, N_EXPERTS, dtype=jnp.float32))
    out = jnp.zeros(h.shape, jnp.float32)
    for e in range(N_EXPERTS):
        hid = jax.nn.silu(h @ w_gate[e]) * (h @ w_up[e])
        out = out + gates[:, e:e + 1] * (hid @ w_down[e]).astype(jnp.float32)
    return out.astype(h.dtype)

def setup_inputs(seed: int = 0) -> dict:
    key = jax.random.key(seed)
    ks = iter(jax.random.split(key, 32))
    D = D_MODEL

    def nrm(shape, scale):
        return jax.random.normal(next(ks), shape, jnp.float32) * scale

    return {
        'x': nrm((BATCH, SEQ, D), 1.0),
        'c': nrm((BATCH, D), 1.0),
        'ctx': nrm((BATCH, CTX_LEN, D), 1.0),
        'c_ctx': nrm((D,), 1.0),
        'norm1_g': 1.0 + nrm((DEPTH, D), 0.02),
        'norm2_g': 1.0 + nrm((DEPTH, D), 0.02),
        'w_mod': nrm((DEPTH, D, N_MOD * D), 0.5 * D ** -0.5),
        'b_mod': nrm((DEPTH, N_MOD * D), 0.02),
        'w_in': nrm((DEPTH, D, IN_WIDTH), D ** -0.5),
        'rpb': nrm((DEPTH, NA_HEADS, 2 * NA_KH_MAX - 1, 2 * NA_KW - 1), 0.1),
        'pool_w': nrm((DEPTH, POOL_GROUPS, POOL_GROUP_DIM, POOL_GROUP_DIM), POOL_GROUP_DIM ** -0.5),
        'pool_scale': 1.0 + nrm((DEPTH, BRANCH_WIDTH), 0.02),
        'hy_short_w': nrm((DEPTH, HY_SHORT, (HY_ORDER + 1) * BRANCH_WIDTH), HY_SHORT ** -0.5),
        'hy_short_b': nrm((DEPTH, (HY_ORDER + 1) * BRANCH_WIDTH), 0.02),
        'hy_w1': nrm((DEPTH, HY_EMB_DIM, HY_FILTER_HIDDEN), HY_EMB_DIM ** -0.5),
        'hy_b1': nrm((DEPTH, HY_FILTER_HIDDEN), 0.02),
        'hy_freq': 1.0 + nrm((DEPTH, HY_FILTER_HIDDEN), 0.02),
        'hy_w2': nrm((DEPTH, HY_FILTER_HIDDEN, HY_FILTER_HIDDEN), HY_FILTER_HIDDEN ** -0.5),
        'hy_b2': nrm((DEPTH, HY_FILTER_HIDDEN), 0.02),
        'hy_w3': nrm((DEPTH, HY_FILTER_HIDDEN, HY_ORDER * 2 * BRANCH_WIDTH), HY_FILTER_HIDDEN ** -0.5),
        'hy_skip': nrm((DEPTH, HY_ORDER, BRANCH_WIDTH), 0.5),
        'w_branch': nrm((DEPTH, N_BRANCH, BRANCH_WIDTH, D), BRANCH_WIDTH ** -0.5),
        'w_out': nrm((DEPTH, D, D), D ** -0.5),
        'w_router': nrm((D, N_EXPERTS), D ** -0.5),
        'router_bias': nrm((N_EXPERTS,), 0.01),
        'w_gate_e': nrm((DEPTH, N_EXPERTS, D, EXPERT_FF), D ** -0.5),
        'w_up_e': nrm((DEPTH, N_EXPERTS, D, EXPERT_FF), D ** -0.5),
        'w_down_e': nrm((DEPTH, N_EXPERTS, EXPERT_FF, D), EXPERT_FF ** -0.5),
        'final_g': 1.0 + nrm((D,), 0.02),
    }

def reference(x, c, ctx, c_ctx, norm1_g, norm2_g, w_mod, b_mod, w_in, rpb, pool_w, pool_scale,
              hy_short_w, hy_short_b, hy_w1, hy_b1, hy_freq, hy_w2, hy_b2, hy_w3, hy_skip,
              w_branch, w_out, w_router, router_bias, w_gate_e, w_up_e, w_down_e, final_g):
    b, s, d = x.shape
    n_ctx = ctx.shape[1]
    cos, sin = axial_rope_tables(s)
    xl, xc = x, ctx
    for l in range(DEPTH):
        need_ctx = l < DEPTH - 1
        ml = (jax.nn.silu(c) @ w_mod[l] + b_mod[l]).reshape(b, 1, N_MOD, d)
        mc = (jax.nn.silu(c_ctx) @ w_mod[l] + b_mod[l]).reshape(1, 1, N_MOD, d)
        hl = modulate(rms_norm(xl, norm1_g[l]), ml[:, :, 0], ml[:, :, 1])
        hc = modulate(rms_norm(xc, norm1_g[l]), mc[:, :, 0], mc[:, :, 1])
        hy_params = (hy_short_w[l], hy_short_b[l], hy_w1[l], hy_b1[l], hy_freq[l],
                     hy_w2[l], hy_b2[l], hy_w3[l], hy_skip[l])
        out_l, out_c = token_mixers(hl, hc, w_in[l], rpb[l], pool_w[l], pool_scale[l], hy_params,
                                    w_branch[l], w_out[l], cos, sin, need_ctx)
        xl = xl + ml[:, :, 2] * out_l
        hl2 = modulate(rms_norm(xl, norm2_g[l]), ml[:, :, 3], ml[:, :, 4])
        if need_ctx:
            xc = xc + mc[:, :, 2] * out_c
            hc2 = modulate(rms_norm(xc, norm2_g[l]), mc[:, :, 3], mc[:, :, 4])
            tokens = jnp.concatenate([hl2.reshape(b * s, d), hc2.reshape(b * n_ctx, d)], axis=0)
            f = grouped_moe(tokens, w_router, router_bias, w_gate_e[l], w_up_e[l], w_down_e[l])
            xl = xl + ml[:, :, 5] * f[:b * s].reshape(b, s, d)
            xc = xc + mc[:, :, 5] * f[b * s:].reshape(b, n_ctx, d)
        else:
            f = grouped_moe(hl2.reshape(b * s, d), w_router, router_bias, w_gate_e[l], w_up_e[l], w_down_e[l])
            xl = xl + ml[:, :, 5] * f.reshape(b, s, d)
    return rms_norm(xl, final_g)


_drawn_inputs = setup_inputs


def setup_inputs(seed=0):
    import zlib

    import numpy as np

    out = dict(_drawn_inputs(seed))
    spreads = {}
    factors = {'norm1_g': 3.386,
     'rpb': 8.0,
     'pool_scale': 4.106,
     'hy_short_b': 4.305,
     'hy_b1': 8.0,
     'hy_freq': 8.0,
     'hy_b2': 5.263,
     'final_g': 7.777,
     'norm2_g': 3.848}
    for name, (base, spread) in spreads.items():
        noise = np.random.default_rng([zlib.crc32(name.encode()), seed]).standard_normal(out[name].shape)
        drawn = base * np.exp(spread * noise) if base else spread * noise
        out[name] = jnp.asarray(drawn.astype(out[name].dtype))
    for name, factor in factors.items():
        out[name] = (out[name] * factor).astype(out[name].dtype)
    return out
```

```python
from contextlib import ExitStack

import concourse.bass as bass
from concourse import mybir

P = 128
D = 1024
DK = D // P
SEQ = 256
CTX = 256
NT = SEQ + CTX
DEPTH = 2
BW = D // 2
BK = BW // P
HEADS = 8
DH = 64
GRID = 64
KW = 16
E_N = 16
FF = 512
FK = FF // P
N_MOD = 6
MOD_T = N_MOD * DK
NTAP = 3
HY_H = 64
HY_E = 33
HY_O = 2
EPS = 1e-6
RPB_W = 2 * KW - 1

F32 = mybir.dt.float32
U32 = mybir.dt.uint32
ALU = mybir.AluOpType
ACT = mybir.ActivationFunctionType
AX = mybir.AxisListType

RS = 6
RW = 2048
MOD_C = 24
IN_C = 14
MERGE_C = 18
OUT_C = 4
PRE_C = MOD_C + IN_C + MERGE_C + OUT_C
EXP_C = 6 * E_N
LAYER_C = PRE_C + EXP_C

C_G1, C_G2, C_BMOD = 0, 8, 16
C_PS = C_BMOD + MOD_T
C_TAP = C_PS + BK
C_SB = C_TAP + NTAP * 12
C_SKIP = C_SB + 12
C_FILT = C_SKIP + HY_O * BK
C_N = C_FILT + 3
IN_ORDER = [8, 9, 10, 11, 12, 13, 6, 7, 0, 1, 2, 3, 4, 5]
GATE_C0 = 14
POOL_PAD = 8
POOL_L = SEQ + 2 * POOL_PAD
TWO_PI = 6.283185307179586


def build(nc, a, out):
    ctx = ExitStack()
    with ctx:
        def sb(name, shape, dt=F32):
            return ctx.enter_context(nc.sbuf_tensor(name, shape, dt))

        def sem(name):
            return ctx.enter_context(nc.semaphore(name))

        def sems(name, n=DEPTH):
            return [sem(f"{name}{i}") for i in range(n)]

        def both(name):
            return [sem(name)] * DEPTH

        def tcols(l):
            return NT if l == 0 else SEQ

        def streams(l):
            return 2 if l == 0 else 1

        h_rows = [nc.dram_tensor(f"h_rows{l}", [NT, D], F32).ap() for l in range(DEPTH)]
        y_rows = [nc.dram_tensor(f"y_rows{l}", [E_N * tcols(l), D], F32).ap() for l in range(DEPTH)]
        slot_tok = [nc.dram_tensor(f"slot_tok{l}", [E_N * NT, 1], F32).ap() for l in range(DEPTH)]

        ring = sb("ring", [P, RS, RW])
        xT = sb("xT", [P, DK, NT])
        hT = sb("hT", [P, DK, NT])
        dft_f = sb("dft_f", [P, 2, 512])
        dft_i = sb("dft_i", [P, 4, SEQ])
        square = sb("square", [P, 4, P])
        ident, perm, tri, ones = (square[:, i, :] for i in range(4))
        rope = sb("rope", [P, 2, SEQ])
        colmask = sb("colmask", [P, GRID])
        edge = sb("edge", [P, BK, 16])
        nyq = sb("nyq", [P, 2])
        slot0 = sb("slot0", [P, E_N])
        tok_id = sb("tok_id", [P, 4])
        par = [sb(f"par{l}", [P, C_N]) for l in range(DEPTH)]
        fin_g = sb("fin_g", [P, DK])
        cc = sb("cc", [P, 4, DK * 2])
        poolw = sb("poolw", [P, BK, P])
        wrt = sb("wrt", [P, DK, E_N])
        rbias = sb("rbias", [P, E_N])
        mods = sb("mods", [P, MOD_T, 2])
        gs = sb("gs", [P, 2, DK, 2])
        half_gate = sb("half_gate", [P, DK, 2])
        small = sb("small", [P, 16])
        MIX = 26624
        mix = sb("mix", [P, MIX])

        def area(o, n):
            assert o + n <= MIX
            return mix[:, o:o + n]

        ys = area(0, 6144).rearrange("p (n c t) -> p n c t", n=3, c=BK)
        qT = ys[:, 0]
        ys_pool = ys[:, 1]
        hv = ys[:, 2]
        kT = area(6144, 2048).rearrange("p (c t) -> p c t", c=BK)
        vtok = area(8192, 2048).rearrange("p (j f) -> p j f", j=4)
        hx = area(10240, 4096).rearrange("p (o c t) -> p o c t", o=2, c=BK)
        spec = area(14336, 4096).rearrange("p (o f c) -> p o f c", o=2, f=4)
        work = area(18432, 4096)
        merged = area(22528, 4096).rearrange("p (k t) -> p k t", k=DK)
        w3s = area(0, 2048)[0:HY_H, :]
        decay = area(2048, 1024).rearrange("p (j c) -> p j c", j=2)
        fz = area(3072, 256)[0:HY_E, :]
        fw1 = area(3328, 64)[0:HY_E, :]
        fw2 = area(3392, 64)[0:HY_H, :]
        fhid = area(3456, 3 * 256).rearrange("p (i t) -> p i t", i=3)
        fpm = area(4352, 2048).rearrange("p (i j c) -> p i j c", i=2, j=2)
        fraw = area(6400, 2048).rearrange("p (i j c) -> p i j c", i=2, j=2)
        fabs_ = area(8448, 1024).rearrange("p (j c) -> p j c", j=2)
        fnorm = area(9472, 512)
        sqb = area(22528, 1024).rearrange("p (i t) -> p i t", i=2)
        nrm = area(22528 + 1024, 2048).rearrange("p (i t) -> p i t", i=4)
        up = work[:, 0:2 * POOL_L].rearrange("p (s t) -> p s t", s=2)
        ps_a = work[:, 576:576 + 2 * POOL_L].rearrange("p (s t) -> p s t", s=2)
        ps_b = work[:, 1152:1152 + 2 * POOL_L].rearrange("p (s t) -> p s t", s=2)
        ypool = work[:, 2048:4096].rearrange("p (c t) -> p c t", c=BK)
        zt = work[:, 0:1024].rearrange("p (j c) -> p j c", j=2)
        hy_y = work[:, 1024:3072].rearrange("p (f c) -> p f c", f=4)
        hy_t = work[:, 3072:4096].rearrange("p (i c) -> p i c", i=2)
        qrot = area(14336, 1024).rearrange("p (c t) -> p c t", c=BK)
        krot = area(15360, 1024).rearrange("p (c t) -> p c t", c=BK)
        rtmp = area(16384, 512).rearrange("p (i t) -> p i t", i=2)
        prob = work[:, 0:2048].rearrange("p (u t) -> p u t", u=4)
        bias = work[:, 2048:2048 + 768].rearrange("p (i s j) -> p i s j", i=2, s=6)
        pstat = work[:, 2816:2816 + 32].rearrange("p (u i) -> p u i", u=4)
        pT_s = area(10240, 3072).rearrange("p (i k t) -> p i k t", i=2, k=6)
        gate_t = work[:, 0:1024].rearrange("p (i t) -> p i t", i=2)
        mtmp = work[:, 1024:1536]
        htok = area(0, 4096).rearrange("p (j d) -> p j d", j=4)
        rt = area(4096, 2048).rearrange("p (i x) -> p i x", i=32)
        ids_f = area(6144, 128)[0:64, :]
        tidx = sb("tidx", [P, 64], U32)
        didx = sb("didx", [P, 2, 4], U32)
        cnt_u = sb("cnt_u", [P, 1], U32)
        wsel = sb("wsel", [P, 2, 4])
        zero_ids = area(6272, 64)
        hg = area(8192, 2048).rearrange("p (i d) -> p i d", i=2)
        heT = area(10240, 2048).rearrange("p (i k t) -> p i k t", i=2, k=DK)
        hid = area(12288, 1024).rearrange("p (i f) -> p i f", i=2)
        thb = area(13312, 1024).rearrange("p (i f) -> p i f", i=2)
        hidT = area(14336, 1024).rearrange("p (i k t) -> p i k t", i=2, k=FK)
        yb = area(15360, 2048).rearrange("p (i d) -> p i d", i=2)
        over_w = area(17408, 8192).rearrange("p (i x) -> p i x", i=2)
        over_idx = sb("over_idx", [P, 1], U32)
        fa = area(0, 4096).rearrange("p (j d) -> p j d", j=4)
        fb = area(8192, 4096).rearrange("p (j d) -> p j d", j=4)

        bank = [ctx.enter_context(nc.psum_tensor(f"bank{i}", [P, 512], F32)) for i in range(8)]

        s_ld = sem("constants_loaded")
        s_ldl = sems("layer_params_loaded")
        ring_full = [sem(f"ring_full{i}") for i in range(RS)]
        ring_used = sem("ring_used")
        dve_c = sem("dve_chain")
        act_c = sem("act_chain")
        s_ce = sem("c_exp")
        s_cs = sem("c_silu")
        f_p = both("filter_pe")
        f_d = both("filter_dve")
        f_a = both("filter_act")
        m_d = both("mod_ready")
        n_sq = sem("norm_squares")
        n_mm = sem("norm_sums")
        n_a = sem("norm_mean")
        n_s = sem("norm_root")
        n_x = sem("norm_scaled")
        n_h = sem("norm_modulated")
        j_pe = sems("proj_products")
        j_c = sems("conv_centre")
        j_d = sems("proj_taken_dve")
        j_a = sems("proj_taken_act")
        pw_pe = both("pool_products")
        pw_a = both("pool_scaled")
        y_tp = sems("z_transposed")
        y_zt = sems("z_rows_ready")
        y_f = sems("spectrum_ready")
        y_m = sems("spectra_multiplied")
        y_i = sems("inverse_ready")
        y_z = sems("z_updated")
        r_pe = both("rope_swapped")
        r_d = both("rope_ready")
        b_ld = [sems(f"bias_loaded{l}_", 2) for l in range(DEPTH)]
        b_fix = sems("bias_masked")
        a_sc = sems("scores_ready")
        a_mx = sems("score_max_ready")
        a_ex = sems("exp_ready")
        a_nm = sems("probs_ready")
        a_tr = sems("probs_transposed")
        a_ev = sems("probsT_ready")
        a_pv = sems("attention_out")
        a_o = sems("attention_taken")
        g_pe = sems("merge_products")
        g_t = sems("gate_tanh")
        g_d = sems("merge_taken")
        o_pe = sems("out_products")
        o_d = sems("residual_added")
        t_pe = sems("rows_transposed")
        t_ev = sems("rows_copied")
        t_st = sems("rows_stored")
        q_z = both("zeros_ready")
        q_zd = sems("slot_table_cleared")
        q_lg = both("logits_ready")
        q_ex = both("logits_exp")
        q_m = both("experts_chosen")
        q_rk = both("ranks_ready")
        q_ix = both("slots_ready")
        q_sc = sems("slots_scattered")
        q_tb = sems("slot_table_loaded")
        q_tt = both("slot_table_transposed")
        q_ti = both("token_index_ready")
        x_g = [sems(f"rows_gathered{l}_", 2) for l in range(DEPTH)]
        x_tr = both("expert_rows_transposed")
        x_ha = both("expert_in_act")
        x_hd = both("expert_in_dve")
        x_gu = both("gate_up_ready")
        x_th = both("expert_tanh")
        x_th2 = both("gate_silu_ready")
        x_hid = both("hidden_ready")
        x_ht = both("hidden_transposed")
        x_hte = both("hiddenT_ready")
        x_y = both("expert_out_ready")
        x_ya = both("expert_out_act")
        x_yd = both("expert_out_dve")
        x_st = [sems(f"expert_out_stored{l}_", 2) for l in range(DEPTH)]
        v_w = sems("over_gate_up_loaded")
        v_wd = sems("over_down_loaded")
        v_g = sems("over_gathered")
        v_pe = sems("over_products")
        v_a = sems("over_tanh")
        v_d = sems("over_vector")
        v_s = sems("over_stored")
        v_done = sems("over_areas_free")
        z_g = sems("combine_gathered")
        z_f = sems("combined")
        z_t = sems("combined_transposed")
        z_x = sems("moe_added")
        e_t = sem("final_transposed")
        e_c = sem("final_copied")
        e_s = sem("output_stored")

        FILT_A, FILT_D, FILT_P = 4, 6, 6
        units_of = [[(x, s) for s in range(streams(l)) for x in range(2)] for l in range(DEPTH)]

        def win(l, c):
            return a["w_in"][l].rearrange("(k p) n -> p k n", p=P)[:, :, c * 256:(c + 1) * 256]

        def chunk_src(l, i):
            if i < IN_C:
                return win(l, IN_ORDER[i]), 8
            i -= IN_C
            if i < MERGE_C:
                n, r = divmod(i, 6)
                h, r = divmod(r, 3)
                if r == 1:
                    v = a["w_branch"][l, n].rearrange("(k p) n -> p k n", p=P)
                    return v[:, :, h * 512:(h + 1) * 512], 4
                return win(l, GATE_C0 + n * 4 + 2 * h + r // 2), 8
            i -= MERGE_C
            return a["w_out"][l].rearrange("(k p) n -> p k n", p=P)[:, :, i * 256:(i + 1) * 256], 8

        def rview(slot, k):
            return ring[:, slot, :].rearrange("p (k n) -> p k n", k=k)

        def full_at(idx):
            return 16 * (idx // RS + 1)

        block = ctx.enter_context(nc.Block())

        @block.sync
        def _(sp):
            for dst, name in ((cc[:, 0, :], "c_cols"), (dft_f[:], "dft_f"), (square[:], "square"), (xT[:], "x_cols"),
                              (dft_i[:], "dft_i"), (rope[:], "rope"), (colmask[:], "colmask"), (edge[:], "edge"),
                              (nyq[:], "nyq"), (slot0[:], "slot0"), (tok_id[:], "tok_id"), (par[0][:], "par0"),
                              (par[1][:], "par1"), (fin_g[:], "fin_g"), (wrt[:], "w_router"), (rbias[:], "router_bias")):
                sp.dma_start(dst, a[name]).then_inc(s_ld, 16)

            for l in range(DEPTH):
                base = l * LAYER_C
                if l:
                    sp.wait_ge(z_x[l - 1], 16)
                sp.dma_start(w3s, a["hy_w3"][l]).then_inc(s_ldl[l], 16)
                sp.dma_start(decay, a["decay"]).then_inc(s_ldl[l], 16)
                sp.dma_start(fz, a["filter_in"]).then_inc(s_ldl[l], 16)
                sp.dma_start(fw1, a["hy_w1"][l]).then_inc(s_ldl[l], 16)
                sp.dma_start(fw2, a["hy_w2"][l]).then_inc(s_ldl[l], 16)
                sp.dma_start(poolw[:], a["pool_w"][l].rearrange("g c d -> c g d")).then_inc(s_ldl[l], 16)
                wm = a["w_mod"][l].rearrange("(k p) (i n) -> p k i n", p=P, n=256)
                if l == 0:
                    for j in range(RS):
                        sp.dma_start(rview(j, 8), wm[:, :, j, :]).then_inc(ring_full[j], 16)
                with sp.Fori(1 if l == 0 else 0, MOD_C // RS) as i:
                    for j in range(RS):
                        sp.wait_ge(ring_used, i * RS + (base + j + 1 - RS))
                        sp.dma_start(rview(j, 8), wm[:, :, bass.ds(i * RS + j, 1), :]).then_inc(ring_full[j], 16)
                for i in range(PRE_C - MOD_C):
                    src, k = chunk_src(l, i)
                    idx = base + MOD_C + i
                    sp.wait_ge(ring_used, idx - RS + 1)
                    sp.dma_start(rview(idx % RS, k), src).then_inc(ring_full[idx % RS], 16)

                wg = a["w_gate_e"][l].rearrange("e (h k p) n -> p e h k n", p=P, h=2)
                wu = a["w_up_e"][l].rearrange("e (h k p) n -> p e h k n", p=P, h=2)
                wd = a["w_down_e"][l].rearrange("e (h k p) n -> p e h k n", p=P, h=2)

                def put(idx, slot, w, e, h, k):
                    sp.wait_ge(ring_used, idx - RS + 1)
                    sp.dma_start(rview(slot, k), w[:, bass.ds(e, 1), h].rearrange("p e k n -> p (e k) n")
                                 ).then_inc(ring_full[slot], 16)

                xb = base + PRE_C
                for h in range(2):
                    put(xb + h, h, wg, 0, h, 4)
                for h in range(2):
                    put(xb + 2 + h, 2 + h, wu, 0, h, 4)

                def step(s):
                    at = s * 6 + (xb - 2)
                    for h in range(2):
                        put(at + h, 4 + h, wg, s, h, 4)
                    for h in range(2):
                        put(at + 2 + h, h, wu, s, h, 4)
                    for h in range(2):
                        put(at + 4 + h, 2 + h, wd, s - 1, h, 2)

                with sp.Fori(0, 7) as i:
                    step(2 * i + 1)
                    step(2 * i + 2)
                step(15)
                for h in range(2):
                    put(xb + 94 + h, 4 + h, wd, E_N - 1, h, 2)
                sp.wait_ge(q_ix[l], l + 1)
                most = sp.value_load(cnt_u[0:1, 0:1], min_val=0, max_val=NT)
                sp.wait_ge(x_hd[l], 16 * l + 1)
                with sp.If(most > P):
                    with sp.Fori(0, tcols(l) // P - 1) as r:
                        with sp.Fori(0, E_N) as e:
                            b = r * E_N + e
                            gu = [a[n][l].rearrange("e (k p) n -> p e k n", p=P) for n in ("w_gate_e", "w_up_e")]
                            dn = a["w_down_e"][l].rearrange("e (k p) n -> p e k n", p=P)
                            sp.wait_ge(x_y[l], 16 * l + 16)
                            sp.wait_ge(v_done[l], b + 1)
                            for i in range(2):
                                sp.dma_start(over_w[:, i, :].rearrange("p (k n) -> p k n", k=8),
                                             gu[i][:, bass.ds(e, 1)].rearrange("p e k n -> p (e k) n")
                                             ).then_inc(v_w[l], 16)
                            sp.wait_ge(v_pe[l], b * 4 + 2)
                            sp.dma_start(over_w[:, 0, :].rearrange("p (k n) -> p k n", k=4),
                                         dn[:, bass.ds(e, 1)].rearrange("p e k n -> p (e k) n")).then_inc(v_wd[l], 16)
            sp.wait_ge(e_c, 2)
            sp.dma_start(out[0, 0:P, :], htok[:, 0, :]).then_inc(e_s, 16)
            sp.wait_ge(e_c, 4)
            sp.dma_start(out[0, P:2 * P, :], htok[:, 1, :]).then_inc(e_s, 16)
            sp.wait_ge(e_s, 32)

        @block.gpsimd
        def _(pool):
            for l in range(DEPTH):
                T = tcols(l)
                nt = T // P
                for h in range(HEADS):
                    if h >= 2:
                        pool.wait_ge(a_mx[l], len(units_of[l]) * (h - 1))
                    else:
                        pool.wait_ge(y_z[l], 2 * streams(l) * BK)
                    pool.dma_start(bias[:, h % 2], a["rpb_win"][l, h]).then_inc(b_ld[l][h % 2], 16)
                pool.wait_ge(o_d[l], 8 * streams(l))
                pool.memset(zero_ids, 0.0).then_inc(q_z[l], 1)
                pool.wait_ge(q_z[l], l + 1)
                pool.dma_start(slot_tok[l].rearrange("(p x) o -> p (x o)", p=P), zero_ids).then_inc(q_zd[l], 16)
                pool.wait_ge(q_zd[l], 16)
                for j in range(nt):
                    pool.wait_ge(t_ev[l], 2 * (j + 1))
                    pool.dma_start(h_rows[l][j * P:(j + 1) * P, :], htok[:, j, :]).then_inc(t_st[l], 16)
                pool.wait_ge(q_ix[l], l + 1)
                for j in range(nt):
                    for i in range(2):
                        pool.indirect_dma_start(
                            out=slot_tok[l], out_offset=bass.IndirectOffsetOnAxis(ap=didx[:, i, j:j + 1], axis=0),
                            in_=tok_id[:, j:j + 1], in_offset=None).then_inc(q_sc[l], 16)
                pool.wait_ge(q_sc[l], 16 * 2 * nt)
                pool.dma_start(ids_f, slot_tok[l].rearrange("(r s) o -> r (s o)", s=P)).then_inc(q_tb[l], 16)
                pool.wait_ge(q_ti[l], l + 1)
                pool.wait_ge(t_st[l], 16 * nt)

                def gather(i, e, dst, done):
                    pool.indirect_dma_start(
                        out=dst, out_offset=None, in_=h_rows[l][0:tcols(l), :],
                        in_offset=bass.IndirectOffsetOnAxis(ap=e, axis=0)).then_inc(done, 16)

                def store(s, par_):
                    pool.wait_ge(x_ya[l], 16 * l + s + 1)
                    pool.wait_ge(x_yd[l], 16 * l + s + 1)
                    pool.dma_start(y_rows[l][s * P:(s + 1) * P, :], yb[:, par_, :]).then_inc(x_st[l][par_], 16)

                for e in range(2):
                    gather(e, tidx[:, e:e + 1], hg[:, e, :], x_g[l][e])
                for s in range(E_N):
                    if s + 2 < E_N:
                        pool.wait_ge(x_tr[l], 16 * l + s + 1)
                        gather(s, tidx[:, s + 2:s + 3], hg[:, s % 2, :], x_g[l][s % 2])
                    if s >= 1:
                        store(s - 1, (s - 1) % 2)
                store(E_N - 1, 1)
                for i in range(2):
                    pool.wait_ge(x_st[l][i], 16 * E_N // 2)

                def combine(rows):
                    for j in range(nt):
                        for i in range(2):
                            pool.indirect_dma_start(
                                out=(fa if i == 0 else fb)[:, j, :], out_offset=None, in_=y_rows[l][0:rows, :],
                                in_offset=bass.IndirectOffsetOnAxis(ap=didx[:, i, j:j + 1], axis=0)
                            ).then_inc(z_g[l], 16)

                most = pool.value_load(cnt_u[0:1, 0:1], min_val=0, max_val=NT)
                with pool.If(most > P):
                    with pool.Fori(0, (nt - 1) * E_N) as b:
                        pool.wait_ge(v_d[l], b * 6 + 1)
                        pool.tensor_tensor(zero_ids[:, 1:2], zero_ids[:, 0:1], zero_ids[:, 0:1], ALU.add)
                        gather(0, over_idx[:], hg[:, 0, :], v_g[l])
                        pool.wait_ge(v_d[l], b * 6 + 6)
                        pool.dma_start(y_rows[l][bass.ds(b * P + E_N * P, P), :], yb[:, 0, :]).then_inc(v_s[l], 16)
                        pool.wait_ge(v_s[l], b * 16 + 16)
                    combine(E_N * T)
                with pool.Else():
                    combine(E_N * P)

        @block.tensor
        def _(pe):
            mm = nc.tensor.matmul
            tp = nc.tensor.transpose

            def norm_pe(inst, cols):
                for k in range(DK):
                    pe.wait_ge(n_sq, inst * DK + k + 1)
                    mm(bank[7][:, 0:cols], ones, sqb[:, k % 2, 0:cols], start=k == 0, stop=k == DK - 1
                       ).then_inc(n_mm, 1)

            pe.wait_ge(s_ld, 16 * 16)
            for l in range(DEPTH):
                T = tcols(l)
                S = streams(l)
                base = l * LAYER_C
                pe.wait_ge(s_ldl[l], 16 * 6)
                mm(bank[0][0:HY_H, 0:SEQ], fw1, fz, start=True, stop=True).then_inc(f_p[l], 1)
                pe.wait_ge(f_a[l], 2 * l + 1)
                mm(bank[1][0:HY_H, 0:SEQ], fw2, fhid[0:HY_H, 1, :], start=True, stop=True).then_inc(f_p[l], 1)
                pe.wait_ge(f_a[l], 2 * l + 2)
                for o in range(HY_O):
                    if o:
                        pe.wait_ge(f_d[l], 6 * l + 4)
                    for i in range(2):
                        for j in range(2):
                            last = mm(bank[2 * i + j][:], fhid[0:HY_H, 2, j * P:(j + 1) * P],
                                      w3s[:, (2 * o + i) * BW:(2 * o + i + 1) * BW], start=True, stop=True)
                    last.then_inc(f_p[l], 1)
                    pe.wait_ge(f_d[l], 6 * l + 3 + 2 * o)
                    for j in range(2):
                        mm(bank[7][:], ones, fabs_[:, j, :], start=j == 0, stop=j == 1)
                    for f in range(4):
                        for j in range(2):
                            mm(bank[f][:], dft_f[:, j, f * P:(f + 1) * P], fpm[:, f // 2, j, :],
                               start=j == 0, stop=j == 1)
                    for j in range(2):
                        last = mm(bank[4][0:1, :], nyq[:, j:j + 1], fpm[:, 0, j, :], start=j == 0, stop=j == 1)
                    last.then_inc(f_p[l], 1)
                if l == 0:
                    pe.wait_ge(s_cs, 1)
                csil = cc[:, 3, :].rearrange("p (k s) -> p k s", s=2)
                with pe.Fori(0, MOD_C // RS) as i:
                    for j in range(RS):
                        pe.wait_ge(ring_full[j], i * 16 + full_at(base + j))
                        for x in range(2):
                            for k in range(DK):
                                last = mm(bank[5][:, bass.ds(i * (4 * RS) + (4 * j + 2 * x), 2)],
                                          rview(j, 8)[:, k, x * P:(x + 1) * P], csil[:, k, :],
                                          start=k == 0, stop=k == DK - 1)
                        last.then_inc(ring_used, 1)
                norm_pe(2 * l, NT)
                pe.wait_ge(n_h, (2 * l + 1) * DK)
                g = 0
                for i in range(IN_C):
                    idx = base + MOD_C + i
                    slot = idx % RS
                    pe.wait_ge(ring_full[slot], full_at(idx))
                    w = rview(slot, 8)
                    if i < 12:
                        cols = NT if i >= 10 else T
                        for x in range(2):
                            if g >= 4:
                                pe.wait_ge(j_d[l] if g - 4 < 16 else j_a[l], g - 3 if g - 4 < 16 else g - 19)
                            for k in range(DK):
                                last = mm(bank[g % 4][:, 0:cols], w[:, k, x * P:(x + 1) * P], hT[:, k, 0:cols],
                                          start=k == 0, stop=k == DK - 1)
                                if i and x + k == 0:
                                    last.then_inc(ring_used, 1)
                            last.then_inc(j_pe[l], 1)
                            g += 1
                    else:
                        for j in range(4):
                            pe.wait_ge(j_a[l], g - 19)
                            for k in range(DK):
                                last = mm(bank[g % 4][:, 0:256], hT[:, k, j * P:(j + 1) * P], w[:, k, :],
                                          start=k == 0, stop=k == DK - 1)
                                if j + k == 0:
                                    last.then_inc(ring_used, 1)
                            last.then_inc(j_pe[l], 1)
                            g += 1
                pe.wait_ge(j_pe[l], g)
                pe.nop().then_inc(ring_used, 1)
                pe.wait_ge(j_d[l], 16)
                for c in range(BK):
                    mm(bank[4 + c][:, 0:T], poolw[:, c, :], ypool[:, c, 0:T], start=True, stop=True
                       ).then_inc(pw_pe[l], 1)
                pe.wait_ge(j_a[l], 16)
                pe.wait_ge(pw_a[l], 4 * l + BK)
                n = 0
                for o in range(HY_O):
                    for s in range(S):
                        if n:
                            pe.wait_ge(y_zt[l], 2 * n)
                        if o:
                            pe.wait_ge(y_z[l], BK * (n + 1 - S))
                        for j in range(2):
                            for c in range(BK):
                                last = tp(bank[4 + j][:, c * P:(c + 1) * P],
                                          hv[:, c, s * SEQ + j * P:s * SEQ + (j + 1) * P], ident)
                            last.then_inc(y_tp[l], 1)
                        pe.wait_ge(y_zt[l], 2 * n + 2)
                        if n:
                            pe.wait_ge(y_m[l], 2 * n)
                        for f in (0, 2, 1, 3):
                            for j in range(2):
                                last = mm(bank[f][:], dft_f[:, j, f * P:(f + 1) * P], zt[:, j, :],
                                          start=j == 0, stop=j == 1)
                            last.then_inc(y_f[l], 1)
                        pe.wait_ge(y_m[l], 2 * n + 2)
                        for c in range(BK):
                            if n * BK + c >= 2:
                                pe.wait_ge(y_z[l], n * BK + c - 1)
                            for f in range(4):
                                last = mm(bank[6 + c % 2][:, 0:SEQ], hy_y[:, f, c * P:(c + 1) * P], dft_i[:, f, :],
                                          start=f == 0, stop=f == 3)
                            last.then_inc(y_i[l], 1)
                        n += 1
                for i, src in enumerate((qT, kT)):
                    for c in range(BK):
                        u = i * BK + c
                        if u >= 2:
                            pe.wait_ge(r_d[l], 8 * l + u - 1)
                        elif u == 0:
                            pe.wait_ge(y_z[l], 2 * S * BK)
                        mm(bank[6 + u % 2][:, 0:SEQ], perm, src[:, c, 0:SEQ], start=True, stop=True
                           ).then_inc(r_pe[l], 1)
                pe.wait_ge(r_d[l], 8 * l + 8)
                units = units_of[l]
                U = len(units)

                def scores(h):
                    c, p0 = h // 2, (h % 2) * DH
                    rows = slice(p0, p0 + DH)
                    for i, (x, s) in enumerate(units):
                        u = h * U + i
                        if u >= U:
                            pe.wait_ge(a_ex[l], u - U + 1)
                        b = bank[i]
                        if s == 0:
                            mm(b[:, 0:SEQ], qrot[rows, c, x * P:(x + 1) * P], krot[rows, c, :], start=True, stop=True)
                            last = mm(b[:, SEQ:NT], qT[rows, c, x * P:(x + 1) * P], kT[rows, c, SEQ:NT],
                                      start=True, stop=True)
                        else:
                            last = mm(b[:, 0:SEQ], qT[rows, c, SEQ + x * P:SEQ + (x + 1) * P], kT[rows, c, SEQ:NT],
                                      start=True, stop=True)
                        last.then_inc(a_sc[l], 1)

                def transposes(h):
                    if h:
                        pe.wait_ge(a_ev[l], (U // 2 + 1) * h)
                    for i, (x, s) in enumerate(units):
                        pe.wait_ge(a_nm[l], h * U + i + 1)
                        for k in range(4 if s == 0 else 2):
                            b = bank[4 + (k // 2 if s == 0 else 2)]
                            col = (k % 2) * SEQ + x * P
                            last = tp(b[:, col:col + P], prob[:, i, k * P:(k + 1) * P], ident)
                        if x == 1:
                            last.then_inc(a_tr[l], 1)

                def values(h):
                    c, p0 = h // 2, (h % 2) * DH
                    if h:
                        pe.wait_ge(a_o[l], h)
                    pe.wait_ge(a_ev[l], (U // 2 + 1) * (h + 1))
                    o = bank[7][p0:p0 + DH, :]
                    for k in range(4):
                        last = mm(o[:, 0:SEQ], vtok[:, k, h * DH:(h + 1) * DH], pT_s[:, h % 2, k, :],
                                  start=k == 0, stop=k == 3)
                    if S == 2:
                        for k in range(2):
                            last = mm(o[:, SEQ:NT], vtok[:, 2 + k, h * DH:(h + 1) * DH], pT_s[:, h % 2, 4 + k, :],
                                      start=k == 0, stop=k == 1)
                    last.then_inc(a_pv[l], 1)

                scores(0)
                for h in range(HEADS):
                    if h + 1 < HEADS:
                        scores(h + 1)
                    transposes(h)
                    values(h)
                pe.wait_ge(a_o[l], HEADS)
                with pe.Fori(0, 3) as n:
                    for m in range(DK):
                        h, r = divmod(m, 4)
                        b_at = base + MOD_C + IN_C + 3 * h + 1
                        g_at = b_at - 1 + 2 * (r // 2)
                        bslot, gslot = b_at % RS, g_at % RS
                        if r == 0:
                            pe.wait_ge(ring_full[bslot], n * 16 + full_at(b_at))
                        if r % 2 == 0:
                            pe.wait_ge(ring_full[gslot], n * 16 + full_at(g_at))
                        pe.wait_ge(g_d[l], n * DK + (m + 1))
                        for k in range(DK):
                            last = mm(bank[m % 2][:, 0:T], rview(gslot, 8)[:, k, (r % 2) * P:(r % 2 + 1) * P],
                                      hT[:, k, 0:T], start=k == 0, stop=k == DK - 1)
                            if k == 0 and m and r % 2 == 0:
                                last.then_inc(ring_used, 1 if r else 2)
                        last.then_inc(g_pe[l], 1)
                        for k in range(BK):
                            last = mm(bank[2 + m % 2][:, 0:T], rview(bslot, 4)[:, k, r * P:(r + 1) * P],
                                      ys[:, bass.ds(n, 1), k, 0:T], start=k == 0, stop=k == BK - 1)
                        last.then_inc(g_pe[l], 1)
                    pe.wait_ge(g_pe[l], n * (2 * DK) + (2 * DK))
                    pe.nop().then_inc(ring_used, 2)
                pe.wait_ge(g_d[l], 3 * DK + 2)
                for m in range(DK):
                    idx = base + PRE_C - OUT_C + m // 2
                    if m % 2 == 0:
                        pe.wait_ge(ring_full[idx % RS], full_at(idx))
                    if m >= 2:
                        pe.wait_ge(o_d[l], S * (m - 1))
                    for k in range(DK):
                        last = mm(bank[m % 2][:, 0:T], rview(idx % RS, 8)[:, k, (m % 2) * P:(m % 2 + 1) * P],
                                  merged[:, k, 0:T], start=k == 0, stop=k == DK - 1)
                        if k == 0 and m and m % 2 == 0:
                            last.then_inc(ring_used, 1)
                    last.then_inc(o_pe[l], 1)
                pe.wait_ge(o_pe[l], DK)
                pe.nop().then_inc(ring_used, 1)
                norm_pe(2 * l + 1, T)
                pe.wait_ge(n_h, (2 * l + 2) * DK)
                nt = T // P
                for j in range(nt):
                    for k in range(DK):
                        last = mm(bank[6][:, j * E_N:(j + 1) * E_N], hT[:, k, j * P:(j + 1) * P], wrt[:, k, :],
                                  start=k == 0, stop=k == DK - 1)
                last.then_inc(q_lg[l], 1)
                for j in range(nt):
                    if j >= 2:
                        pe.wait_ge(t_ev[l], 2 * (j - 1))
                    for i in range(2):
                        for k in range(4):
                            last = tp(bank[2 * (j % 2) + i][:, k * P:(k + 1) * P],
                                      hT[:, 4 * i + k, j * P:(j + 1) * P], ident)
                        last.then_inc(t_pe[l], 1)
                pe.wait_ge(q_m[l], l + 1)
                msk = rt[:, 0, :].rearrange("p (j e) -> p j e", e=E_N)
                for j in range(nt):
                    for i in range(j + 1):
                        mm(bank[7][:, j * E_N:(j + 1) * E_N], tri if i == j else ones, msk[:, i, :],
                           start=i == 0, stop=i == j)
                for i in range(nt):
                    last = mm(bank[7][:, 64:64 + E_N], ones, msk[:, i, :], start=i == 0, stop=i == nt - 1)
                last.then_inc(q_rk[l], 1)
                pe.wait_ge(q_tb[l], 16)
                tp(bank[6][:, 64:128], ids_f, ident[0:64, 0:64]).then_inc(q_tt[l], 1)
                xb = base + PRE_C
                pe.wait_ge(t_ev[l], 2 * nt)

                def rows_t(par_, e, owed):
                    for i in range(2):
                        for k in range(4):
                            last = tp(bank[i][:, k * P:(k + 1) * P], hg[:, par_, (4 * i + k) * P:(4 * i + k + 1) * P],
                                      ident)
                            if owed and i + k == 0:
                                last.then_inc(ring_used, 1)
                    last.then_inc(x_tr[l], 1)

                def gate_up(par_, s, idx, slots):
                    pe.wait_ge(x_ha[l], 16 * l + s + 1)
                    pe.wait_ge(x_hd[l], 16 * l + s + 1)
                    for w in range(2):
                        for h in range(2):
                            c = 2 * w + h
                            pe.wait_ge(ring_full[slots[c]], idx[c])
                            for k in range(4):
                                last = mm(bank[2 + w][:], heT[:, par_, 4 * h + k, :], rview(slots[c], 4)[:, k, :],
                                          start=h + k == 0, stop=h == 1 and k == 3)
                            last.then_inc(ring_used if c < 3 else x_gu[l], 1)

                def hidden_t(par_, s, owed):
                    pe.wait_ge(x_hid[l], 16 * l + s + 1)
                    for k in range(FK):
                        last = tp(bank[4][:, k * P:(k + 1) * P], hid[:, par_, k * P:(k + 1) * P], ident)
                        if owed and k == 0:
                            last.then_inc(ring_used, 1)
                    last.then_inc(x_ht[l], 1)

                def down(par_, s, idx, slots, owed):
                    pe.wait_ge(x_hte[l], 16 * l + s + 1)
                    for h in range(2):
                        pe.wait_ge(ring_full[slots[h]], idx[h])
                        for k in range(2):
                            for x in range(2):
                                last = mm(bank[5 + x][:], hidT[:, par_, 2 * h + k, :],
                                          rview(slots[h], 2)[:, k, x * 512:(x + 1) * 512],
                                          start=h + k == 0, stop=h + k == 2)
                                if owed and h + k + x == 0:
                                    last.then_inc(ring_used, 1)
                        last.then_inc(x_y[l] if h else ring_used, 1)

                def fulls(off):
                    return [full_at(xb + off + i) for i in range(6)]

                for e in range(2):
                    pe.wait_ge(x_g[l][e], 16)
                    if e:
                        pe.wait_ge(x_ha[l], 16 * l + 1)
                        pe.wait_ge(x_hd[l], 16 * l + 1)
                    rows_t(e, e, e == 1)
                    if e == 0:
                        gate_up(0, 0, fulls(0)[0:4], (0, 1, 2, 3))
                        pe.wait_ge(x_gu[l], 16 * l + 1)

                def step(par_, s, i, off, more):
                    f = [i * 32 + v for v in fulls(off)]
                    hidden_t(1 - par_, s - 1, False)
                    gate_up(par_, s, f[0:4], (4, 5, 0, 1))
                    down(1 - par_, s - 1, f[4:6], (2, 3), True)
                    if more:
                        pe.wait_ge(x_g[l][1 - par_], 16 * ((s + 1) // 2 + 1) if isinstance(s, int) else
                                   (i * 16 + 32))
                        pe.wait_ge(x_ha[l], 16 * l + s + 1)
                        pe.wait_ge(x_hd[l], 16 * l + s + 1)
                        rows_t(1 - par_, s + 1, True)

                with pe.Fori(0, 7) as i:
                    step(1, 2 * i + 1, i, 4, True)
                    step(0, 2 * i + 2, i, 10, True)
                step(1, 15, 7, 4, False)
                hidden_t(1, 15, True)
                pe.wait_ge(x_ya[l], 16 * l + 15)
                pe.wait_ge(x_yd[l], 16 * l + 15)
                down(1, 15, [full_at(xb + 94), full_at(xb + 95)], (4, 5), False)
                pe.wait_ge(x_y[l], 16 * l + 16)
                pe.nop().then_inc(ring_used, 1)
                pe.wait_ge(q_ix[l], l + 1)
                most = pe.value_load(cnt_u[0:1, 0:1], min_val=0, max_val=NT)
                with pe.If(most > P):
                    pe.nop().then_inc(v_done[l], 1)
                    with pe.Fori(0, (nt - 1) * E_N) as b:
                        pe.wait_ge(v_g[l], b * 16 + 16)
                        for i in range(2):
                            for k in range(4):
                                last = tp(bank[i][:, k * P:(k + 1) * P], hg[:, 0, (4 * i + k) * P:(4 * i + k + 1) * P],
                                          ident)
                        last.then_inc(v_pe[l], 1)
                        pe.wait_ge(v_d[l], b * 6 + 2)
                        pe.wait_ge(v_w[l], b * 32 + 32)
                        for i in range(2):
                            for k in range(DK):
                                last = mm(bank[2 + i][:], heT[:, 0, k, :], over_w[:, i, k * FF:(k + 1) * FF],
                                          start=k == 0, stop=k == DK - 1)
                        last.then_inc(v_pe[l], 1)
                        pe.wait_ge(v_d[l], b * 6 + 4)
                        for k in range(FK):
                            last = tp(bank[4][:, k * P:(k + 1) * P], hid[:, 0, k * P:(k + 1) * P], ident)
                        last.then_inc(v_pe[l], 1)
                        pe.wait_ge(v_d[l], b * 6 + 5)
                        pe.wait_ge(v_wd[l], b * 16 + 16)
                        for i in range(2):
                            for k in range(FK):
                                last = mm(bank[5 + i][:], hidT[:, 0, k, :],
                                          over_w[:, 0, k * D + i * 512:k * D + (i + 1) * 512],
                                          start=k == 0, stop=k == FK - 1)
                        last.then_inc(v_pe[l], 1)
                        pe.wait_ge(v_pe[l], b * 4 + 4)
                        pe.nop().then_inc(v_done[l], 1)
                with pe.Else():
                    pe.nop()
                pe.wait_ge(z_f[l], nt)
                pe.wait_ge(x_ya[l], 16 * l + E_N)
                pe.wait_ge(x_yd[l], 16 * l + E_N)
                for k in range(DK):
                    for j in range(nt):
                        last = tp(bank[k][:, j * P:(j + 1) * P], fa[:, j, k * P:(k + 1) * P], ident)
                    last.then_inc(z_t[l], 1)
                pe.wait_ge(z_x[l], 16)
            norm_pe(4, SEQ)
            pe.wait_ge(n_h, 5 * DK)
            for j in range(2):
                for i in range(2):
                    for k in range(4):
                        last = tp(bank[2 * j + i][:, k * P:(k + 1) * P], hT[:, 4 * i + k, j * P:(j + 1) * P], ident)
                    last.then_inc(e_t, 1)

        @block.scalar
        def _(act):
            A = nc.scalar.activation

            def norm_act(inst, cols, nstream):
                if inst:
                    l = (inst - 1) // 2
                    act.wait_ge(o_d[l] if inst % 2 else z_x[l], 8 * nstream if inst % 2 else 16)
                for k in range(DK):
                    if k >= 2:
                        act.wait_ge(n_mm, inst * DK + k - 1)
                    A(sqb[:, k % 2, 0:cols], xT[:, k, 0:cols], ACT.Square).then_inc(n_sq, 1)
                act.wait_ge(n_a, inst + 1)
                A(nrm[:, 1, 0:cols], nrm[:, 0, 0:cols], ACT.Sqrt).then_inc(n_s, 1)
                for k in range(DK):
                    act.wait_ge(n_x, inst * DK + k + 1)
                    if inst == 4:
                        A(hT[:, k, 0:cols], hT[:, k, 0:cols], ACT.Identity, scale=fin_g[:, k:k + 1]).then_inc(n_h, 1)
                        continue
                    w = inst % 2
                    for s in range(nstream):
                        v = hT[:, k, s * SEQ:(s + 1) * SEQ]
                        last = A(v, v, ACT.Identity, scale=gs[:, w, k, s:s + 1],
                                 bias=mods[:, 3 * w * DK + k, s:s + 1])
                    last.then_inc(n_h, 1)

            act.wait_ge(s_ld, 16 * 16)
            A(cc[:, 1, :], cc[:, 0, :], ACT.Exp, scale=-1.0).then_inc(s_ce, 1)
            for l in range(DEPTH):
                T = tcols(l)
                S = streams(l)
                pc = par[l]
                for i in range(2):
                    act.wait_ge(f_d[l], 6 * l + 1 + i)
                    A(fhid[0:HY_H, 1 + i, :], fhid[0:HY_H, 0, :], ACT.Sin).then_inc(f_a[l], 1)
                if l == 0:
                    pass
                act.wait_ge(m_d[l], l + 1)
                norm_act(2 * l, NT, 2)
                for g in range(12):
                    act.wait_ge(j_pe[l], g + 1)
                    dst = hv[:, g, 0:T] if g < 4 else hx[:, (g - 4) // 4, g % 4, 0:T]
                    A(dst, bank[g % 4][:, 0:T], ACT.Identity, scale=pc[:, C_TAP + 12 + g:C_TAP + 13 + g],
                      bias=pc[:, C_SB + g:C_SB + g + 1]).then_inc(j_c[l], 1)
                for g in range(16, 32):
                    act.wait_ge(j_pe[l], g + 1)
                    b = bank[g % 4]
                    if g < 20:
                        A(qT[:, g - 16, 0:T], b[:, 0:T], ACT.Copy, scale=DH ** -0.5).then_inc(j_a[l], 1)
                    elif g < 24:
                        A(kT[:, g - 20, :], b[:, :], ACT.Copy).then_inc(j_a[l], 1)
                    else:
                        h, j = divmod(g - 24, 4)
                        A(vtok[:, j, h * 256:(h + 1) * 256], b[:, 0:256], ACT.Copy).then_inc(j_a[l], 1)
                for c in range(BK):
                    act.wait_ge(pw_pe[l], 4 * l + c + 1)
                    A(ys_pool[:, c, 0:T], bank[4 + c][:, 0:T], ACT.Copy, scale=pc[:, C_PS + c:C_PS + c + 1]
                      ).then_inc(pw_a[l], 1)
                for n in range(2 * S):
                    if n:
                        act.wait_ge(y_f[l], 4 * n)
                    for j in range(2):
                        act.wait_ge(y_tp[l], 2 * n + j + 1)
                        A(zt[:, j, :], bank[4 + j][:, :], ACT.Copy).then_inc(y_zt[l], 1)
                units = units_of[l]
                U = len(units)

                def exps(h):
                    for i, (x, s) in enumerate(units):
                        act.wait_ge(a_mx[l], h * U + i + 1)
                        if h:
                            act.wait_ge(a_tr[l], (U // 2) * (h - 1) + s + 1)
                        w = NT if s == 0 else SEQ
                        A(prob[:, i, 0:w], bank[i][:, 0:w], ACT.Exp, bias=pstat[:, i, 0:1],
                          accum_out=pstat[:, i, 1:2]).then_inc(a_ex[l], 1)

                def evac(h):
                    act.wait_ge(a_tr[l], (U // 2) * h + 1)
                    if h >= 2:
                        act.wait_ge(a_pv[l], h - 1)
                    A(pT_s[:, h % 2, 0:2, :], bank[4][:, :].rearrange("p (k t) -> p k t", k=2), ACT.Copy
                      ).then_inc(a_ev[l], 1)
                    A(pT_s[:, h % 2, 2:4, :], bank[5][:, :].rearrange("p (k t) -> p k t", k=2), ACT.Copy
                      ).then_inc(a_ev[l], 1)
                    if S == 2:
                        act.wait_ge(a_tr[l], 2 * h + 2)
                        A(pT_s[:, h % 2, 4:6, :], bank[6][:, :].rearrange("p (k t) -> p k t", k=2), ACT.Copy
                          ).then_inc(a_ev[l], 1)
                    act.wait_ge(a_pv[l], h + 1)
                    c, p0 = h // 2, (h % 2) * DH
                    A(qT[p0:p0 + DH, c, 0:T], bank[7][p0:p0 + DH, 0:T], ACT.Copy).then_inc(a_o[l], 1)

                act.wait_ge(y_z[l], 2 * S * BK)
                exps(0)
                for h in range(HEADS):
                    evac(h)
                    if h + 1 < HEADS:
                        exps(h + 1)
                act.wait_ge(a_tr[l], HEADS * (U // 2))
                with act.Fori(0, 3) as n:
                    for m in range(DK):
                        act.wait_ge(g_pe[l], n * (2 * DK) + (2 * m + 1))
                        act.wait_ge(g_d[l], n * DK + (m + 1))
                        A(gate_t[:, m % 2, 0:T], bank[m % 2][:, 0:T], ACT.Tanh, scale=0.5).then_inc(g_t[l], 1)
                norm_act(2 * l + 1, T, S)
                nt = T // P
                act.wait_ge(q_lg[l], l + 1)
                A(rt[:, 1, 0:nt * E_N], bank[6][:, 0:nt * E_N], ACT.Exp, scale=-1.0).then_inc(q_ex[l], 1)
                for j in range(nt):
                    for i in range(2):
                        act.wait_ge(t_pe[l], 2 * j + i + 1)
                        A(htok[:, j, i * 512:(i + 1) * 512], bank[2 * (j % 2) + i][:, :], ACT.Copy
                          ).then_inc(t_ev[l], 1)

                def rows_in(par_, e):
                    act.wait_ge(x_tr[l], 16 * l + e + 1)
                    A(heT[:, par_, 0:4, :], bank[0][:, :].rearrange("p (k t) -> p k t", k=4), ACT.Copy
                      ).then_inc(x_ha[l], 1)

                def tanh(par_, s):
                    act.wait_ge(x_gu[l], 16 * l + s + 1)
                    A(thb[:, par_, :], bank[2][:, :], ACT.Tanh, scale=0.5).then_inc(x_th[l], 1)

                def hid_in(par_, s):
                    act.wait_ge(x_ht[l], 16 * l + s + 1)
                    A(hidT[:, par_, :, :], bank[4][:, :].rearrange("p (k t) -> p k t", k=4), ACT.Copy
                      ).then_inc(x_hte[l], 1)

                def y_out(par_, s, free):
                    act.wait_ge(x_y[l], 16 * l + s + 1)
                    if free is not None:
                        act.wait_ge(x_st[l][par_], free)
                    A(yb[:, par_, 0:512], bank[5][:, :], ACT.Copy).then_inc(x_ya[l], 1)

                rows_in(0, 0)
                tanh(0, 0)
                rows_in(1, 1)
                for s in (1, 2):
                    hid_in((s - 1) % 2, s - 1)
                    tanh(s % 2, s)
                    y_out((s - 1) % 2, s - 1, None)
                    rows_in((s + 1) % 2, s + 1)
                with act.Fori(1, 7) as i:
                    hid_in(0, 2 * i)
                    tanh(1, 2 * i + 1)
                    y_out(0, 2 * i, i * 16)
                    rows_in(0, 2 * i + 2)
                    hid_in(1, 2 * i + 1)
                    tanh(0, 2 * i + 2)
                    y_out(1, 2 * i + 1, i * 16)
                    rows_in(1, 2 * i + 3)
                hid_in(0, 14)
                tanh(1, 15)
                y_out(0, 14, 16 * 7)
                hid_in(1, 15)
                y_out(1, 15, 16 * 7)
                act.wait_ge(q_ix[l], l + 1)
                most = act.value_load(cnt_u[0:1, 0:1], min_val=0, max_val=NT)
                with act.If(most > P):
                    with act.Fori(0, (nt - 1) * E_N) as b:
                        act.wait_ge(v_pe[l], b * 4 + 2)
                        A(thb[:, 0, :], bank[2][:, :], ACT.Tanh, scale=0.5).then_inc(v_a[l], 1)
                with act.Else():
                    act.nop()
            norm_act(4, SEQ, 1)
            for j in range(2):
                for i in range(2):
                    act.wait_ge(e_t, 2 * j + i + 1)
                    A(htok[:, j, i * 512:(i + 1) * 512], bank[2 * j + i][:, :], ACT.Copy).then_inc(e_c, 1)

        @block.vector
        def _(dve):
            V = nc.vector
            chain = [0]

            def link(ins):
                chain[0] += 1
                ins.then_inc(dve_c, 1)
                dve.wait_ge(dve_c, chain[0])

            def norm_dve(inst, cols):
                dve.wait_ge(n_mm, (inst + 1) * DK)
                V.tensor_scalar(nrm[:, 0, 0:cols], bank[7][:, 0:cols], 1.0 / D, EPS, ALU.mult, ALU.add).then_inc(n_a, 1)
                dve.wait_ge(n_s, inst + 1)
                link(V.reciprocal(nrm[:, 2, 0:cols], nrm[:, 1, 0:cols]))
                link(V.tensor_tensor(nrm[:, 3, 0:cols], nrm[:, 2, 0:cols], nrm[:, 2, 0:cols], ALU.mult))
                link(V.scalar_tensor_tensor(nrm[:, 3, 0:cols], nrm[:, 0, 0:cols], -0.5, nrm[:, 3, 0:cols],
                                            ALU.mult, ALU.mult))
                link(V.scalar_tensor_tensor(nrm[:, 1, 0:cols], nrm[:, 3, 0:cols], 1.5, nrm[:, 2, 0:cols],
                                            ALU.add, ALU.mult))
                for k in range(DK):
                    V.tensor_tensor(hT[:, k, 0:cols], xT[:, k, 0:cols], nrm[:, 1, 0:cols], ALU.mult).then_inc(n_x, 1)

            dve.wait_ge(s_ce, 1)
            link(V.tensor_scalar(cc[:, 2, :], cc[:, 1, :], 1.0, None, ALU.add))
            link(V.reciprocal(cc[:, 1, :], cc[:, 2, :]))
            V.tensor_tensor(cc[:, 3, :], cc[:, 0, :], cc[:, 1, :], ALU.mult).then_inc(s_cs, 1)
            for l in range(DEPTH):
                T = tcols(l)
                S = streams(l)
                pc = par[l]
                fc = [pc[0:HY_H, C_FILT + i:C_FILT + i + 1] for i in range(3)]

                for i in range(2):
                    dve.wait_ge(f_p[l], 6 * l + i + 1)
                    x0, x1 = fhid[0:HY_H, 0, :], nrm[0:HY_H, 0, 0:SEQ]
                    if i:
                        dve.wait_ge(f_a[l], 2 * l + 1)
                    link(V.tensor_scalar(x1, bank[i][0:HY_H, 0:SEQ], fc[2 * i], fc[1], ALU.add, ALU.mult))
                    x2 = nrm[0:HY_H, 1, 0:SEQ]
                    link(V.tensor_scalar(x2, x1, 1.0 / TWO_PI, 12582912.0, ALU.mult, ALU.add))
                    link(V.tensor_scalar(x2, x2, -12582912.0, None, ALU.add))
                    link(V.scalar_tensor_tensor(x1, x2, -6.28125, x1, ALU.mult, ALU.add))
                    link(V.scalar_tensor_tensor(x1, x2, -0.0019350051879882812, x1, ALU.mult, ALU.add))
                    link(V.scalar_tensor_tensor(x1, x2, -3.0199157663445e-07, x1, ALU.mult, ALU.add))
                    V.tensor_scalar(x0, x1, 3.1415925, -3.1415925, ALU.min, ALU.max).then_inc(f_d[l], 1)
                for o in range(HY_O):
                    dve.wait_ge(f_p[l], 6 * l + 3 + 2 * o)
                    for i in range(2):
                        for j in range(2):
                            link(V.tensor_tensor(fraw[:, i, j, :], bank[2 * i + j][:, :], decay[:, j, :], ALU.mult))
                    link(V.memset(fraw[0:1, 1, 0, :], 0.0))
                    link(V.tensor_tensor(fpm[:, 0], fraw[:, 0], fraw[:, 1], ALU.add))
                    link(V.tensor_tensor(fpm[:, 1], fraw[:, 0], fraw[:, 1], ALU.subtract))
                    link(V.scalar_tensor_tensor(fraw[:, 0], fraw[:, 0], -1.0, fraw[:, 0], ALU.mult, ALU.max))
                    link(V.scalar_tensor_tensor(fraw[:, 1], fraw[:, 1], -1.0, fraw[:, 1], ALU.mult, ALU.max))
                    V.tensor_tensor(fabs_, fraw[:, 0], fraw[:, 1], ALU.add).then_inc(f_d[l], 1)
                    dve.wait_ge(f_p[l], 6 * l + 4 + 2 * o)
                    link(V.reciprocal(fnorm, bank[7][:, :]))
                    for f in range(4):
                        link(V.tensor_tensor(spec[:, o, f, :], bank[f][:, :], fnorm, ALU.mult))
                    V.tensor_tensor(spec[0:1, o, 2, :], bank[4][0:1, :], fnorm[0:1, :], ALU.mult).then_inc(f_d[l], 1)
                dve.wait_ge(ring_used, l * LAYER_C + MOD_C)
                pm = bank[5][:, 0:2 * MOD_T].rearrange("p (m s) -> p m s", s=2)
                for s in range(2):
                    link(V.tensor_tensor(mods[:, :, s], pm[:, :, s], pc[:, C_BMOD:C_BMOD + MOD_T], ALU.add))
                for w in range(2):
                    for s in range(2):
                        link(V.scalar_tensor_tensor(gs[:, w, :, s], mods[:, (3 * w + 1) * DK:(3 * w + 2) * DK, s], 1.0,
                                                    pc[:, C_G1 + 8 * w:C_G1 + 8 * w + 8], ALU.add, ALU.mult))
                V.tensor_scalar(half_gate[:], mods[:, 2 * DK:3 * DK, :], 0.5, None, ALU.mult).then_inc(m_d[l], 1)
                dve.wait_ge(m_d[l], l + 1)
                norm_dve(2 * l, NT)
                for g in range(12):
                    dve.wait_ge(j_c[l], g + 1)
                    dst = hv[:, g, 0:T] if g < 4 else hx[:, (g - 4) // 4, g % 4, 0:T]
                    dst = dst.rearrange("p (s t) -> p s t", t=SEQ)
                    src = bank[g % 4][:, 0:T].rearrange("p (s t) -> p s t", t=SEQ)
                    link(V.scalar_tensor_tensor(dst[:, :, 1:SEQ], src[:, :, 0:SEQ - 1], pc[:, C_TAP + g:C_TAP + g + 1],
                                                dst[:, :, 1:SEQ], ALU.mult, ALU.add))
                    V.scalar_tensor_tensor(dst[:, :, 0:SEQ - 1], src[:, :, 1:SEQ],
                                           pc[:, C_TAP + 24 + g:C_TAP + 25 + g], dst[:, :, 0:SEQ - 1],
                                           ALU.mult, ALU.add).then_inc(j_d[l], 1)
                link(V.memset(up[:, :, 0:POOL_PAD], 0.0))
                link(V.memset(up[:, :, POOL_PAD + SEQ:POOL_L], 0.0))
                for c in range(BK):
                    dve.wait_ge(j_pe[l], 12 + c + 1)
                    link(V.tensor_copy(up[:, 0:S, POOL_PAD:POOL_PAD + SEQ],
                                       bank[(12 + c) % 4][:, 0:T].rearrange("p (s t) -> p s t", t=SEQ)))
                    lo, hi = 1, POOL_L
                    link(V.tensor_tensor(ps_a[:, 0:S, lo:hi], up[:, 0:S, lo - 1:hi - 1], up[:, 0:S, lo:hi], ALU.add))
                    src, dst = ps_a, ps_b
                    for i in range(c):
                        h = 1 << i
                        lo, hi = lo + h, hi - h
                        link(V.tensor_tensor(dst[:, 0:S, lo:hi], src[:, 0:S, lo - h:hi - h], src[:, 0:S, lo + h:hi + h],
                                             ALU.add))
                        src, dst = dst, src
                    for s in range(S):
                        for x, t in ((0, 0), (8, SEQ - 8)):
                            v = src[:, s, POOL_PAD + t:POOL_PAD + t + 8]
                            link(V.tensor_tensor(v, v, edge[:, c, x:x + 8], ALU.mult))
                    V.scalar_tensor_tensor(ypool[:, c, 0:T].rearrange("p (s t) -> p s t", t=SEQ),
                                           src[:, 0:S, POOL_PAD:POOL_PAD + SEQ], 1.0 / (2 << c),
                                           up[:, 0:S, POOL_PAD:POOL_PAD + SEQ], ALU.mult, ALU.subtract
                                           ).then_inc(j_d[l], 1)
                    dve.wait_ge(j_d[l], 12 + c + 1)
                dve.wait_ge(pw_a[l], 4 * l + BK)
                n = 0
                for o in range(HY_O):
                    for s in range(S):
                        if n:
                            dve.wait_ge(y_i[l], BK * n)
                        for h in range(2):
                            zr, zi = bank[h], bank[2 + h]
                            hr, hi = spec[:, o, h, :], spec[:, o, 2 + h, :]
                            dve.wait_ge(y_f[l], 4 * n + 2 * h + 2)
                            link(V.tensor_tensor(hy_t[:, 0, :], zr[:, :], hr, ALU.mult))
                            link(V.tensor_tensor(hy_t[:, 1, :], zi[:, :], hi, ALU.mult))
                            link(V.tensor_tensor(hy_y[:, h, :], hy_t[:, 0, :], hy_t[:, 1, :], ALU.subtract))
                            link(V.tensor_tensor(hy_t[:, 0, :], zr[:, :], hi, ALU.mult))
                            link(V.tensor_tensor(hy_t[:, 1, :], zi[:, :], hr, ALU.mult))
                            last = V.tensor_tensor(hy_y[:, 2 + h, :], hy_t[:, 0, :], hy_t[:, 1, :], ALU.add)
                            if h == 0:
                                link(last)
                                link(V.tensor_tensor(hy_y[0:1, 0, :], zr[0:1, :], hr[0:1, :], ALU.mult))
                                last = V.tensor_tensor(hy_y[0:1, 2, :], zi[0:1, :], hi[0:1, :], ALU.mult)
                            last.then_inc(y_m[l], 1)
                            dve.wait_ge(y_m[l], 2 * n + h + 1)
                        for c in range(BK):
                            dve.wait_ge(y_i[l], BK * n + c + 1)
                            z = hv[:, c, s * SEQ:(s + 1) * SEQ]
                            sk = C_SKIP + o * BK + c
                            link(V.scalar_tensor_tensor(hy_t[:, 0, 0:SEQ], z, pc[:, sk:sk + 1],
                                                        bank[6 + c % 2][:, 0:SEQ], ALU.mult, ALU.add))
                            V.tensor_tensor(z, hy_t[:, 0, 0:SEQ], hx[:, o, c, s * SEQ:(s + 1) * SEQ], ALU.mult
                                            ).then_inc(y_z[l], 1)
                            dve.wait_ge(y_z[l], BK * n + c + 1)
                        n += 1
                for i, (src, dst) in enumerate(((qT, qrot), (kT, krot))):
                    for c in range(BK):
                        u = i * BK + c
                        dve.wait_ge(r_pe[l], 8 * l + u + 1)
                        link(V.tensor_tensor(rtmp[:, 0, :], bank[6 + u % 2][:, 0:SEQ], rope[:, 1, :], ALU.mult))
                        link(V.tensor_tensor(rtmp[:, 1, :], src[:, c, 0:SEQ], rope[:, 0, :], ALU.mult))
                        V.tensor_tensor(dst[:, c, :], rtmp[:, 0, :], rtmp[:, 1, :], ALU.add).then_inc(r_d[l], 1)
                        dve.wait_ge(r_d[l], 8 * l + u + 1)
                units = units_of[l]
                U = len(units)

                def maxes(h):
                    dve.wait_ge(b_ld[l][h % 2], 16 * (h // 2 + 1))
                    v = bias[:, h % 2]
                    V.tensor_tensor(v, v, colmask[:].unsqueeze(1).to_broadcast([P, 6, GRID]), ALU.add
                                    ).then_inc(b_fix[l], 1)
                    dve.wait_ge(b_fix[l], h + 1)
                    for i, (x, s) in enumerate(units):
                        dve.wait_ge(a_sc[l], h * U + i + 1)
                        b = bank[i]
                        w = NT if s == 0 else SEQ
                        if s == 0:
                            k0 = 2 - 2 * x
                            link(V.tensor_tensor(b[:, 0:SEQ].rearrange("p (s j) -> p s j", s=4),
                                                 b[:, 0:SEQ].rearrange("p (s j) -> p s j", s=4),
                                                 v[:, k0:k0 + 4, :], ALU.add))
                        if h:
                            dve.wait_ge(a_nm[l], (h - 1) * U + i + 1)
                        V.tensor_reduce(pstat[:, i, 0:1], b[:, 0:w], AX.X, ALU.max, negate=True).then_inc(a_mx[l], 1)

                def probs(h):
                    for i, (x, s) in enumerate(units):
                        dve.wait_ge(a_ex[l], h * U + i + 1)
                        w = NT if s == 0 else SEQ
                        link(V.reciprocal(pstat[:, i, 2:3], pstat[:, i, 1:2]))
                        V.tensor_scalar(prob[:, i, 0:w], prob[:, i, 0:w], pstat[:, i, 2:3], None, ALU.mult
                                        ).then_inc(a_nm[l], 1)

                maxes(0)
                for h in range(HEADS):
                    probs(h)
                    if h + 1 < HEADS:
                        maxes(h + 1)
                dve.wait_ge(a_o[l], HEADS)
                V.memset(merged, 0.0).then_inc(g_d[l], 2)
                dve.wait_ge(g_d[l], 2)
                with dve.Fori(0, 3) as n:
                    for m in range(DK):
                        dve.wait_ge(g_t[l], n * DK + (m + 1))
                        dve.wait_ge(g_pe[l], n * (2 * DK) + (2 * m + 2))
                        dve.wait_ge(g_d[l], n * DK + (m + 2))
                        V.scalar_tensor_tensor(mtmp[:, 0:T], gate_t[:, m % 2, 0:T], 1.0, bank[2 + m % 2][:, 0:T],
                                               ALU.add, ALU.mult).then_inc(dve_c, 1)
                        dve.wait_ge(dve_c, n * DK + (chain[0] + m + 1))
                        V.tensor_tensor(merged[:, m, 0:T], merged[:, m, 0:T], mtmp[:, 0:T], ALU.add
                                        ).then_inc(g_d[l], 1)
                chain[0] += 3 * DK
                for m in range(DK):
                    dve.wait_ge(o_pe[l], m + 1)
                    for s in range(S):
                        v = xT[:, m, s * SEQ:(s + 1) * SEQ]
                        V.scalar_tensor_tensor(v, bank[m % 2][:, s * SEQ:(s + 1) * SEQ], half_gate[:, m, s:s + 1], v,
                                               ALU.mult, ALU.add).then_inc(o_d[l], 1)
                dve.wait_ge(o_d[l], 8 * S)
                norm_dve(2 * l + 1, T)
                nt = T // P
                NE = nt * E_N
                G4 = nt * 4

                def r16(i):
                    return rt[:, i, 0:NE]

                def r4(i):
                    return rt[:, i, 0:NE].rearrange("p (g k) -> p g k", k=4)

                def r1(i):
                    return rt[:, i, 0:G4]

                def rje(i):
                    return rt[:, i, 0:NE].rearrange("p (j e) -> p j e", e=E_N)

                dve.wait_ge(q_ex[l], l + 1)
                link(V.tensor_scalar(r16(2), r16(1), 1.0, None, ALU.add))
                link(V.reciprocal(r16(1), r16(2)))
                link(V.tensor_tensor(rje(2), rje(1), rbias[:].unsqueeze(1).to_broadcast([P, nt, E_N]), ALU.add))

                def place(src, dst, n, view):
                    link(V.memset(dst, 0.0))
                    v, d = view(src), view(dst)
                    for i in range(n):
                        for j in range(i + 1, n):
                            t = rt[:, 30, 0:v.shape[1]]
                            link(V.tensor_tensor(t, v[:, :, i], v[:, :, j], ALU.is_ge))
                            link(V.tensor_tensor(d[:, :, j], d[:, :, j], t, ALU.add))
                            link(V.scalar_tensor_tensor(d[:, :, i], d[:, :, i], 1.0, t, ALU.add, ALU.subtract))

                place(r16(2), r16(3), 4, lambda v: v.rearrange("p (g k) -> p g k", k=4))
                link(V.tensor_scalar(r16(4), r16(3), 1.5, None, ALU.is_lt))
                link(V.tensor_tensor(r16(5), r16(4), r16(2), ALU.mult))
                link(V.tensor_reduce(r1(6), r4(5), AX.X, ALU.add))
                place(r1(6), r1(7), 4, lambda v: v.rearrange("p (j g) -> p j g", g=4))
                link(V.tensor_scalar(r1(8), r1(7), 0.5, None, ALU.is_lt))
                V.tensor_tensor(r4(0), r4(4), r1(8).unsqueeze(2).to_broadcast([P, G4, 4]), ALU.mult
                                ).then_inc(q_m[l], 1)
                dve.wait_ge(q_m[l], l + 1)
                link(V.tensor_tensor(r16(9), r16(0), r16(1), ALU.mult))
                link(V.tensor_reduce(rt[:, 10, 0:nt], rje(9), AX.X, ALU.add))
                link(V.reciprocal(rt[:, 11, 0:nt], rt[:, 10, 0:nt]))
                link(V.tensor_scalar(rt[:, 11, 0:nt], rt[:, 11, 0:nt], 0.5, None, ALU.mult))
                link(V.tensor_tensor(rje(9), rje(9), rt[:, 11, 0:nt].unsqueeze(2).to_broadcast([P, nt, E_N]), ALU.mult))
                dve.wait_ge(q_rk[l], l + 1)
                link(V.tensor_tensor(rje(12), bank[7][:, 0:NE].rearrange("p (j e) -> p j e", e=E_N),
                                     slot0[:].unsqueeze(1).to_broadcast([P, nt, E_N]), ALU.add))
                for i in range(1, nt):
                    link(V.tensor_scalar(rje(18), bank[7][:, 0:NE].rearrange("p (j e) -> p j e", e=E_N),
                                         float(i * P), float((E_N - 1) * P), ALU.is_ge, ALU.mult))
                    link(V.tensor_tensor(r16(12), r16(12), r16(18), ALU.add))
                link(V.scalar_tensor_tensor(r16(12), r16(12), 1.0, r16(0), ALU.add, ALU.mult))
                link(V.tensor_reduce(rt[:, 13, 0:nt], rje(12), AX.X, ALU.max))
                link(V.tensor_reduce(rt[:, 14, 0:nt], rje(12), AX.X, ALU.add))
                link(V.tensor_tensor(rt[:, 14, 0:nt], rt[:, 14, 0:nt], rt[:, 13, 0:nt], ALU.subtract))
                link(V.tensor_scalar(didx[:, 0, 0:nt], rt[:, 14, 0:nt], -1.0, None, ALU.add))
                link(V.tensor_scalar(didx[:, 1, 0:nt], rt[:, 13, 0:nt], -1.0, None, ALU.add))
                link(V.tensor_reduce(rt[:, 15, 0:1], bank[7][:, 64:64 + E_N], AX.X, ALU.max))
                V.tensor_copy(cnt_u[:], rt[:, 15, 0:1]).then_inc(q_ix[l], 1)
                link(V.tensor_tensor(rje(16), rje(12), rt[:, 13, 0:nt].unsqueeze(2).to_broadcast([P, nt, E_N]),
                                     ALU.is_equal))
                link(V.tensor_tensor(r16(16), r16(16), r16(9), ALU.mult))
                link(V.tensor_reduce(wsel[:, 1, 0:nt], rje(16), AX.X, ALU.add))
                link(V.tensor_reduce(rt[:, 17, 0:nt], rje(9), AX.X, ALU.add))
                link(V.tensor_tensor(wsel[:, 0, 0:nt], rt[:, 17, 0:nt], wsel[:, 1, 0:nt], ALU.subtract))
                dve.wait_ge(q_tt[l], l + 1)
                V.tensor_copy(tidx[:], bank[6][:, 64:128]).then_inc(q_ti[l], 1)

                def rows_in(par_, e):
                    dve.wait_ge(x_tr[l], 16 * l + e + 1)
                    V.tensor_copy(heT[:, par_, 4:8, :], bank[1][:, :].rearrange("p (k t) -> p k t", k=4)
                                  ).then_inc(x_hd[l], 1)

                def hidden(par_, s):
                    dve.wait_ge(x_th[l], 16 * l + s + 1)
                    V.scalar_tensor_tensor(thb[:, par_, :], thb[:, par_, :], 1.0, bank[2][:, :], ALU.add, ALU.mult
                                           ).then_inc(x_th2[l], 1)
                    dve.wait_ge(x_th2[l], 16 * l + s + 1)
                    V.tensor_tensor(hid[:, par_, :], thb[:, par_, :], bank[3][:, :], ALU.mult).then_inc(x_hid[l], 1)

                def y_out(par_, s, free):
                    dve.wait_ge(x_y[l], 16 * l + s + 1)
                    if free is not None:
                        dve.wait_ge(x_st[l][par_], free)
                    V.tensor_copy(yb[:, par_, 512:1024], bank[6][:, :]).then_inc(x_yd[l], 1)

                rows_in(0, 0)
                hidden(0, 0)
                rows_in(1, 1)
                for s in (1, 2):
                    hidden(s % 2, s)
                    y_out((s - 1) % 2, s - 1, None)
                    rows_in((s + 1) % 2, s + 1)
                with dve.Fori(1, 7) as i:
                    hidden(1, 2 * i + 1)
                    y_out(0, 2 * i, i * 16)
                    rows_in(0, 2 * i + 2)
                    hidden(0, 2 * i + 2)
                    y_out(1, 2 * i + 1, i * 16)
                    rows_in(1, 2 * i + 3)
                hidden(1, 15)
                y_out(0, 14, 16 * 7)
                y_out(1, 15, 16 * 7)
                most = dve.value_load(cnt_u[0:1, 0:1], min_val=0, max_val=NT)
                with dve.If(most > P):
                    for i in range(2):
                        dve.wait_ge(x_st[l][i], 16 * E_N // 2)
                    with dve.Fori(0, (nt - 1) * E_N) as b:
                        V.tensor_copy(over_idx[:], tidx[:, bass.ds(b + E_N, 1)]).then_inc(v_d[l], 1)
                        dve.wait_ge(v_pe[l], b * 4 + 1)
                        V.tensor_copy(heT[:, 0, 0:4, :], bank[0][:, :].rearrange("p (k t) -> p k t", k=4))
                        V.tensor_copy(heT[:, 0, 4:8, :], bank[1][:, :].rearrange("p (k t) -> p k t", k=4)
                                      ).then_inc(v_d[l], 1)
                        dve.wait_ge(v_a[l], b + 1)
                        V.scalar_tensor_tensor(thb[:, 0, :], thb[:, 0, :], 1.0, bank[2][:, :], ALU.add, ALU.mult
                                               ).then_inc(v_d[l], 1)
                        dve.wait_ge(v_d[l], b * 6 + 3)
                        V.tensor_tensor(hid[:, 0, :], thb[:, 0, :], bank[3][:, :], ALU.mult).then_inc(v_d[l], 1)
                        dve.wait_ge(v_pe[l], b * 4 + 3)
                        V.tensor_copy(hidT[:, 0, :, :], bank[4][:, :].rearrange("p (k t) -> p k t", k=4)
                                      ).then_inc(v_d[l], 1)
                        dve.wait_ge(v_pe[l], b * 4 + 4)
                        V.tensor_copy(yb[:, 0, 0:512], bank[5][:, :])
                        V.tensor_copy(yb[:, 0, 512:1024], bank[6][:, :]).then_inc(v_d[l], 1)
                with dve.Else():
                    dve.nop()
                dve.wait_ge(z_g[l], 32 * nt)
                for j in range(nt):
                    link(V.tensor_scalar(fa[:, j, :], fa[:, j, :], wsel[:, 0, j:j + 1], None, ALU.mult))
                    V.scalar_tensor_tensor(fa[:, j, :], fb[:, j, :], wsel[:, 1, j:j + 1], fa[:, j, :],
                                           ALU.mult, ALU.add).then_inc(z_f[l], 1)
                for k in range(DK):
                    dve.wait_ge(z_t[l], k + 1)
                    for s in range(S):
                        v = xT[:, k, s * SEQ:(s + 1) * SEQ]
                        V.scalar_tensor_tensor(v, bank[k][:, s * SEQ:(s + 1) * SEQ], mods[:, 5 * DK + k, s:s + 1], v,
                                               ALU.mult, ALU.add).then_inc(z_x[l], 2 // S)
                dve.wait_ge(z_x[l], 16)
            norm_dve(4, SEQ)


def shape_constants():
    import numpy as np
    n = SEQ
    t = np.arange(n, dtype=np.float64)
    f = np.arange(n, dtype=np.float64)
    ang = 2 * np.pi * np.outer(t, f) / (2 * n)
    cos, sin = np.cos(ang), np.sin(ang)
    alt = (-1.0) ** t
    fwd = np.concatenate([cos, -sin], axis=1)
    fwd[:, n] = alt
    inv = np.concatenate([2 * cos.T, -2 * sin.T], axis=0) / (2 * n)
    inv[0] = 1.0 / (2 * n)
    inv[n] = alt / (2 * n)
    c = {}
    c["dft_f"] = fwd.reshape(2, P, 512).transpose(1, 0, 2)
    c["dft_i"] = inv.reshape(4, P, n).transpose(1, 0, 2)
    c["nyq"] = alt.reshape(2, P).T
    ident = np.eye(P)
    perm = np.zeros((P, P))
    for m in range(P):
        if m % 64 < 32:
            perm[m + 32, m] = -1.0
        else:
            perm[m - 32, m] = 1.0
    tri = np.triu(np.ones((P, P)), 1)
    c["square"] = np.stack([ident, perm, tri, np.ones((P, P))], axis=1)
    nf = DH // 4
    inv_f = (10000.0 ** (-np.arange(nf, dtype=np.float32) / nf)).astype(np.float32)
    row = (np.arange(n) // GRID).astype(np.float32)
    col = (np.arange(n) % GRID).astype(np.float32)
    an = np.concatenate([row[:, None] * inv_f, col[:, None] * inv_f], axis=-1)
    idx = np.arange(P) % 32
    c["rope"] = np.stack([np.cos(an)[:, idx].T, np.sin(an)[:, idx].T], axis=1)
    j = np.arange(GRID)
    st = np.clip(j - KW // 2, 0, GRID - KW)
    ok = (j[None, :] >= st[:, None]) & (j[None, :] < st[:, None] + KW)
    c["colmask"] = np.tile(np.where(ok, 0.0, -1e30), (2, 1))
    edge = np.ones((BK, 16))
    for g in range(BK):
        w = 2 << g
        for x in range(16):
            tt = x if x < 8 else n - 16 + x
            edge[g, x] = w / (min(tt + w - w // 2, n) - max(tt - w // 2, 0))
    c["edge"] = np.broadcast_to(edge, (P, BK, 16))
    c["slot0"] = np.broadcast_to(np.arange(E_N) * P, (P, E_N))
    c["tok_id"] = np.arange(4)[None, :] * P + np.arange(P)[:, None]
    tl = np.linspace(0.0, 1.0, n, dtype=np.float32)
    bands = (HY_E - 1) // 2
    fr = np.linspace(1e-4, bands - 1, bands, dtype=np.float32)
    an = np.float32(2.0 * np.pi / n) * np.arange(n, dtype=np.float32)
    z = np.concatenate([tl[:, None], np.cos(fr[None, :] * an[:, None]), -np.sin(fr[None, :] * an[:, None])], axis=-1)
    c["filter_in"] = z.T
    lo, hi = np.log(1e-2) / 0.3, np.log(1e-2) / 1.5
    deltas = np.abs(np.linspace(lo, hi, BW, dtype=np.float32))
    c["decay"] = np.exp(-tl[:, None] * deltas).reshape(2, P, BW).transpose(1, 0, 2)
    return {k: np.ascontiguousarray(v, dtype=np.float32) for k, v in c.items()}


def kernel(x, c, ctx, c_ctx, norm1_g, norm2_g, w_mod, b_mod, w_in, rpb, pool_w, pool_scale,
           hy_short_w, hy_short_b, hy_w1, hy_b1, hy_freq, hy_w2, hy_b2, hy_w3, hy_skip,
           w_branch, w_out, w_router, router_bias, w_gate_e, w_up_e, w_down_e, final_g):
    import numpy as np
    import concourse.bacc as bacc
    from concourse.bass_utils import run_bass_kernel_spmd

    def cols(v):
        return np.asarray(v).reshape(-1, P).T

    data = dict(shape_constants())
    tokens = np.concatenate([np.asarray(x)[0], np.asarray(ctx)[0]], axis=0)
    data["x_cols"] = tokens.T.reshape(DK, P, NT).transpose(1, 0, 2)
    data["c_cols"] = np.stack([cols(np.asarray(c)[0]), cols(c_ctx)], axis=2).reshape(P, DK * 2)
    for l in range(DEPTH):
        filt = np.zeros((P, 3), np.float32)
        filt[0:HY_H, 0] = hy_b1[l]
        filt[0:HY_H, 1] = hy_freq[l]
        filt[0:HY_H, 2] = hy_b2[l]
        data[f"par{l}"] = np.concatenate(
            [cols(norm1_g[l]), cols(norm2_g[l]), cols(b_mod[l]), cols(pool_scale[l])]
            + [cols(hy_short_w[l, i]) for i in range(NTAP)] + [cols(hy_short_b[l])]
            + [cols(hy_skip[l, i]) for i in range(HY_O)] + [filt], axis=1)
    pad = np.zeros((DEPTH, HEADS, 15, 128), np.float32)
    pad[:, :, :, 63 - (KW - 1):63 + KW] = rpb
    r, q, slot, k = np.ix_(range(2), range(GRID), range(6), range(GRID))
    data["rpb_win"] = pad[:, :, 5 - r + slot, 63 + k - q].reshape(DEPTH, HEADS, P, 6, GRID)
    data["fin_g"] = cols(final_g)
    data["w_router"] = np.asarray(w_router).reshape(DK, P, E_N).transpose(1, 0, 2)
    data["router_bias"] = np.broadcast_to(np.asarray(router_bias), (P, E_N))
    for name, v in (("w_mod", w_mod), ("w_in", w_in), ("pool_w", pool_w), ("hy_w1", hy_w1), ("hy_w2", hy_w2),
                    ("hy_w3", hy_w3), ("w_branch", w_branch), ("w_out", w_out), ("w_gate_e", w_gate_e),
                    ("w_up_e", w_up_e), ("w_down_e", w_down_e)):
        data[name] = v
    nc = bacc.Bacc("TRN2", target_bir_lowering=False, num_devices=1)
    arrays, aps = {}, {}
    for name, v in data.items():
        v = np.ascontiguousarray(v)
        arrays[f"in_{name}"] = v
        aps[name] = nc.dram_tensor(f"in_{name}", v.shape, mybir.dt.from_np(v.dtype), kind="ExternalInput").ap()
    out = nc.dram_tensor("out", (1, SEQ, D), F32, kind="ExternalOutput").ap()
    build(nc, aps, out)
    r = run_bass_kernel_spmd(nc, [arrays], core_ids=[0])
    return r.results[0]["out"]
```

```python
from contextlib import ExitStack

import concourse.bass as bass
from concourse import mybir

P = 128
D = 1024
DK = D // P
SEQ = 256
CTX = 256
NT = SEQ + CTX
DEPTH = 2
BW = D // 2
BK = BW // P
HEADS = 8
DH = 64
GRID = 64
KW = 16
E_N = 16
FF = 512
FK = FF // P
N_MOD = 6
MOD_T = N_MOD * DK
NTAP = 3
HY_H = 64
HY_E = 33
HY_O = 2
EPS = 1e-6
RPB_W = 2 * KW - 1

F32 = mybir.dt.float32
F32R = mybir.dt.float32r
U32 = mybir.dt.uint32
ALU = mybir.AluOpType
ACT = mybir.ActivationFunctionType
AX = mybir.AxisListType

RS = 3
RW = 2048
WS = 4
AHEAD = 2
MOD_C = 24
IN_C = 14
MERGE_C = 18
OUT_C = 4
PRE_C = MOD_C + IN_C + MERGE_C + OUT_C
EXP_C = 6 * E_N
LAYER_C = PRE_C + EXP_C
HALVES = 2 * (IN_C + 2 * MERGE_C // 3 + OUT_C)
DIRECT_C = LAYER_C - HALVES // 2

C_G1, C_G2, C_BMOD = 0, 8, 16
C_PS = C_BMOD + MOD_T
C_TAP = C_PS + BK
C_SB = C_TAP + NTAP * 12
C_SKIP = C_SB + 12
C_FILT = C_SKIP + HY_O * BK
C_N = C_FILT + 3
IN_ORDER = [8, 9, 10, 11, 12, 13, 6, 7, 0, 1, 2, 3, 4, 5]
GATE_C0 = 14
POOL_PAD = 8
POOL_L = SEQ + 2 * POOL_PAD
TWO_PI = 6.283185307179586


def build(nc, a, out):
    ctx = ExitStack()
    with ctx:
        def sb(name, shape, dt=F32):
            return ctx.enter_context(nc.sbuf_tensor(name, shape, dt))

        def sem(name):
            return ctx.enter_context(nc.semaphore(name))

        def sems(name, n=DEPTH):
            return [sem(f"{name}{i}") for i in range(n)]

        def both(name):
            return [sem(name)] * DEPTH

        def tcols(l):
            return NT if l == 0 else SEQ

        def streams(l):
            return 2 if l == 0 else 1

        h_rows = [nc.dram_tensor(f"h_rows{l}", [NT, D], F32).ap() for l in range(DEPTH)]
        y_rows = [nc.dram_tensor(f"y_rows{l}", [E_N * tcols(l), D], F32).ap() for l in range(DEPTH)]
        slot_tok = [nc.dram_tensor(f"slot_tok{l}", [E_N * NT, 1], F32).ap() for l in range(DEPTH)]

        ring = sb("ring", [P, RS, RW])
        xT = sb("xT", [P, DK, NT])
        h_hi = sb("h_hi", [P, DK, NT], F32R)
        h_lo = sb("h_lo", [P, DK, NT], F32R)
        w_hi = sb("w_hi", [P, WS, DK, P], F32R)
        w_lo = sb("w_lo", [P, WS, DK, P], F32R)
        dft_f = sb("dft_f", [P, 2, 512])
        dft_i = sb("dft_i", [P, 4, SEQ])
        square = sb("square", [P, 4, P])
        ident, perm, tri, ones = (square[:, i, :] for i in range(4))
        edge = sb("edge", [P, BK, 16])
        nyq = sb("nyq", [P, 2])
        sel2 = sb("sel2", [P, 2])
        csil = sb("csil", [P, DK, 32])
        slot0 = sb("slot0", [P, E_N])
        tok_id = sb("tok_id", [P, 4])
        par = [sb(f"par{l}", [P, C_N]) for l in range(DEPTH)]
        fin_g = sb("fin_g", [P, DK])
        cc = sb("cc", [P, 3, DK * 2])
        poolw = sb("poolw", [P, BK, P])
        rbias = sb("rbias", [P, E_N])
        mods = sb("mods", [P, MOD_T, 2])
        gs = sb("gs", [P, 2, DK, 2])
        half_gate = sb("half_gate", [P, DK, 2])
        small = sb("small", [P, 16])
        MIX = 22528
        mix = sb("mix", [P, MIX])

        def area(o, n):
            assert o + n <= MIX
            return mix[:, o:o + n]

        ys = area(0, 6144).rearrange("p (n c t) -> p n c t", n=3, c=BK)
        qT = ys[:, 0]
        ys_pool = ys[:, 1]
        hv = ys[:, 2]
        kT = area(6144, 2048).rearrange("p (c t) -> p c t", c=BK)
        vtok = area(8192, 2048).rearrange("p (j f) -> p j f", j=4)
        hx = area(10240, 4096).rearrange("p (o c t) -> p o c t", o=2, c=BK)
        spec = area(14336, 4096).rearrange("p (o f c) -> p o f c", o=2, f=4)
        work = area(18432, 4096)
        merged = area(6144, 4096).rearrange("p (k t) -> p k t", k=DK)
        hT = area(10240, 4096).rearrange("p (k t) -> p k t", k=DK)
        w3s = area(0, 2048)[0:HY_H, :]
        decay = area(2048, 1024).rearrange("p (j c) -> p j c", j=2)
        fz = area(3072, 256)[0:HY_E, :]
        fw1 = area(3328, 64)[0:HY_E, :]
        fw2 = area(3392, 64)[0:HY_H, :]
        fhid = area(3456, 3 * 256).rearrange("p (i t) -> p i t", i=3)
        fpm = area(4352, 2048).rearrange("p (i j c) -> p i j c", i=2, j=2)
        fraw = area(6400, 2048).rearrange("p (i j c) -> p i j c", i=2, j=2)
        fabs_ = area(8448, 1024).rearrange("p (j c) -> p j c", j=2)
        fnorm = area(9472, 512)
        mrow = area(10240, 1024).rearrange("p (i c) -> p i c", i=2)
        sqb = area(18432, 1024).rearrange("p (i t) -> p i t", i=2)
        nrm = area(18432 + 1024, 2048).rearrange("p (i t) -> p i t", i=4)
        up = work[:, 0:2 * POOL_L].rearrange("p (s t) -> p s t", s=2)
        ps_a = work[:, 576:576 + 2 * POOL_L].rearrange("p (s t) -> p s t", s=2)
        ps_b = work[:, 1152:1152 + 2 * POOL_L].rearrange("p (s t) -> p s t", s=2)
        ypool = work[:, 2048:4096].rearrange("p (c t) -> p c t", c=BK)
        zt = work[:, 0:1024].rearrange("p (j c) -> p j c", j=2)
        hy_y = work[:, 1024:3072].rearrange("p (f c) -> p f c", f=4)
        hy_t = work[:, 3072:4096].rearrange("p (i c) -> p i c", i=2)
        qrot = area(14336, 1024).rearrange("p (c t) -> p c t", c=BK)
        krot = area(15360, 1024).rearrange("p (c t) -> p c t", c=BK)
        rtmp = area(16384, 512).rearrange("p (i t) -> p i t", i=2)
        rope = area(16896, 512).rearrange("p (i t) -> p i t", i=2)
        colmask = area(17408, GRID)
        wrt = area(17472, DK * E_N).rearrange("p (k e) -> p k e", k=DK)
        prob = work[:, 0:2048].rearrange("p (u t) -> p u t", u=4)
        bias = work[:, 2048:2048 + 768].rearrange("p (i s j) -> p i s j", i=2, s=6)
        pstat = work[:, 2816:2816 + 32].rearrange("p (u i) -> p u i", u=4)
        pT_s = area(10240, 3072).rearrange("p (i k t) -> p i k t", i=2, k=6)
        gate_t = work[:, 0:1024].rearrange("p (i t) -> p i t", i=2)
        mtmp = work[:, 1024:1536]
        htok = area(0, 4096).rearrange("p (j d) -> p j d", j=4)
        rt = area(4096, 2048).rearrange("p (i x) -> p i x", i=32)
        ids_f = area(6144, 128)[0:64, :]
        tidx = sb("tidx", [P, 64], U32)
        didx = sb("didx", [P, 2, 4], U32)
        cnt_u = sb("cnt_u", [P, 1], U32)
        wsel = sb("wsel", [P, 2, 4])
        zero_ids = area(6272, 64)
        hg = area(8192, 2048).rearrange("p (i d) -> p i d", i=2)
        heT = area(10240, 2048).rearrange("p (i k t) -> p i k t", i=2, k=DK)
        hid = area(12288, 1024).rearrange("p (i f) -> p i f", i=2)
        thb = area(13312, 1024).rearrange("p (i f) -> p i f", i=2)
        hidT = area(14336, 1024).rearrange("p (i k t) -> p i k t", i=2, k=FK)
        yb = area(15360, 2048).rearrange("p (i d) -> p i d", i=2)
        over_w = [area(0, 4096), area(17408, 4096)]
        over_idx = sb("over_idx", [P, 1], U32)
        fa = area(0, 4096).rearrange("p (j d) -> p j d", j=4)
        fb = area(8192, 4096).rearrange("p (j d) -> p j d", j=4)

        bank = [ctx.enter_context(nc.psum_tensor(f"bank{i}", [P, 512], F32)) for i in range(8)]

        s_ld = sem("constants_loaded")
        s_ldl = sems("layer_params_loaded")
        ring_full = [sem(f"ring_full{i}") for i in range(RS)]
        ring_used = sem("ring_used")
        w_h = sem("weight_half_leading")
        w_l = sem("weight_half_split")
        w_u = sem("weight_half_used")
        h_h = sem("operand_leading")
        h_l = sem("operand_split")
        dve_c = sem("dve_chain")
        act_c = sem("act_chain")
        s_ce = sem("c_exp")
        s_cs = sem("c_silu")
        f_p = both("filter_pe")
        f_d = both("filter_dve")
        f_a = both("filter_act")
        m_ev = both("mod_rows_copied")
        m_co = both("mod_columns_ready")
        m_tk = both("mod_columns_taken")
        m_d = both("mod_ready")
        n_sq = sem("norm_squares")
        n_mm = sem("norm_sums")
        n_a = sem("norm_mean")
        n_s = sem("norm_root")
        n_x = sem("norm_scaled")
        n_h = sem("norm_modulated")
        j_pe = sems("proj_products")
        j_c = sems("conv_centre")
        j_d = sems("proj_taken_dve")
        j_a = sems("proj_taken_act")
        pw_pe = both("pool_products")
        pw_a = both("pool_scaled")
        y_tp = sems("z_transposed")
        y_zt = sems("z_rows_ready")
        y_f = sems("spectrum_ready")
        y_m = sems("spectra_multiplied")
        y_i = sems("inverse_ready")
        y_z = sems("z_updated")
        r_ld = both("rope_tables_loaded")
        r_pe = both("rope_swapped")
        r_d = both("rope_ready")
        b_ld = [sems(f"bias_loaded{l}_", 2) for l in range(DEPTH)]
        b_fix = sems("bias_masked")
        a_sc = sems("scores_ready")
        a_mx = sems("score_max_ready")
        a_ex = sems("exp_ready")
        a_nm = sems("probs_ready")
        a_tr = sems("probs_transposed")
        a_ev = sems("probsT_ready")
        a_pv = sems("attention_out")
        a_o = sems("attention_taken")
        g_pe = sems("merge_products")
        g_t = sems("gate_tanh")
        g_d = sems("merge_taken")
        o_pe = sems("out_products")
        o_d = sems("residual_added")
        t_pe = sems("rows_transposed")
        t_ev = sems("rows_copied")
        t_st = sems("rows_stored")
        q_z = both("zeros_ready")
        q_zd = sems("slot_table_cleared")
        q_lg = both("logits_ready")
        q_ex = both("logits_exp")
        q_m = both("experts_chosen")
        q_rk = both("ranks_ready")
        q_ix = both("slots_ready")
        q_sc = sems("slots_scattered")
        q_tb = sems("slot_table_loaded")
        q_tt = both("slot_table_transposed")
        q_ti = both("token_index_ready")
        x_g = [sems(f"rows_gathered{l}_", 2) for l in range(DEPTH)]
        x_tr = both("expert_rows_transposed")
        x_ha = both("expert_in_act")
        x_hd = both("expert_in_dve")
        x_gu = both("gate_up_ready")
        x_th = both("expert_tanh")
        x_th2 = both("gate_silu_ready")
        x_hid = both("hidden_ready")
        x_ht = both("hidden_transposed")
        x_hte = both("hiddenT_ready")
        x_y = both("expert_out_ready")
        x_ya = both("expert_out_act")
        x_yd = both("expert_out_dve")
        x_st = [sems(f"expert_out_stored{l}_", 2) for l in range(DEPTH)]
        v_w = sems("over_gate_up_loaded")
        v_wd = sems("over_down_loaded")
        v_g = sems("over_gathered")
        v_pe = sems("over_products")
        v_a = sems("over_tanh")
        v_d = sems("over_vector")
        v_s = sems("over_stored")
        v_done = sems("over_areas_free")
        v_t = sems("over_wait_taken")
        z_g = sems("combine_gathered")
        z_f = sems("combined")
        z_t = sems("combined_transposed")
        z_x = sems("moe_added")
        e_t = sem("final_transposed")
        e_c = sem("final_copied")
        e_s = sem("output_stored")

        FILT_A, FILT_D, FILT_P = 4, 6, 6
        units_of = [[(x, s) for s in range(streams(l)) for x in range(2)] for l in range(DEPTH)]

        def win(l, c):
            return a["w_in"][l].rearrange("(k p) n -> p k n", p=P)[:, :, c * 256:(c + 1) * 256]

        def chunk_src(l, i):
            if i < IN_C:
                return win(l, IN_ORDER[i]), 8
            i -= IN_C
            if i < MERGE_C:
                n, r = divmod(i, 6)
                h, r = divmod(r, 3)
                if r == 1:
                    v = a["w_branch"][l, n].rearrange("(k p) n -> p k n", p=P)
                    return v[:, :, h * 512:(h + 1) * 512], 4
                return win(l, GATE_C0 + n * 4 + 2 * h + r // 2), 8
            i -= MERGE_C
            return a["w_out"][l].rearrange("(k p) n -> p k n", p=P)[:, :, i * 256:(i + 1) * 256], 8

        def rview(slot, k):
            return ring[:, slot, :].rearrange("p (k n) -> p k n", k=k)

        def merge_chunk(m):
            n, r = divmod(m, DK)
            return 6 * n + 3 * (r // 4) + 2 * (r % 4 // 2)

        split_c = [MOD_C <= i < PRE_C and not (MOD_C + IN_C <= i < PRE_C - OUT_C and (i - MOD_C - IN_C) % 3 == 1)
                   for i in range(LAYER_C)]
        halves_to = [2 * sum(split_c[:i + 1]) for i in range(LAYER_C)]
        direct_to = [i + 1 - sum(split_c[:i + 1]) for i in range(LAYER_C)]

        def full_at(idx):
            return 16 * (idx // RS + 1)

        block = ctx.enter_context(nc.Block())

        @block.sync
        def _(sp):
            for dst, name in ((cc[:, 0, :], "c_cols"), (dft_f[:], "dft_f"), (square[:], "square"), (xT[:], "x_cols"),
                              (dft_i[:], "dft_i"), (edge[:], "edge"),
                              (nyq[:], "nyq"), (sel2[:], "sel2"), (slot0[:], "slot0"), (tok_id[:], "tok_id"), (par[0][:], "par0"),
                              (par[1][:], "par1"), (fin_g[:], "fin_g"), (rbias[:], "router_bias")):
                sp.dma_start(dst, a[name]).then_inc(s_ld, 16)

            for l in range(DEPTH):
                base = l * LAYER_C
                if l:
                    sp.wait_ge(z_x[l - 1], 16)
                sp.dma_start(w3s, a["hy_w3"][l]).then_inc(s_ldl[l], 16)
                sp.dma_start(decay, a["decay"]).then_inc(s_ldl[l], 16)
                sp.dma_start(fz, a["filter_in"]).then_inc(s_ldl[l], 16)
                sp.dma_start(fw1, a["hy_w1"][l]).then_inc(s_ldl[l], 16)
                sp.dma_start(fw2, a["hy_w2"][l]).then_inc(s_ldl[l], 16)
                sp.dma_start(poolw[:], a["pool_w"][l].rearrange("g c d -> c g d")).then_inc(s_ldl[l], 16)
                wm = a["w_mod"][l].rearrange("(h k p) (g n) -> p h k g n", p=P, h=2, n=512)

                def slot_free(c):
                    if c >= RS and split_c[c - RS]:
                        sp.wait_ge(w_l, l * HALVES + halves_to[c - RS])
                    elif l or c >= RS:
                        sp.wait_ge(ring_used, l * DIRECT_C + (direct_to[c - RS] if c >= RS else c + 1 - RS))

                for j in range(2 * RS):
                    slot_free(j)
                    sp.dma_start(rview(j % RS, 4), wm[:, j % 2, :, j // 2, :]).then_inc(ring_full[j % RS], 16)
                with sp.Fori(1, MOD_C // (2 * RS)) as i:
                    for j in range(2 * RS):
                        sp.wait_ge(ring_used, i * (2 * RS) + (l * DIRECT_C + j + 1 - RS))
                        sp.dma_start(rview(j % RS, 4), wm[:, j % 2, :, bass.ds(i * RS + j // 2, 1), :]
                                     ).then_inc(ring_full[j % RS], 16)
                for i in range(PRE_C - MOD_C):
                    src, k = chunk_src(l, i)
                    idx = base + MOD_C + i
                    slot_free(MOD_C + i)
                    sp.dma_start(rview(idx % RS, k), src).then_inc(ring_full[idx % RS], 16)

                wg = a["w_gate_e"][l].rearrange("e (h k p) n -> p e h k n", p=P, h=2)
                wu = a["w_up_e"][l].rearrange("e (h k p) n -> p e h k n", p=P, h=2)
                wd = a["w_down_e"][l].rearrange("e (h k p) n -> p e h k n", p=P, h=2)

                xd = l * DIRECT_C + direct_to[PRE_C - 1]

                def put(c, slot, w, e, h, k):
                    if isinstance(c, int) and c < RS:
                        slot_free(PRE_C + c)
                    else:
                        sp.wait_ge(ring_used, c + (xd - RS + 1))
                    sp.dma_start(rview(slot % RS, k), w[:, bass.ds(e, 1), h].rearrange("p e k n -> p (e k) n")
                                 ).then_inc(ring_full[slot % RS], 16)

                for h in range(2):
                    put(h, h, wg, 0, h, 4)
                for h in range(2):
                    put(2 + h, 2 + h, wu, 0, h, 4)

                def step(s):
                    at = s * 6 - 2
                    for h in range(2):
                        put(at + h, 4 + h, wg, s, h, 4)
                    for h in range(2):
                        put(at + 2 + h, h, wu, s, h, 4)
                    for h in range(2):
                        put(at + 4 + h, 2 + h, wd, s - 1, h, 2)

                with sp.Fori(0, 7) as i:
                    step(2 * i + 1)
                    step(2 * i + 2)
                step(15)
                for h in range(2):
                    put(EXP_C - 2 + h, 4 + h, wd, E_N - 1, h, 2)
                sp.wait_ge(q_ix[l], l + 1)
                most = sp.value_load(cnt_u[0:1, 0:1], min_val=0, max_val=NT)
                sp.wait_ge(x_hd[l], 16 * l + 1)
                with sp.If(most > P):
                    with sp.Fori(0, tcols(l) // P - 1) as r:
                        with sp.Fori(0, E_N) as e:
                            b = r * E_N + e
                            gu = [a[n][l].rearrange("e (k p) n -> p e k n", p=P) for n in ("w_gate_e", "w_up_e")]
                            dn = a["w_down_e"][l].rearrange("e (k p) n -> p e k n", p=P)
                            sp.wait_ge(x_y[l], 16 * l + 16)
                            sp.wait_ge(v_done[l], b + 1)
                            for i in range(2):
                                sp.dma_start(over_w[i].rearrange("p (k n) -> p k n", k=8),
                                             gu[i][:, bass.ds(e, 1)].rearrange("p e k n -> p (e k) n")
                                             ).then_inc(v_w[l], 16)
                            sp.wait_ge(v_pe[l], b * 4 + 2)
                            sp.dma_start(over_w[0].rearrange("p (k n) -> p k n", k=4),
                                         dn[:, bass.ds(e, 1)].rearrange("p e k n -> p (e k) n")).then_inc(v_wd[l], 16)
            sp.wait_ge(e_c, 2)
            sp.dma_start(out[0, 0:P, :], htok[:, 0, :]).then_inc(e_s, 16)
            sp.wait_ge(e_c, 4)
            sp.dma_start(out[0, P:2 * P, :], htok[:, 1, :]).then_inc(e_s, 16)
            sp.wait_ge(e_s, 32)

        @block.gpsimd
        def _(pool):
            for l in range(DEPTH):
                T = tcols(l)
                nt = T // P

                def trail(q, slot, x, raw):
                    pool.wait_ge(w_h, q + 1)
                    pool.tensor_tensor(w_lo[:, slot], rview(raw, 8)[:, :, x * P:(x + 1) * P],
                                       w_hi[:, slot].bitcast(F32), ALU.subtract).then_inc(w_l, 1)

                q0 = l * HALVES
                for q in range(2 * IN_C + AHEAD):
                    trail(q0 + q, q % WS, q % 2, (MOD_C + q // 2) % RS)
                pool.wait_ge(y_m[l], 4 * streams(l))
                pool.dma_start(rope, a["rope"]).then_inc(r_ld[l], 16)
                pool.dma_start(colmask, a["colmask"]).then_inc(r_ld[l], 16)
                pool.dma_start(wrt, a["w_router"]).then_inc(r_ld[l], 16)
                for h in range(HEADS):
                    if h >= 2:
                        pool.wait_ge(a_mx[l], len(units_of[l]) * (h - 1))
                    else:
                        pool.wait_ge(y_z[l], 2 * streams(l) * BK)
                    pool.dma_start(bias[:, h % 2], a["rpb_win"][l, h]).then_inc(b_ld[l][h % 2], 16)
                m0 = 2 * IN_C
                with pool.Fori(0, 3) as n:
                    for m in range(AHEAD, DK + AHEAD):
                        trail(n * DK + (q0 + m0 + m), m % WS, m % 2, (MOD_C + IN_C + merge_chunk(m)) % RS)
                for m in range(AHEAD, DK):
                    trail(q0 + m0 + 3 * DK + m, m % WS, m % 2, (MOD_C + IN_C + MERGE_C + m // 2) % RS)
                pool.wait_ge(o_d[l], 8 * streams(l))
                pool.memset(zero_ids, 0.0).then_inc(q_z[l], 1)
                pool.wait_ge(q_z[l], l + 1)
                pool.dma_start(slot_tok[l].rearrange("(p x) o -> p (x o)", p=P), zero_ids).then_inc(q_zd[l], 16)
                pool.wait_ge(q_zd[l], 16)
                for j in range(nt):
                    pool.wait_ge(t_ev[l], 2 * (j + 1))
                    pool.dma_start(h_rows[l][j * P:(j + 1) * P, :], htok[:, j, :]).then_inc(t_st[l], 16)
                pool.wait_ge(q_ix[l], l + 1)
                for j in range(nt):
                    for i in range(2):
                        pool.indirect_dma_start(
                            out=slot_tok[l], out_offset=bass.IndirectOffsetOnAxis(ap=didx[:, i, j:j + 1], axis=0),
                            in_=tok_id[:, j:j + 1], in_offset=None).then_inc(q_sc[l], 16)
                pool.wait_ge(q_sc[l], 16 * 2 * nt)
                pool.dma_start(ids_f, slot_tok[l].rearrange("(r s) o -> r (s o)", s=P)).then_inc(q_tb[l], 16)
                pool.wait_ge(q_ti[l], l + 1)
                pool.wait_ge(t_st[l], 16 * nt)

                def gather(i, e, dst, done):
                    pool.indirect_dma_start(
                        out=dst, out_offset=None, in_=h_rows[l][0:tcols(l), :],
                        in_offset=bass.IndirectOffsetOnAxis(ap=e, axis=0)).then_inc(done, 16)

                def store(s, par_):
                    pool.wait_ge(x_ya[l], 16 * l + s + 1)
                    pool.wait_ge(x_yd[l], 16 * l + s + 1)
                    pool.dma_start(y_rows[l][s * P:(s + 1) * P, :], yb[:, par_, :]).then_inc(x_st[l][par_], 16)

                for e in range(2):
                    gather(e, tidx[:, e:e + 1], hg[:, e, :], x_g[l][e])
                for s in range(E_N):
                    if s + 2 < E_N:
                        pool.wait_ge(x_tr[l], 16 * l + s + 1)
                        gather(s, tidx[:, s + 2:s + 3], hg[:, s % 2, :], x_g[l][s % 2])
                    if s >= 1:
                        store(s - 1, (s - 1) % 2)
                store(E_N - 1, 1)
                for i in range(2):
                    pool.wait_ge(x_st[l][i], 16 * E_N // 2)

                def combine(rows):
                    for j in range(nt):
                        for i in range(2):
                            pool.indirect_dma_start(
                                out=(fa if i == 0 else fb)[:, j, :], out_offset=None, in_=y_rows[l][0:rows, :],
                                in_offset=bass.IndirectOffsetOnAxis(ap=didx[:, i, j:j + 1], axis=0)
                            ).then_inc(z_g[l], 16)

                most = pool.value_load(cnt_u[0:1, 0:1], min_val=0, max_val=NT)
                with pool.If(most > P):
                    with pool.Fori(0, (nt - 1) * E_N) as b:
                        pool.wait_ge(v_d[l], b * 6 + 1)
                        pool.tensor_tensor(zero_ids[:, 1:2], zero_ids[:, 0:1], zero_ids[:, 0:1], ALU.add
                                           ).then_inc(v_t[l], 1)
                        gather(0, over_idx[:], hg[:, 0, :], v_g[l])
                        pool.wait_ge(v_d[l], b * 6 + 6)
                        pool.dma_start(y_rows[l][bass.ds(b * P + E_N * P, P), :], yb[:, 0, :]).then_inc(v_s[l], 16)
                        pool.wait_ge(v_t[l], b + 1)
                        pool.wait_ge(v_s[l], b * 16 + 16)
                    combine(E_N * T)
                with pool.Else():
                    combine(E_N * P)

        @block.tensor
        def _(pe):
            mm = nc.tensor.matmul
            tp = nc.tensor.transpose

            def norm_pe(inst, cols):
                for k in range(DK):
                    pe.wait_ge(n_sq, inst * DK + k + 1)
                    mm(bank[7][:, 0:cols], ones, sqb[:, k % 2, 0:cols], start=k == 0, stop=k == DK - 1
                       ).then_inc(n_mm, 1)

            def mm3(dst, stat, mov, start, stop):
                first = mm(dst, stat[0], mov[0], start=start, stop=False)
                mm(dst, stat[1], mov[0], start=False, stop=False)
                return first, mm(dst, stat[0], mov[1], start=False, stop=stop)

            pe.wait_ge(s_ld, 16 * 14)
            for l in range(DEPTH):
                T = tcols(l)
                S = streams(l)
                base = l * LAYER_C
                q0 = l * HALVES

                def w_part(slot, k):
                    return w_hi[:, slot, k, :], w_lo[:, slot, k, :]

                def h_part(k, c0, c1):
                    return h_hi[:, k, c0:c1], h_lo[:, k, c0:c1]

                def mod_columns(g):
                    pe.wait_ge(m_ev[l], 12 * l + g + 1)
                    for c in range(4):
                        last = mm(bank[5 + g % 2][:, 2 * c:2 * c + 2], mrow[:, g % 2, c * P:(c + 1) * P], sel2[:],
                                  start=True, stop=True)
                    last.then_inc(m_co[l], 1)

                def mod(g):
                    if g >= 2:
                        pe.wait_ge(m_tk[l], 12 * l + g - 1)
                    for h in range(2):
                        slot = (2 * g + h) % RS
                        pe.wait_ge(ring_full[slot], full_at(base + 2 * g + h))
                        for k in range(4):
                            last = mm(bank[5 + g % 2][32 * k:32 * k + 32, :], csil[:, 4 * h + k, :],
                                      rview(slot, 4)[:, k, :], start=h == 0, stop=h == 1)
                        last.then_inc(ring_used, 1)
                    if g:
                        mod_columns(g - 1)

                def filters(o):
                    if o:
                        pe.wait_ge(f_d[l], 6 * l + 4)
                    for i in range(2):
                        for j in range(2):
                            last = mm(bank[2 * i + j][:], fhid[0:HY_H, 2, j * P:(j + 1) * P],
                                      w3s[:, (2 * o + i) * BW:(2 * o + i + 1) * BW], start=True, stop=True)
                    last.then_inc(f_p[l], 1)

                def spectra(o):
                    pe.wait_ge(f_d[l], 6 * l + 3 + 2 * o)
                    for j in range(2):
                        mm(bank[7][:], ones, fabs_[:, j, :], start=j == 0, stop=j == 1)
                    for f in range(4):
                        for j in range(2):
                            mm(bank[f][:], dft_f[:, j, f * P:(f + 1) * P], fpm[:, f // 2, j, :],
                               start=j == 0, stop=j == 1)
                    for j in range(2):
                        last = mm(bank[4][0:1, :], nyq[:, j:j + 1], fpm[:, 0, j, :], start=j == 0, stop=j == 1)
                    last.then_inc(f_p[l], 1)

                pe.wait_ge(s_ldl[l], 16 * 6)
                mm(bank[0][0:HY_H, 0:SEQ], fw1, fz, start=True, stop=True).then_inc(f_p[l], 1)
                if l == 0:
                    pe.wait_ge(s_cs, 1)
                mod(0)
                pe.wait_ge(f_a[l], 2 * l + 1)
                mm(bank[1][0:HY_H, 0:SEQ], fw2, fhid[0:HY_H, 1, :], start=True, stop=True).then_inc(f_p[l], 1)
                mod(1)
                pe.wait_ge(f_a[l], 2 * l + 2)
                filters(0)
                mod(2)
                mod(3)
                spectra(0)
                filters(1)
                mod(4)
                mod(5)
                spectra(1)
                for g in range(6, 12):
                    mod(g)
                mod_columns(11)
                norm_pe(2 * l, NT)
                g = 0
                for i in range(12):
                    cols = NT if i >= 10 else T
                    for x in range(2):
                        pe.wait_ge(w_l, q0 + g + 1)
                        if g >= 4:
                            pe.wait_ge(j_d[l] if g - 4 < 16 else j_a[l], g - 3 if g - 4 < 16 else g - 19)
                        for k in range(DK):
                            if g == 0:
                                pe.wait_ge(h_l, 2 * DK * l + k + 1)
                            first, last = mm3(bank[g % 4][:, 0:cols], w_part(g % WS, k), h_part(k, 0, cols),
                                              k == 0, k == DK - 1)
                            if g and k == 0:
                                first.then_inc(w_u, 1)
                        last.then_inc(j_pe[l], 1)
                        g += 1
                for i in range(2):
                    pe.wait_ge(w_l, q0 + 24 + 2 * i + 2)
                    for j in range(4):
                        pe.wait_ge(j_a[l], g - 19)
                        for k in range(DK):
                            w = [v[:, 2 * i:2 * i + 2, k, :] for v in (w_hi, w_lo)]
                            first, last = mm3(bank[g % 4][:, 0:256].rearrange("p (x n) -> p x n", x=2),
                                              h_part(k, j * P, (j + 1) * P), w, k == 0, k == DK - 1)
                            if j + k == 0:
                                first.then_inc(w_u, 2 if i else 1)
                        last.then_inc(j_pe[l], 1)
                        g += 1
                pe.wait_ge(j_pe[l], g)
                pe.nop().then_inc(w_u, 2)
                pe.wait_ge(j_d[l], 16)
                for c in range(BK):
                    mm(bank[4 + c][:, 0:T], poolw[:, c, :], ypool[:, c, 0:T], start=True, stop=True
                       ).then_inc(pw_pe[l], 1)
                pe.wait_ge(j_a[l], 16)
                pe.wait_ge(pw_a[l], 4 * l + BK)
                n = 0
                for o in range(HY_O):
                    for s in range(S):
                        if n:
                            pe.wait_ge(y_zt[l], 2 * n)
                        if o:
                            pe.wait_ge(y_z[l], BK * (n + 1 - S))
                        for j in range(2):
                            for c in range(BK):
                                last = tp(bank[4 + j][:, c * P:(c + 1) * P],
                                          hv[:, c, s * SEQ + j * P:s * SEQ + (j + 1) * P], ident)
                            last.then_inc(y_tp[l], 1)
                        pe.wait_ge(y_zt[l], 2 * n + 2)
                        if n:
                            pe.wait_ge(y_m[l], 2 * n)
                        for f in (0, 2, 1, 3):
                            for j in range(2):
                                last = mm(bank[f][:], dft_f[:, j, f * P:(f + 1) * P], zt[:, j, :],
                                          start=j == 0, stop=j == 1)
                            last.then_inc(y_f[l], 1)
                        pe.wait_ge(y_m[l], 2 * n + 2)
                        for c in range(BK):
                            if n * BK + c >= 2:
                                pe.wait_ge(y_z[l], n * BK + c - 1)
                            for f in range(4):
                                last = mm(bank[6 + c % 2][:, 0:SEQ], hy_y[:, f, c * P:(c + 1) * P], dft_i[:, f, :],
                                          start=f == 0, stop=f == 3)
                            last.then_inc(y_i[l], 1)
                        n += 1
                for i, src in enumerate((qT, kT)):
                    for c in range(BK):
                        u = i * BK + c
                        if u >= 2:
                            pe.wait_ge(r_d[l], 8 * l + u - 1)
                        elif u == 0:
                            pe.wait_ge(y_z[l], 2 * S * BK)
                        mm(bank[6 + u % 2][:, 0:SEQ], perm, src[:, c, 0:SEQ], start=True, stop=True
                           ).then_inc(r_pe[l], 1)
                pe.wait_ge(r_d[l], 8 * l + 8)
                units = units_of[l]
                U = len(units)

                def scores(h):
                    c, p0 = h // 2, (h % 2) * DH
                    rows = slice(p0, p0 + DH)
                    for i, (x, s) in enumerate(units):
                        u = h * U + i
                        if u >= U:
                            pe.wait_ge(a_ex[l], u - U + 1)
                        b = bank[i]
                        if s == 0:
                            mm(b[:, 0:SEQ], qrot[rows, c, x * P:(x + 1) * P], krot[rows, c, :], start=True, stop=True)
                            last = mm(b[:, SEQ:NT], qT[rows, c, x * P:(x + 1) * P], kT[rows, c, SEQ:NT],
                                      start=True, stop=True)
                        else:
                            last = mm(b[:, 0:SEQ], qT[rows, c, SEQ + x * P:SEQ + (x + 1) * P], kT[rows, c, SEQ:NT],
                                      start=True, stop=True)
                        last.then_inc(a_sc[l], 1)

                def transposes(h):
                    if h:
                        pe.wait_ge(a_ev[l], (U // 2 + 1) * h)
                    for i, (x, s) in enumerate(units):
                        pe.wait_ge(a_nm[l], h * U + i + 1)
                        for k in range(4 if s == 0 else 2):
                            b = bank[4 + (k // 2 if s == 0 else 2)]
                            col = (k % 2) * SEQ + x * P
                            last = tp(b[:, col:col + P], prob[:, i, k * P:(k + 1) * P], ident)
                        if x == 1:
                            last.then_inc(a_tr[l], 1)

                def values(h):
                    c, p0 = h // 2, (h % 2) * DH
                    if h:
                        pe.wait_ge(a_o[l], h)
                    pe.wait_ge(a_ev[l], (U // 2 + 1) * (h + 1))
                    o = bank[7][p0:p0 + DH, :]
                    for k in range(4):
                        last = mm(o[:, 0:SEQ], vtok[:, k, h * DH:(h + 1) * DH], pT_s[:, h % 2, k, :],
                                  start=k == 0, stop=k == 3)
                    if S == 2:
                        for k in range(2):
                            last = mm(o[:, SEQ:NT], vtok[:, 2 + k, h * DH:(h + 1) * DH], pT_s[:, h % 2, 4 + k, :],
                                      start=k == 0, stop=k == 1)
                    last.then_inc(a_pv[l], 1)

                scores(0)
                for h in range(HEADS):
                    if h + 1 < HEADS:
                        scores(h + 1)
                    transposes(h)
                    values(h)
                pe.wait_ge(a_o[l], HEADS)
                with pe.Fori(0, 3) as n:
                    for m in range(DK):
                        h, r = divmod(m, 4)
                        b_at = base + MOD_C + IN_C + 3 * h + 1
                        bslot = b_at % RS
                        pe.wait_ge(w_l, n * DK + (q0 + 2 * IN_C + m + 1))
                        pe.wait_ge(g_d[l], n * DK + (m + 1))
                        for k in range(DK):
                            first, last = mm3(bank[m % 2][:, 0:T], w_part(m % WS, k), h_part(k, 0, T),
                                              k == 0, k == DK - 1)
                            if k == 0 and r == 0 and m:
                                first.then_inc(ring_used, 1)
                        last.then_inc(g_pe[l], 1)
                        if r == 0:
                            pe.wait_ge(ring_full[bslot], n * (16 * 6 // RS) + full_at(b_at))
                        for k in range(BK):
                            last = mm(bank[2 + m % 2][:, 0:T], rview(bslot, 4)[:, k, r * P:(r + 1) * P],
                                      ys[:, bass.ds(n, 1), k, 0:T], start=k == 0, stop=k == BK - 1)
                            if k == 0:
                                last.then_inc(w_u, 1)
                        last.then_inc(g_pe[l], 1)
                    pe.wait_ge(g_pe[l], n * (2 * DK) + (2 * DK))
                    pe.nop().then_inc(ring_used, 1)
                for m in range(DK):
                    pe.wait_ge(w_l, q0 + 2 * IN_C + 3 * DK + m + 1)
                    if m >= 2:
                        pe.wait_ge(o_d[l], S * (m - 1))
                    for k in range(DK):
                        if m == 0:
                            pe.wait_ge(h_l, 2 * DK * l + DK + k + 1)
                        first, last = mm3(bank[m % 2][:, 0:T], w_part(m % WS, k), h_part(k, 0, T),
                                          k == 0, k == DK - 1)
                        if k == 0 and m:
                            first.then_inc(w_u, 1)
                    last.then_inc(o_pe[l], 1)
                pe.wait_ge(o_pe[l], DK)
                pe.nop().then_inc(w_u, 1)
                norm_pe(2 * l + 1, T)
                pe.wait_ge(n_h, (2 * l + 2) * DK)
                nt = T // P
                for j in range(nt):
                    for k in range(DK):
                        last = mm(bank[6][:, j * E_N:(j + 1) * E_N], hT[:, k, j * P:(j + 1) * P], wrt[:, k, :],
                                  start=k == 0, stop=k == DK - 1)
                last.then_inc(q_lg[l], 1)
                for j in range(nt):
                    if j >= 2:
                        pe.wait_ge(t_ev[l], 2 * (j - 1))
                    for i in range(2):
                        for k in range(4):
                            last = tp(bank[2 * (j % 2) + i][:, k * P:(k + 1) * P],
                                      hT[:, 4 * i + k, j * P:(j + 1) * P], ident)
                        last.then_inc(t_pe[l], 1)
                pe.wait_ge(q_m[l], l + 1)
                msk = rt[:, 0, :].rearrange("p (j e) -> p j e", e=E_N)
                for j in range(nt):
                    for i in range(j + 1):
                        mm(bank[7][:, j * E_N:(j + 1) * E_N], tri if i == j else ones, msk[:, i, :],
                           start=i == 0, stop=i == j)
                for i in range(nt):
                    last = mm(bank[7][:, 64:64 + E_N], ones, msk[:, i, :], start=i == 0, stop=i == nt - 1)
                last.then_inc(q_rk[l], 1)
                pe.wait_ge(q_tb[l], 16)
                tp(bank[6][:, 64:128], ids_f, ident[0:64, 0:64]).then_inc(q_tt[l], 1)
                xb = base + PRE_C
                pe.wait_ge(t_ev[l], 2 * nt)

                def rows_t(par_, e, owed):
                    for i in range(2):
                        for k in range(4):
                            last = tp(bank[i][:, k * P:(k + 1) * P], hg[:, par_, (4 * i + k) * P:(4 * i + k + 1) * P],
                                      ident)
                            if owed and i + k == 0:
                                last.then_inc(ring_used, 1)
                    last.then_inc(x_tr[l], 1)

                def gate_up(par_, s, idx, slots):
                    pe.wait_ge(x_ha[l], 16 * l + s + 1)
                    pe.wait_ge(x_hd[l], 16 * l + s + 1)
                    for w in range(2):
                        for h in range(2):
                            c = 2 * w + h
                            pe.wait_ge(ring_full[slots[c] % RS], idx[c])
                            for k in range(4):
                                last = mm(bank[2 + w][:], heT[:, par_, 4 * h + k, :], rview(slots[c] % RS, 4)[:, k, :],
                                          start=h + k == 0, stop=h == 1 and k == 3)
                            last.then_inc(ring_used if c < 3 else x_gu[l], 1)

                def hidden_t(par_, s, owed):
                    pe.wait_ge(x_hid[l], 16 * l + s + 1)
                    for k in range(FK):
                        last = tp(bank[4][:, k * P:(k + 1) * P], hid[:, par_, k * P:(k + 1) * P], ident)
                        if owed and k == 0:
                            last.then_inc(ring_used, 1)
                    last.then_inc(x_ht[l], 1)

                def down(par_, s, idx, slots, owed):
                    pe.wait_ge(x_hte[l], 16 * l + s + 1)
                    for h in range(2):
                        pe.wait_ge(ring_full[slots[h] % RS], idx[h])
                        for k in range(2):
                            for x in range(2):
                                last = mm(bank[5 + x][:], hidT[:, par_, 2 * h + k, :],
                                          rview(slots[h] % RS, 2)[:, k, x * 512:(x + 1) * 512],
                                          start=h + k == 0, stop=h + k == 2)
                                if owed and h + k + x == 0:
                                    last.then_inc(ring_used, 1)
                        last.then_inc(x_y[l] if h else ring_used, 1)

                def fulls(off):
                    return [full_at(xb + off + i) for i in range(6)]

                for e in range(2):
                    pe.wait_ge(x_g[l][e], 16)
                    if e:
                        pe.wait_ge(x_ha[l], 16 * l + 1)
                        pe.wait_ge(x_hd[l], 16 * l + 1)
                    rows_t(e, e, e == 1)
                    if e == 0:
                        gate_up(0, 0, fulls(0)[0:4], (0, 1, 2, 3))
                        pe.wait_ge(x_gu[l], 16 * l + 1)

                def step(par_, s, i, off, more):
                    f = [i * (16 * 12 // RS) + v for v in fulls(off)]
                    hidden_t(1 - par_, s - 1, False)
                    gate_up(par_, s, f[0:4], (4, 5, 0, 1))
                    down(1 - par_, s - 1, f[4:6], (2, 3), True)
                    if more:
                        pe.wait_ge(x_g[l][1 - par_], 16 * ((s + 1) // 2 + 1) if isinstance(s, int) else
                                   (i * 16 + 32))
                        pe.wait_ge(x_ha[l], 16 * l + s + 1)
                        pe.wait_ge(x_hd[l], 16 * l + s + 1)
                        rows_t(1 - par_, s + 1, True)

                with pe.Fori(0, 7) as i:
                    step(1, 2 * i + 1, i, 4, True)
                    step(0, 2 * i + 2, i, 10, True)
                step(1, 15, 7, 4, False)
                hidden_t(1, 15, True)
                pe.wait_ge(x_ya[l], 16 * l + 15)
                pe.wait_ge(x_yd[l], 16 * l + 15)
                down(1, 15, [full_at(xb + 94), full_at(xb + 95)], (4, 5), False)
                pe.wait_ge(x_y[l], 16 * l + 16)
                pe.nop().then_inc(ring_used, 1)
                pe.wait_ge(q_ix[l], l + 1)
                most = pe.value_load(cnt_u[0:1, 0:1], min_val=0, max_val=NT)
                with pe.If(most > P):
                    pe.nop().then_inc(v_done[l], 1)
                    with pe.Fori(0, (nt - 1) * E_N) as b:
                        pe.wait_ge(v_g[l], b * 16 + 16)
                        for i in range(2):
                            for k in range(4):
                                last = tp(bank[i][:, k * P:(k + 1) * P], hg[:, 0, (4 * i + k) * P:(4 * i + k + 1) * P],
                                          ident)
                        last.then_inc(v_pe[l], 1)
                        pe.wait_ge(v_d[l], b * 6 + 2)
                        pe.wait_ge(v_w[l], b * 32 + 32)
                        for i in range(2):
                            for k in range(DK):
                                last = mm(bank[2 + i][:], heT[:, 0, k, :], over_w[i][:, k * FF:(k + 1) * FF],
                                          start=k == 0, stop=k == DK - 1)
                        last.then_inc(v_pe[l], 1)
                        pe.wait_ge(v_d[l], b * 6 + 4)
                        for k in range(FK):
                            last = tp(bank[4][:, k * P:(k + 1) * P], hid[:, 0, k * P:(k + 1) * P], ident)
                        last.then_inc(v_pe[l], 1)
                        pe.wait_ge(v_d[l], b * 6 + 5)
                        pe.wait_ge(v_wd[l], b * 16 + 16)
                        for i in range(2):
                            for k in range(FK):
                                last = mm(bank[5 + i][:], hidT[:, 0, k, :],
                                          over_w[0][:, k * D + i * 512:k * D + (i + 1) * 512],
                                          start=k == 0, stop=k == FK - 1)
                        last.then_inc(v_pe[l], 1)
                        pe.wait_ge(v_pe[l], b * 4 + 4)
                        pe.nop().then_inc(v_done[l], 1)
                with pe.Else():
                    pe.nop()
                pe.wait_ge(z_f[l], nt)
                pe.wait_ge(x_ya[l], 16 * l + E_N)
                pe.wait_ge(x_yd[l], 16 * l + E_N)
                for k in range(DK):
                    for j in range(nt):
                        last = tp(bank[k][:, j * P:(j + 1) * P], fa[:, j, k * P:(k + 1) * P], ident)
                    last.then_inc(z_t[l], 1)
                pe.wait_ge(z_x[l], 16)
            norm_pe(4, SEQ)
            pe.wait_ge(n_h, 5 * DK)
            for j in range(2):
                for i in range(2):
                    for k in range(4):
                        last = tp(bank[2 * j + i][:, k * P:(k + 1) * P], hT[:, 4 * i + k, j * P:(j + 1) * P], ident)
                    last.then_inc(e_t, 1)

        @block.scalar
        def _(act):
            A = nc.scalar.activation

            def norm_act(inst, cols, nstream):
                if inst:
                    l = (inst - 1) // 2
                    act.wait_ge(o_d[l] if inst % 2 else z_x[l], 8 * nstream if inst % 2 else 16)
                for k in range(DK):
                    if k >= 2:
                        act.wait_ge(n_mm, inst * DK + k - 1)
                    A(sqb[:, k % 2, 0:cols], xT[:, k, 0:cols], ACT.Square).then_inc(n_sq, 1)
                act.wait_ge(n_a, inst + 1)
                A(nrm[:, 1, 0:cols], nrm[:, 0, 0:cols], ACT.Sqrt).then_inc(n_s, 1)
                for k in range(DK):
                    act.wait_ge(n_x, inst * DK + k + 1)
                    if inst == 4:
                        A(hT[:, k, 0:cols], hT[:, k, 0:cols], ACT.Identity, scale=fin_g[:, k:k + 1]).then_inc(n_h, 1)
                        continue
                    w = inst % 2
                    for s in range(nstream):
                        v = hT[:, k, s * SEQ:(s + 1) * SEQ]
                        last = A(v, v, ACT.Identity, scale=gs[:, w, k, s:s + 1],
                                 bias=mods[:, 3 * w * DK + k, s:s + 1])
                    last.then_inc(n_h, 1)
                    if w == 0:
                        act.wait_ge(n_h, inst * DK + k + 1)
                        A(h_hi[:, k, :], hT[:, k, :], ACT.Copy).then_inc(h_h, 1)

            act.wait_ge(s_ld, 16 * 14)
            A(cc[:, 1, :], cc[:, 0, :], ACT.Exp, scale=-1.0).then_inc(s_ce, 1)
            for l in range(DEPTH):
                T = tcols(l)
                S = streams(l)
                base = l * LAYER_C
                pc = par[l]
                def mod_rows(g):
                    act.wait_ge(ring_used, l * DIRECT_C + 2 * g + 2)
                    if g >= 2:
                        act.wait_ge(m_co[l], 12 * l + g - 1)
                    A(mrow[:, g % 2, :], bank[5 + g % 2][:, :], ACT.Copy).then_inc(m_ev[l], 1)

                q0 = l * HALVES

                def lead(q, slot, x, raw, full):
                    act.wait_ge(ring_full[raw], full)
                    if not isinstance(q, int) or q >= WS:
                        act.wait_ge(w_u, q - (WS - 1))
                    A(w_hi[:, slot], rview(raw, 8)[:, :, x * P:(x + 1) * P], ACT.Copy).then_inc(w_h, 1)

                def lead_in(q):
                    at = base + MOD_C + q // 2
                    lead(q0 + q, q % WS, q % 2, at % RS, full_at(at))

                for i in range(2):
                    act.wait_ge(f_d[l], 6 * l + 1 + i)
                    A(fhid[0:HY_H, 1 + i, :], fhid[0:HY_H, 0, :], ACT.Sin).then_inc(f_a[l], 1)
                    mod_rows(i)
                for g in range(2, 12):
                    mod_rows(g)
                for q in range(AHEAD):
                    lead_in(q)
                act.wait_ge(m_d[l], l + 1)
                norm_act(2 * l, NT, 2)
                for g in range(12):
                    lead_in(g + AHEAD)
                    act.wait_ge(j_pe[l], g + 1)
                    dst = hv[:, g, 0:T] if g < 4 else hx[:, (g - 4) // 4, g % 4, 0:T]
                    A(dst, bank[g % 4][:, 0:T], ACT.Identity, scale=pc[:, C_TAP + 12 + g:C_TAP + 13 + g],
                      bias=pc[:, C_SB + g:C_SB + g + 1]).then_inc(j_c[l], 1)
                for g in range(12, 16):
                    lead_in(g + AHEAD)
                for g in range(16, 32):
                    if g < 24:
                        lead_in(g + AHEAD)
                    elif g % 4 == 0:
                        for x in range(2):
                            lead_in(26 + (g - 24) // 2 + x)
                    act.wait_ge(j_pe[l], g + 1)
                    b = bank[g % 4]
                    if g < 20:
                        A(qT[:, g - 16, 0:T], b[:, 0:T], ACT.Copy, scale=DH ** -0.5).then_inc(j_a[l], 1)
                    elif g < 24:
                        A(kT[:, g - 20, :], b[:, :], ACT.Copy).then_inc(j_a[l], 1)
                    else:
                        h, j = divmod(g - 24, 4)
                        A(vtok[:, j, h * 256:(h + 1) * 256], b[:, 0:256], ACT.Copy).then_inc(j_a[l], 1)
                for c in range(BK):
                    act.wait_ge(pw_pe[l], 4 * l + c + 1)
                    A(ys_pool[:, c, 0:T], bank[4 + c][:, 0:T], ACT.Copy, scale=pc[:, C_PS + c:C_PS + c + 1]
                      ).then_inc(pw_a[l], 1)
                for n in range(2 * S):
                    if n:
                        act.wait_ge(y_f[l], 4 * n)
                    for j in range(2):
                        act.wait_ge(y_tp[l], 2 * n + j + 1)
                        A(zt[:, j, :], bank[4 + j][:, :], ACT.Copy).then_inc(y_zt[l], 1)
                units = units_of[l]
                U = len(units)

                def exps(h):
                    for i, (x, s) in enumerate(units):
                        act.wait_ge(a_mx[l], h * U + i + 1)
                        if h:
                            act.wait_ge(a_tr[l], (U // 2) * (h - 1) + s + 1)
                        w = NT if s == 0 else SEQ
                        A(prob[:, i, 0:w], bank[i][:, 0:w], ACT.Exp, bias=pstat[:, i, 0:1],
                          accum_out=pstat[:, i, 1:2]).then_inc(a_ex[l], 1)

                def evac(h):
                    act.wait_ge(a_tr[l], (U // 2) * h + 1)
                    if h >= 2:
                        act.wait_ge(a_pv[l], h - 1)
                    A(pT_s[:, h % 2, 0:2, :], bank[4][:, :].rearrange("p (k t) -> p k t", k=2), ACT.Copy
                      ).then_inc(a_ev[l], 1)
                    A(pT_s[:, h % 2, 2:4, :], bank[5][:, :].rearrange("p (k t) -> p k t", k=2), ACT.Copy
                      ).then_inc(a_ev[l], 1)
                    if S == 2:
                        act.wait_ge(a_tr[l], 2 * h + 2)
                        A(pT_s[:, h % 2, 4:6, :], bank[6][:, :].rearrange("p (k t) -> p k t", k=2), ACT.Copy
                          ).then_inc(a_ev[l], 1)
                    act.wait_ge(a_pv[l], h + 1)
                    c, p0 = h // 2, (h % 2) * DH
                    A(qT[p0:p0 + DH, c, 0:T], bank[7][p0:p0 + DH, 0:T], ACT.Copy).then_inc(a_o[l], 1)

                act.wait_ge(y_z[l], 2 * S * BK)
                exps(0)
                for h in range(HEADS):
                    evac(h)
                    if h + 1 < HEADS:
                        exps(h + 1)
                act.wait_ge(a_tr[l], HEADS * (U // 2))
                at0 = base + MOD_C + IN_C
                with act.Fori(0, 3) as n:
                    for m in range(DK):
                        q = m + AHEAD
                        at = at0 + merge_chunk(q)
                        lead(n * DK + (q0 + 2 * IN_C + q), q % WS, q % 2, at % RS, n * (16 * 6 // RS) + full_at(at))
                        act.wait_ge(g_pe[l], n * (2 * DK) + (2 * m + 1))
                        act.wait_ge(g_d[l], n * DK + (m + 1))
                        A(gate_t[:, m % 2, 0:T], bank[m % 2][:, 0:T], ACT.Tanh, scale=0.5).then_inc(g_t[l], 1)
                act.wait_ge(g_pe[l], 3 * 2 * DK - 1)
                for k in range(DK):
                    act.wait_ge(g_d[l], 2 + 2 * DK + k + 1)
                    A(h_hi[:, k, 0:T], merged[:, k, 0:T], ACT.Copy).then_inc(h_h, 1)
                for m in range(AHEAD, DK):
                    at = base + PRE_C - OUT_C + m // 2
                    lead(q0 + 2 * IN_C + 3 * DK + m, m % WS, m % 2, at % RS, full_at(at))
                norm_act(2 * l + 1, T, S)
                nt = T // P
                act.wait_ge(q_lg[l], l + 1)
                A(rt[:, 1, 0:nt * E_N], bank[6][:, 0:nt * E_N], ACT.Exp, scale=-1.0).then_inc(q_ex[l], 1)
                for j in range(nt):
                    for i in range(2):
                        act.wait_ge(t_pe[l], 2 * j + i + 1)
                        A(htok[:, j, i * 512:(i + 1) * 512], bank[2 * (j % 2) + i][:, :], ACT.Copy
                          ).then_inc(t_ev[l], 1)

                def rows_in(par_, e):
                    act.wait_ge(x_tr[l], 16 * l + e + 1)
                    A(heT[:, par_, 0:4, :], bank[0][:, :].rearrange("p (k t) -> p k t", k=4), ACT.Copy
                      ).then_inc(x_ha[l], 1)

                def tanh(par_, s):
                    act.wait_ge(x_gu[l], 16 * l + s + 1)
                    A(thb[:, par_, :], bank[2][:, :], ACT.Tanh, scale=0.5).then_inc(x_th[l], 1)

                def hid_in(par_, s):
                    act.wait_ge(x_ht[l], 16 * l + s + 1)
                    A(hidT[:, par_, :, :], bank[4][:, :].rearrange("p (k t) -> p k t", k=4), ACT.Copy
                      ).then_inc(x_hte[l], 1)

                def y_out(par_, s, free):
                    act.wait_ge(x_y[l], 16 * l + s + 1)
                    if free is not None:
                        act.wait_ge(x_st[l][par_], free)
                    A(yb[:, par_, 0:512], bank[5][:, :], ACT.Copy).then_inc(x_ya[l], 1)

                rows_in(0, 0)
                tanh(0, 0)
                rows_in(1, 1)
                for s in (1, 2):
                    hid_in((s - 1) % 2, s - 1)
                    tanh(s % 2, s)
                    y_out((s - 1) % 2, s - 1, None)
                    rows_in((s + 1) % 2, s + 1)
                with act.Fori(1, 7) as i:
                    hid_in(0, 2 * i)
                    tanh(1, 2 * i + 1)
                    y_out(0, 2 * i, i * 16)
                    rows_in(0, 2 * i + 2)
                    hid_in(1, 2 * i + 1)
                    tanh(0, 2 * i + 2)
                    y_out(1, 2 * i + 1, i * 16)
                    rows_in(1, 2 * i + 3)
                hid_in(0, 14)
                tanh(1, 15)
                y_out(0, 14, 16 * 7)
                hid_in(1, 15)
                y_out(1, 15, 16 * 7)
                act.wait_ge(q_ix[l], l + 1)
                most = act.value_load(cnt_u[0:1, 0:1], min_val=0, max_val=NT)
                with act.If(most > P):
                    with act.Fori(0, (nt - 1) * E_N) as b:
                        act.wait_ge(v_pe[l], b * 4 + 2)
                        A(thb[:, 0, :], bank[2][:, :], ACT.Tanh, scale=0.5).then_inc(v_a[l], 1)
                with act.Else():
                    act.nop()
            norm_act(4, SEQ, 1)
            for j in range(2):
                for i in range(2):
                    act.wait_ge(e_t, 2 * j + i + 1)
                    A(htok[:, j, i * 512:(i + 1) * 512], bank[2 * j + i][:, :], ACT.Copy).then_inc(e_c, 1)

        @block.vector
        def _(dve):
            V = nc.vector
            chain = [0]

            def link(ins):
                chain[0] += 1
                ins.then_inc(dve_c, 1)
                dve.wait_ge(dve_c, chain[0])

            def norm_dve(inst, cols):
                dve.wait_ge(n_mm, (inst + 1) * DK)
                V.tensor_scalar(nrm[:, 0, 0:cols], bank[7][:, 0:cols], 1.0 / D, EPS, ALU.mult, ALU.add).then_inc(n_a, 1)
                dve.wait_ge(n_s, inst + 1)
                link(V.reciprocal(nrm[:, 2, 0:cols], nrm[:, 1, 0:cols]))
                link(V.tensor_tensor(nrm[:, 3, 0:cols], nrm[:, 2, 0:cols], nrm[:, 2, 0:cols], ALU.mult))
                link(V.scalar_tensor_tensor(nrm[:, 3, 0:cols], nrm[:, 0, 0:cols], -0.5, nrm[:, 3, 0:cols],
                                            ALU.mult, ALU.mult))
                link(V.scalar_tensor_tensor(nrm[:, 1, 0:cols], nrm[:, 3, 0:cols], 1.5, nrm[:, 2, 0:cols],
                                            ALU.add, ALU.mult))
                lag = 2 if inst in (0, 2) else 0
                for k in range(DK + lag):
                    if k < DK:
                        V.tensor_tensor(hT[:, k, 0:cols], xT[:, k, 0:cols], nrm[:, 1, 0:cols], ALU.mult
                                        ).then_inc(n_x, 1)
                    if lag and k >= lag:
                        trail_h(k - lag, 8 * inst, hT, cols)

            def trail_h(k, before, src, cols):
                dve.wait_ge(h_h, before + k + 1)
                V.tensor_tensor(h_lo[:, k, 0:cols], src[:, k, 0:cols], h_hi[:, k, 0:cols].bitcast(F32), ALU.subtract
                                ).then_inc(h_l, 1)

            dve.wait_ge(s_ce, 1)
            link(V.tensor_scalar(cc[:, 2, :], cc[:, 1, :], 1.0, None, ALU.add))
            link(V.reciprocal(cc[:, 1, :], cc[:, 2, :]))
            link(V.memset(csil[:], 0.0))
            V.tensor_tensor(csil[:, :, 0:2], cc[:, 0, :].rearrange("p (k s) -> p k s", s=2),
                            cc[:, 1, :].rearrange("p (k s) -> p k s", s=2), ALU.mult).then_inc(s_cs, 1)
            for l in range(DEPTH):
                T = tcols(l)
                S = streams(l)
                pc = par[l]
                fc = [pc[0:HY_H, C_FILT + i:C_FILT + i + 1] for i in range(3)]

                def angle(i):
                    dve.wait_ge(f_p[l], 6 * l + i + 1)
                    x0, x1 = fhid[0:HY_H, 0, :], nrm[0:HY_H, 0, 0:SEQ]
                    if i:
                        dve.wait_ge(f_a[l], 2 * l + 1)
                    link(V.tensor_scalar(x1, bank[i][0:HY_H, 0:SEQ], fc[2 * i], fc[1], ALU.add, ALU.mult))
                    x2 = nrm[0:HY_H, 1, 0:SEQ]
                    link(V.tensor_scalar(x2, x1, 1.0 / TWO_PI, 12582912.0, ALU.mult, ALU.add))
                    link(V.tensor_scalar(x2, x2, -12582912.0, None, ALU.add))
                    link(V.scalar_tensor_tensor(x1, x2, -6.28125, x1, ALU.mult, ALU.add))
                    link(V.scalar_tensor_tensor(x1, x2, -0.0019350051879882812, x1, ALU.mult, ALU.add))
                    link(V.scalar_tensor_tensor(x1, x2, -3.0199157663445e-07, x1, ALU.mult, ALU.add))
                    V.tensor_scalar(x0, x1, 3.1415925, -3.1415925, ALU.min, ALU.max).then_inc(f_d[l], 1)

                def taps(o):
                    dve.wait_ge(f_p[l], 6 * l + 3 + 2 * o)
                    for i in range(2):
                        for j in range(2):
                            V.tensor_tensor(fraw[:, i, j, :], bank[2 * i + j][:, :], decay[:, j, :], ALU.mult
                                            ).then_inc(dve_c, 1)
                    chain[0] += 4
                    dve.wait_ge(dve_c, chain[0])
                    link(V.memset(fraw[0:1, 1, 0, :], 0.0))
                    V.tensor_tensor(fpm[:, 0], fraw[:, 0], fraw[:, 1], ALU.add)
                    link(V.tensor_tensor(fpm[:, 1], fraw[:, 0], fraw[:, 1], ALU.subtract))
                    link(V.scalar_tensor_tensor(fraw[:, 0], fraw[:, 0], -1.0, fraw[:, 0], ALU.mult, ALU.max))
                    link(V.scalar_tensor_tensor(fraw[:, 1], fraw[:, 1], -1.0, fraw[:, 1], ALU.mult, ALU.max))
                    V.tensor_tensor(fabs_, fraw[:, 0], fraw[:, 1], ALU.add).then_inc(f_d[l], 1)

                def normed(o):
                    dve.wait_ge(f_p[l], 6 * l + 4 + 2 * o)
                    link(V.reciprocal(fnorm, bank[7][:, :]))
                    for f in range(3):
                        V.tensor_tensor(spec[:, o, f, :], bank[f][:, :], fnorm, ALU.mult)
                    link(V.tensor_tensor(spec[:, o, 3, :], bank[3][:, :], fnorm, ALU.mult))
                    V.tensor_tensor(spec[0:1, o, 2, :], bank[4][0:1, :], fnorm[0:1, :], ALU.mult).then_inc(f_d[l], 1)

                def mod_take(g):
                    dve.wait_ge(m_co[l], 12 * l + g + 1)
                    V.tensor_tensor(mods[:, 4 * g:4 * g + 4, :],
                                    bank[5 + g % 2][:, 0:8].rearrange("p (m s) -> p m s", s=2),
                                    pc[:, C_BMOD + 4 * g:C_BMOD + 4 * g + 4].unsqueeze(2).to_broadcast([P, 4, 2]),
                                    ALU.add).then_inc(m_tk[l], 1)

                angle(0)
                angle(1)
                mod_take(0)
                taps(0)
                mod_take(1)
                mod_take(2)
                normed(0)
                taps(1)
                mod_take(3)
                mod_take(4)
                normed(1)
                for g in range(5, 12):
                    mod_take(g)
                dve.wait_ge(m_tk[l], 12 * l + 12)
                for w in range(2):
                    for s in range(2):
                        link(V.scalar_tensor_tensor(gs[:, w, :, s], mods[:, (3 * w + 1) * DK:(3 * w + 2) * DK, s], 1.0,
                                                    pc[:, C_G1 + 8 * w:C_G1 + 8 * w + 8], ALU.add, ALU.mult))
                V.tensor_scalar(half_gate[:], mods[:, 2 * DK:3 * DK, :], 0.5, None, ALU.mult).then_inc(m_d[l], 1)
                dve.wait_ge(m_d[l], l + 1)
                norm_dve(2 * l, NT)
                for g in range(12):
                    dve.wait_ge(j_c[l], g + 1)
                    dst = hv[:, g, 0:T] if g < 4 else hx[:, (g - 4) // 4, g % 4, 0:T]
                    dst = dst.rearrange("p (s t) -> p s t", t=SEQ)
                    src = bank[g % 4][:, 0:T].rearrange("p (s t) -> p s t", t=SEQ)
                    link(V.scalar_tensor_tensor(dst[:, :, 1:SEQ], src[:, :, 0:SEQ - 1], pc[:, C_TAP + g:C_TAP + g + 1],
                                                dst[:, :, 1:SEQ], ALU.mult, ALU.add))
                    V.scalar_tensor_tensor(dst[:, :, 0:SEQ - 1], src[:, :, 1:SEQ],
                                           pc[:, C_TAP + 24 + g:C_TAP + 25 + g], dst[:, :, 0:SEQ - 1],
                                           ALU.mult, ALU.add).then_inc(j_d[l], 1)
                link(V.memset(up[:, :, 0:POOL_PAD], 0.0))
                link(V.memset(up[:, :, POOL_PAD + SEQ:POOL_L], 0.0))
                for c in range(BK):
                    dve.wait_ge(j_pe[l], 12 + c + 1)
                    link(V.tensor_copy(up[:, 0:S, POOL_PAD:POOL_PAD + SEQ],
                                       bank[(12 + c) % 4][:, 0:T].rearrange("p (s t) -> p s t", t=SEQ)))
                    lo, hi = 1, POOL_L
                    link(V.tensor_tensor(ps_a[:, 0:S, lo:hi], up[:, 0:S, lo - 1:hi - 1], up[:, 0:S, lo:hi], ALU.add))
                    src, dst = ps_a, ps_b
                    for i in range(c):
                        h = 1 << i
                        lo, hi = lo + h, hi - h
                        link(V.tensor_tensor(dst[:, 0:S, lo:hi], src[:, 0:S, lo - h:hi - h], src[:, 0:S, lo + h:hi + h],
                                             ALU.add))
                        src, dst = dst, src
                    for s in range(S):
                        for x, t in ((0, 0), (8, SEQ - 8)):
                            v = src[:, s, POOL_PAD + t:POOL_PAD + t + 8]
                            link(V.tensor_tensor(v, v, edge[:, c, x:x + 8], ALU.mult))
                    V.scalar_tensor_tensor(ypool[:, c, 0:T].rearrange("p (s t) -> p s t", t=SEQ),
                                           src[:, 0:S, POOL_PAD:POOL_PAD + SEQ], 1.0 / (2 << c),
                                           up[:, 0:S, POOL_PAD:POOL_PAD + SEQ], ALU.mult, ALU.subtract
                                           ).then_inc(j_d[l], 1)
                    dve.wait_ge(j_d[l], 12 + c + 1)
                dve.wait_ge(pw_a[l], 4 * l + BK)
                n = 0
                for o in range(HY_O):
                    for s in range(S):
                        if n:
                            dve.wait_ge(y_i[l], BK * n)
                        for h in range(2):
                            zr, zi = bank[h], bank[2 + h]
                            hr, hi = spec[:, o, h, :], spec[:, o, 2 + h, :]
                            dve.wait_ge(y_f[l], 4 * n + 2 * h + 2)
                            link(V.tensor_tensor(hy_t[:, 0, :], zr[:, :], hr, ALU.mult))
                            link(V.tensor_tensor(hy_t[:, 1, :], zi[:, :], hi, ALU.mult))
                            link(V.tensor_tensor(hy_y[:, h, :], hy_t[:, 0, :], hy_t[:, 1, :], ALU.subtract))
                            link(V.tensor_tensor(hy_t[:, 0, :], zr[:, :], hi, ALU.mult))
                            link(V.tensor_tensor(hy_t[:, 1, :], zi[:, :], hr, ALU.mult))
                            last = V.tensor_tensor(hy_y[:, 2 + h, :], hy_t[:, 0, :], hy_t[:, 1, :], ALU.add)
                            if h == 0:
                                link(last)
                                link(V.tensor_tensor(hy_y[0:1, 0, :], zr[0:1, :], hr[0:1, :], ALU.mult))
                                last = V.tensor_tensor(hy_y[0:1, 2, :], zi[0:1, :], hi[0:1, :], ALU.mult)
                            last.then_inc(y_m[l], 1)
                            dve.wait_ge(y_m[l], 2 * n + h + 1)
                        for c in range(BK):
                            dve.wait_ge(y_i[l], BK * n + c + 1)
                            z = hv[:, c, s * SEQ:(s + 1) * SEQ]
                            sk = C_SKIP + o * BK + c
                            link(V.scalar_tensor_tensor(hy_t[:, 0, 0:SEQ], z, pc[:, sk:sk + 1],
                                                        bank[6 + c % 2][:, 0:SEQ], ALU.mult, ALU.add))
                            V.tensor_tensor(z, hy_t[:, 0, 0:SEQ], hx[:, o, c, s * SEQ:(s + 1) * SEQ], ALU.mult
                                            ).then_inc(y_z[l], 1)
                            dve.wait_ge(y_z[l], BK * n + c + 1)
                        n += 1
                dve.wait_ge(r_ld[l], 48 * (l + 1))
                for i, (src, dst) in enumerate(((qT, qrot), (kT, krot))):
                    for c in range(BK):
                        u = i * BK + c
                        dve.wait_ge(r_pe[l], 8 * l + u + 1)
                        link(V.tensor_tensor(rtmp[:, 0, :], bank[6 + u % 2][:, 0:SEQ], rope[:, 1, :], ALU.mult))
                        link(V.tensor_tensor(rtmp[:, 1, :], src[:, c, 0:SEQ], rope[:, 0, :], ALU.mult))
                        V.tensor_tensor(dst[:, c, :], rtmp[:, 0, :], rtmp[:, 1, :], ALU.add).then_inc(r_d[l], 1)
                        dve.wait_ge(r_d[l], 8 * l + u + 1)
                units = units_of[l]
                U = len(units)

                def maxes(h):
                    dve.wait_ge(b_ld[l][h % 2], 16 * (h // 2 + 1))
                    v = bias[:, h % 2]
                    V.tensor_tensor(v, v, colmask.unsqueeze(1).to_broadcast([P, 6, GRID]), ALU.add
                                    ).then_inc(b_fix[l], 1)
                    dve.wait_ge(b_fix[l], h + 1)
                    for i, (x, s) in enumerate(units):
                        dve.wait_ge(a_sc[l], h * U + i + 1)
                        b = bank[i]
                        w = NT if s == 0 else SEQ
                        if s == 0:
                            k0 = 2 - 2 * x
                            link(V.tensor_tensor(b[:, 0:SEQ].rearrange("p (s j) -> p s j", s=4),
                                                 b[:, 0:SEQ].rearrange("p (s j) -> p s j", s=4),
                                                 v[:, k0:k0 + 4, :], ALU.add))
                        if h:
                            dve.wait_ge(a_nm[l], (h - 1) * U + i + 1)
                        V.tensor_reduce(pstat[:, i, 0:1], b[:, 0:w], AX.X, ALU.max, negate=True).then_inc(a_mx[l], 1)

                def probs(h):
                    for i, (x, s) in enumerate(units):
                        dve.wait_ge(a_ex[l], h * U + i + 1)
                        w = NT if s == 0 else SEQ
                        link(V.reciprocal(pstat[:, i, 2:3], pstat[:, i, 1:2]))
                        V.tensor_scalar(prob[:, i, 0:w], prob[:, i, 0:w], pstat[:, i, 2:3], None, ALU.mult
                                        ).then_inc(a_nm[l], 1)

                maxes(0)
                for h in range(HEADS):
                    probs(h)
                    if h + 1 < HEADS:
                        maxes(h + 1)
                dve.wait_ge(a_o[l], HEADS)
                V.memset(merged, 0.0).then_inc(g_d[l], 2)
                dve.wait_ge(g_d[l], 2)
                with dve.Fori(0, 3) as n:
                    for m in range(DK):
                        dve.wait_ge(g_t[l], n * DK + (m + 1))
                        dve.wait_ge(g_pe[l], n * (2 * DK) + (2 * m + 2))
                        dve.wait_ge(g_d[l], n * DK + (m + 2))
                        V.scalar_tensor_tensor(mtmp[:, 0:T], gate_t[:, m % 2, 0:T], 1.0, bank[2 + m % 2][:, 0:T],
                                               ALU.add, ALU.mult).then_inc(dve_c, 1)
                        dve.wait_ge(dve_c, n * DK + (chain[0] + m + 1))
                        V.tensor_tensor(merged[:, m, 0:T], merged[:, m, 0:T], mtmp[:, 0:T], ALU.add
                                        ).then_inc(g_d[l], 1)
                chain[0] += 3 * DK
                for k in range(DK):
                    trail_h(k, 2 * DK * l + DK, merged, T)
                for m in range(DK):
                    dve.wait_ge(o_pe[l], m + 1)
                    for s in range(S):
                        v = xT[:, m, s * SEQ:(s + 1) * SEQ]
                        V.scalar_tensor_tensor(v, bank[m % 2][:, s * SEQ:(s + 1) * SEQ], half_gate[:, m, s:s + 1], v,
                                               ALU.mult, ALU.add).then_inc(o_d[l], 1)
                dve.wait_ge(o_d[l], 8 * S)
                norm_dve(2 * l + 1, T)
                nt = T // P
                NE = nt * E_N
                G4 = nt * 4

                def r16(i):
                    return rt[:, i, 0:NE]

                def r4(i):
                    return rt[:, i, 0:NE].rearrange("p (g k) -> p g k", k=4)

                def r1(i):
                    return rt[:, i, 0:G4]

                def rje(i):
                    return rt[:, i, 0:NE].rearrange("p (j e) -> p j e", e=E_N)

                dve.wait_ge(q_ex[l], l + 1)
                link(V.tensor_scalar(r16(2), r16(1), 1.0, None, ALU.add))
                link(V.reciprocal(r16(1), r16(2)))
                link(V.tensor_tensor(rje(2), rje(1), rbias[:].unsqueeze(1).to_broadcast([P, nt, E_N]), ALU.add))

                def place(src, dst, n, view):
                    link(V.memset(dst, 0.0))
                    v, d = view(src), view(dst)
                    for i in range(n):
                        for j in range(i + 1, n):
                            t = rt[:, 30, 0:v.shape[1]]
                            link(V.tensor_tensor(t, v[:, :, i], v[:, :, j], ALU.is_ge))
                            link(V.tensor_tensor(d[:, :, j], d[:, :, j], t, ALU.add))
                            link(V.scalar_tensor_tensor(d[:, :, i], d[:, :, i], 1.0, t, ALU.add, ALU.subtract))

                place(r16(2), r16(3), 4, lambda v: v.rearrange("p (g k) -> p g k", k=4))
                link(V.tensor_scalar(r16(4), r16(3), 1.5, None, ALU.is_lt))
                link(V.tensor_tensor(r16(5), r16(4), r16(2), ALU.mult))
                link(V.tensor_reduce(r1(6), r4(5), AX.X, ALU.add))
                place(r1(6), r1(7), 4, lambda v: v.rearrange("p (j g) -> p j g", g=4))
                link(V.tensor_scalar(r1(8), r1(7), 0.5, None, ALU.is_lt))
                V.tensor_tensor(r4(0), r4(4), r1(8).unsqueeze(2).to_broadcast([P, G4, 4]), ALU.mult
                                ).then_inc(q_m[l], 1)
                dve.wait_ge(q_m[l], l + 1)
                link(V.tensor_tensor(r16(9), r16(0), r16(1), ALU.mult))
                link(V.tensor_reduce(rt[:, 10, 0:nt], rje(9), AX.X, ALU.add))
                link(V.reciprocal(rt[:, 11, 0:nt], rt[:, 10, 0:nt]))
                link(V.tensor_scalar(rt[:, 11, 0:nt], rt[:, 11, 0:nt], 0.5, None, ALU.mult))
                link(V.tensor_tensor(rje(9), rje(9), rt[:, 11, 0:nt].unsqueeze(2).to_broadcast([P, nt, E_N]), ALU.mult))
                dve.wait_ge(q_rk[l], l + 1)
                link(V.tensor_tensor(rje(12), bank[7][:, 0:NE].rearrange("p (j e) -> p j e", e=E_N),
                                     slot0[:].unsqueeze(1).to_broadcast([P, nt, E_N]), ALU.add))
                for i in range(1, nt):
                    link(V.tensor_scalar(rje(18), bank[7][:, 0:NE].rearrange("p (j e) -> p j e", e=E_N),
                                         float(i * P), float((E_N - 1) * P), ALU.is_ge, ALU.mult))
                    link(V.tensor_tensor(r16(12), r16(12), r16(18), ALU.add))
                link(V.scalar_tensor_tensor(r16(12), r16(12), 1.0, r16(0), ALU.add, ALU.mult))
                link(V.tensor_reduce(rt[:, 13, 0:nt], rje(12), AX.X, ALU.max))
                link(V.tensor_reduce(rt[:, 14, 0:nt], rje(12), AX.X, ALU.add))
                link(V.tensor_tensor(rt[:, 14, 0:nt], rt[:, 14, 0:nt], rt[:, 13, 0:nt], ALU.subtract))
                link(V.tensor_scalar(didx[:, 0, 0:nt], rt[:, 14, 0:nt], -1.0, None, ALU.add))
                link(V.tensor_scalar(didx[:, 1, 0:nt], rt[:, 13, 0:nt], -1.0, None, ALU.add))
                link(V.tensor_reduce(rt[:, 15, 0:1], bank[7][:, 64:64 + E_N], AX.X, ALU.max))
                V.tensor_copy(cnt_u[:], rt[:, 15, 0:1]).then_inc(q_ix[l], 1)
                link(V.tensor_tensor(rje(16), rje(12), rt[:, 13, 0:nt].unsqueeze(2).to_broadcast([P, nt, E_N]),
                                     ALU.is_equal))
                link(V.tensor_tensor(r16(16), r16(16), r16(9), ALU.mult))
                link(V.tensor_reduce(wsel[:, 1, 0:nt], rje(16), AX.X, ALU.add))
                link(V.tensor_reduce(rt[:, 17, 0:nt], rje(9), AX.X, ALU.add))
                link(V.tensor_tensor(wsel[:, 0, 0:nt], rt[:, 17, 0:nt], wsel[:, 1, 0:nt], ALU.subtract))
                dve.wait_ge(q_tt[l], l + 1)
                V.tensor_copy(tidx[:], bank[6][:, 64:128]).then_inc(q_ti[l], 1)

                def rows_in(par_, e):
                    dve.wait_ge(x_tr[l], 16 * l + e + 1)
                    V.tensor_copy(heT[:, par_, 4:8, :], bank[1][:, :].rearrange("p (k t) -> p k t", k=4)
                                  ).then_inc(x_hd[l], 1)

                def hidden(par_, s):
                    dve.wait_ge(x_th[l], 16 * l + s + 1)
                    V.scalar_tensor_tensor(thb[:, par_, :], thb[:, par_, :], 1.0, bank[2][:, :], ALU.add, ALU.mult
                                           ).then_inc(x_th2[l], 1)
                    dve.wait_ge(x_th2[l], 16 * l + s + 1)
                    V.tensor_tensor(hid[:, par_, :], thb[:, par_, :], bank[3][:, :], ALU.mult).then_inc(x_hid[l], 1)

                def y_out(par_, s, free):
                    dve.wait_ge(x_y[l], 16 * l + s + 1)
                    if free is not None:
                        dve.wait_ge(x_st[l][par_], free)
                    V.tensor_copy(yb[:, par_, 512:1024], bank[6][:, :]).then_inc(x_yd[l], 1)

                rows_in(0, 0)
                hidden(0, 0)
                rows_in(1, 1)
                for s in (1, 2):
                    hidden(s % 2, s)
                    y_out((s - 1) % 2, s - 1, None)
                    rows_in((s + 1) % 2, s + 1)
                with dve.Fori(1, 7) as i:
                    hidden(1, 2 * i + 1)
                    y_out(0, 2 * i, i * 16)
                    rows_in(0, 2 * i + 2)
                    hidden(0, 2 * i + 2)
                    y_out(1, 2 * i + 1, i * 16)
                    rows_in(1, 2 * i + 3)
                hidden(1, 15)
                y_out(0, 14, 16 * 7)
                y_out(1, 15, 16 * 7)
                most = dve.value_load(cnt_u[0:1, 0:1], min_val=0, max_val=NT)
                with dve.If(most > P):
                    for i in range(2):
                        dve.wait_ge(x_st[l][i], 16 * E_N // 2)
                    with dve.Fori(0, (nt - 1) * E_N) as b:
                        V.tensor_copy(over_idx[:], tidx[:, bass.ds(b + E_N, 1)]).then_inc(v_d[l], 1)
                        dve.wait_ge(v_pe[l], b * 4 + 1)
                        V.tensor_copy(heT[:, 0, 0:4, :], bank[0][:, :].rearrange("p (k t) -> p k t", k=4))
                        V.tensor_copy(heT[:, 0, 4:8, :], bank[1][:, :].rearrange("p (k t) -> p k t", k=4)
                                      ).then_inc(v_d[l], 1)
                        dve.wait_ge(v_a[l], b + 1)
                        V.scalar_tensor_tensor(thb[:, 0, :], thb[:, 0, :], 1.0, bank[2][:, :], ALU.add, ALU.mult
                                               ).then_inc(v_d[l], 1)
                        dve.wait_ge(v_d[l], b * 6 + 3)
                        V.tensor_tensor(hid[:, 0, :], thb[:, 0, :], bank[3][:, :], ALU.mult).then_inc(v_d[l], 1)
                        dve.wait_ge(v_pe[l], b * 4 + 3)
                        V.tensor_copy(hidT[:, 0, :, :], bank[4][:, :].rearrange("p (k t) -> p k t", k=4)
                                      ).then_inc(v_d[l], 1)
                        dve.wait_ge(v_pe[l], b * 4 + 4)
                        V.tensor_copy(yb[:, 0, 0:512], bank[5][:, :])
                        V.tensor_copy(yb[:, 0, 512:1024], bank[6][:, :]).then_inc(v_d[l], 1)
                with dve.Else():
                    dve.nop()
                dve.wait_ge(z_g[l], 32 * nt)
                for j in range(nt):
                    link(V.tensor_scalar(fa[:, j, :], fa[:, j, :], wsel[:, 0, j:j + 1], None, ALU.mult))
                    V.scalar_tensor_tensor(fa[:, j, :], fb[:, j, :], wsel[:, 1, j:j + 1], fa[:, j, :],
                                           ALU.mult, ALU.add).then_inc(z_f[l], 1)
                for k in range(DK):
                    dve.wait_ge(z_t[l], k + 1)
                    for s in range(S):
                        v = xT[:, k, s * SEQ:(s + 1) * SEQ]
                        V.scalar_tensor_tensor(v, bank[k][:, s * SEQ:(s + 1) * SEQ], mods[:, 5 * DK + k, s:s + 1], v,
                                               ALU.mult, ALU.add).then_inc(z_x[l], 2 // S)
                dve.wait_ge(z_x[l], 16)
            norm_dve(4, SEQ)


def shape_constants():
    import numpy as np
    n = SEQ
    t = np.arange(n, dtype=np.float64)
    f = np.arange(n, dtype=np.float64)
    ang = 2 * np.pi * np.outer(t, f) / (2 * n)
    cos, sin = np.cos(ang), np.sin(ang)
    alt = (-1.0) ** t
    fwd = np.concatenate([cos, -sin], axis=1)
    fwd[:, n] = alt
    inv = np.concatenate([2 * cos.T, -2 * sin.T], axis=0) / (2 * n)
    inv[0] = 1.0 / (2 * n)
    inv[n] = alt / (2 * n)
    c = {}
    c["dft_f"] = fwd.reshape(2, P, 512).transpose(1, 0, 2)
    c["dft_i"] = inv.reshape(4, P, n).transpose(1, 0, 2)
    c["sel2"] = (np.arange(P)[:, None] % 32 == np.arange(2)[None, :])
    c["nyq"] = alt.reshape(2, P).T
    ident = np.eye(P)
    perm = np.zeros((P, P))
    for m in range(P):
        if m % 64 < 32:
            perm[m + 32, m] = -1.0
        else:
            perm[m - 32, m] = 1.0
    tri = np.triu(np.ones((P, P)), 1)
    c["square"] = np.stack([ident, perm, tri, np.ones((P, P))], axis=1)
    nf = DH // 4
    inv_f = (10000.0 ** (-np.arange(nf, dtype=np.float32) / nf)).astype(np.float32)
    row = (np.arange(n) // GRID).astype(np.float32)
    col = (np.arange(n) % GRID).astype(np.float32)
    an = np.concatenate([row[:, None] * inv_f, col[:, None] * inv_f], axis=-1)
    idx = np.arange(P) % 32
    c["rope"] = np.stack([np.cos(an)[:, idx].T, np.sin(an)[:, idx].T], axis=1)
    j = np.arange(GRID)
    st = np.clip(j - KW // 2, 0, GRID - KW)
    ok = (j[None, :] >= st[:, None]) & (j[None, :] < st[:, None] + KW)
    c["colmask"] = np.tile(np.where(ok, 0.0, -1e30), (2, 1))
    edge = np.ones((BK, 16))
    for g in range(BK):
        w = 2 << g
        for x in range(16):
            tt = x if x < 8 else n - 16 + x
            edge[g, x] = w / (min(tt + w - w // 2, n) - max(tt - w // 2, 0))
    c["edge"] = np.broadcast_to(edge, (P, BK, 16))
    c["slot0"] = np.broadcast_to(np.arange(E_N) * P, (P, E_N))
    c["tok_id"] = np.arange(4)[None, :] * P + np.arange(P)[:, None]
    tl = np.linspace(0.0, 1.0, n, dtype=np.float32)
    bands = (HY_E - 1) // 2
    fr = np.linspace(1e-4, bands - 1, bands, dtype=np.float32)
    an = np.float32(2.0 * np.pi / n) * np.arange(n, dtype=np.float32)
    z = np.concatenate([tl[:, None], np.cos(fr[None, :] * an[:, None]), -np.sin(fr[None, :] * an[:, None])], axis=-1)
    c["filter_in"] = z.T
    lo, hi = np.log(1e-2) / 0.3, np.log(1e-2) / 1.5
    deltas = np.abs(np.linspace(lo, hi, BW, dtype=np.float32))
    c["decay"] = np.exp(-tl[:, None] * deltas).reshape(2, P, BW).transpose(1, 0, 2)
    return {k: np.ascontiguousarray(v, dtype=np.float32) for k, v in c.items()}


def kernel(x, c, ctx, c_ctx, norm1_g, norm2_g, w_mod, b_mod, w_in, rpb, pool_w, pool_scale,
           hy_short_w, hy_short_b, hy_w1, hy_b1, hy_freq, hy_w2, hy_b2, hy_w3, hy_skip,
           w_branch, w_out, w_router, router_bias, w_gate_e, w_up_e, w_down_e, final_g):
    import numpy as np
    import concourse.bacc as bacc
    from concourse.bass_utils import run_bass_kernel_spmd

    def cols(v):
        return np.asarray(v).reshape(-1, P).T

    data = dict(shape_constants())
    tokens = np.concatenate([np.asarray(x)[0], np.asarray(ctx)[0]], axis=0)
    data["x_cols"] = tokens.T.reshape(DK, P, NT).transpose(1, 0, 2)
    data["c_cols"] = np.stack([cols(np.asarray(c)[0]), cols(c_ctx)], axis=2).reshape(P, DK * 2)
    for l in range(DEPTH):
        filt = np.zeros((P, 3), np.float32)
        filt[0:HY_H, 0] = hy_b1[l]
        filt[0:HY_H, 1] = hy_freq[l]
        filt[0:HY_H, 2] = hy_b2[l]
        data[f"par{l}"] = np.concatenate(
            [cols(norm1_g[l]), cols(norm2_g[l]), cols(b_mod[l]), cols(pool_scale[l])]
            + [cols(hy_short_w[l, i]) for i in range(NTAP)] + [cols(hy_short_b[l])]
            + [cols(hy_skip[l, i]) for i in range(HY_O)] + [filt], axis=1)
    pad = np.zeros((DEPTH, HEADS, 15, 128), np.float32)
    pad[:, :, :, 63 - (KW - 1):63 + KW] = rpb
    r, q, slot, k = np.ix_(range(2), range(GRID), range(6), range(GRID))
    data["rpb_win"] = pad[:, :, 5 - r + slot, 63 + k - q].reshape(DEPTH, HEADS, P, 6, GRID)
    data["fin_g"] = cols(final_g)
    data["w_router"] = np.asarray(w_router).reshape(DK, P, E_N).transpose(1, 0, 2)
    data["router_bias"] = np.broadcast_to(np.asarray(router_bias), (P, E_N))
    for name, v in (("w_mod", w_mod), ("w_in", w_in), ("pool_w", pool_w), ("hy_w1", hy_w1), ("hy_w2", hy_w2),
                    ("hy_w3", hy_w3), ("w_branch", w_branch), ("w_out", w_out), ("w_gate_e", w_gate_e),
                    ("w_up_e", w_up_e), ("w_down_e", w_down_e)):
        data[name] = v
    nc = bacc.Bacc("TRN2", target_bir_lowering=False, num_devices=1)
    arrays, aps = {}, {}
    for name, v in data.items():
        v = np.ascontiguousarray(v)
        arrays[f"in_{name}"] = v
        aps[name] = nc.dram_tensor(f"in_{name}", v.shape, mybir.dt.from_np(v.dtype), kind="ExternalInput").ap()
    out = nc.dram_tensor("out", (1, SEQ, D), F32, kind="ExternalOutput").ap()
    build(nc, aps, out)
    r = run_bass_kernel_spmd(nc, [arrays], core_ids=[0])
    return r.results[0]["out"]
```

```python
from contextlib import ExitStack

import concourse.bass as bass
from concourse import mybir

P = 128
D = 1024
DK = D // P
SEQ = 256
CTX = 256
NT = SEQ + CTX
DEPTH = 2
BW = D // 2
BK = BW // P
HEADS = 8
DH = 64
GRID = 64
KW = 16
E_N = 16
FF = 512
FK = FF // P
N_MOD = 6
MOD_T = N_MOD * DK
NTAP = 3
HY_H = 64
HY_E = 33
HY_O = 2
EPS = 1e-6
RPB_W = 2 * KW - 1

F32 = mybir.dt.float32
F32R = mybir.dt.float32r
U32 = mybir.dt.uint32
ALU = mybir.AluOpType
ACT = mybir.ActivationFunctionType
AX = mybir.AxisListType

RS = 3
RW = 2048
WS = 4
AHEAD = 2
MOD_C = 24
MOD_G = MOD_C // 2
MOD_FIRST = 4
MOD_EARLY, MOD_MID, MOD_LATE = 5, 8, 10
IN_C = 14
MERGE_C = 18
OUT_C = 4
EXP_C = 6 * E_N
HALVES = 2 * (IN_C + 2 * MERGE_C // 3 + OUT_C)

C_G1, C_G2, C_BMOD = 0, 8, 16
C_PS = C_BMOD + MOD_T
C_TAP = C_PS + BK
C_SB = C_TAP + NTAP * 12
C_SKIP = C_SB + 12
C_FILT = C_SKIP + HY_O * BK
C_N = C_FILT + 3
IN_ORDER = [8, 9, 10, 11, 12, 13, 6, 7, 0, 1, 2, 3, 4, 5]
GATE_C0 = 14
MOD_AFTER_1 = {1: 10, 3: 11}
MOD_AFTER_0 = {1: 4, 3: 5, 4: 6, 6: 7, 7: 8, 8: 9, 10: 10, 11: 11}
POOL_PAD = 8
POOL_L = SEQ + 2 * POOL_PAD
TWO_PI = 6.283185307179586


def build(nc, a, out):
    ctx = ExitStack()
    with ctx:
        def sb(name, shape, dt=F32):
            return ctx.enter_context(nc.sbuf_tensor(name, shape, dt))

        def sem(name):
            return ctx.enter_context(nc.semaphore(name))

        def sems(name, n=DEPTH):
            return [sem(f"{name}{i}") for i in range(n)]

        def both(name):
            return [sem(name)] * DEPTH

        def tcols(l):
            return NT if l == 0 else SEQ

        def streams(l):
            return 2 if l == 0 else 1

        h_rows = [nc.dram_tensor(f"h_rows{l}", [NT, D], F32).ap() for l in range(DEPTH)]
        y_rows = [nc.dram_tensor(f"y_rows{l}", [E_N * tcols(l), D], F32).ap() for l in range(DEPTH)]
        slot_tok = [nc.dram_tensor(f"slot_tok{l}", [E_N * NT, 1], F32).ap() for l in range(DEPTH)]

        ring = sb("ring", [P, RS, RW])
        xT = sb("xT", [P, DK, NT])
        h_hi = sb("h_hi", [P, DK, NT], F32R)
        h_lo = sb("h_lo", [P, DK, NT], F32R)
        w_hi = sb("w_hi", [P, WS, DK, P], F32R)
        w_lo = sb("w_lo", [P, WS, DK, P], F32R)
        dft_f = sb("dft_f", [P, 2, 512])
        dft_i = sb("dft_i", [P, 4, SEQ])
        square = sb("square", [P, 4, P])
        ident, perm, tri, ones = (square[:, i, :] for i in range(4))
        earlier = sb("earlier", [P, 16])
        edge = sb("edge", [P, BK, 16])
        nyq = sb("nyq", [P, 2])
        sel2 = sb("sel2", [P, 2])
        csil = sb("csil", [P, DK, 32])
        slot0 = sb("slot0", [P, E_N])
        tok_id = sb("tok_id", [P, 4])
        par = [sb(f"par{l}", [P, C_N]) for l in range(DEPTH)]
        fin_g = sb("fin_g", [P, DK])
        cc = sb("cc", [P, 3, DK * 2])
        poolw = sb("poolw", [P, BK, P])
        rbias = sb("rbias", [P, E_N])
        mods = sb("mods", [P, MOD_T, 2])
        gs = sb("gs", [P, 2, DK, 2])
        half_gate = sb("half_gate", [P, DK, 2])
        small = sb("small", [P, 16])
        MIX = 22528
        mix = sb("mix", [P, MIX])

        def area(o, n):
            assert o + n <= MIX
            return mix[:, o:o + n]

        ys = area(0, 6144).rearrange("p (n c t) -> p n c t", n=3, c=BK)
        qT = ys[:, 0]
        ys_pool = ys[:, 1]
        hv = ys[:, 2]
        kT = area(6144, 2048).rearrange("p (c t) -> p c t", c=BK)
        vtok = area(8192, 2048).rearrange("p (j f) -> p j f", j=4)
        hx = area(10240, 4096).rearrange("p (o c t) -> p o c t", o=2, c=BK)
        spec = area(14336, 4096).rearrange("p (o f c) -> p o f c", o=2, f=4)
        work = area(18432, 4096)
        merged = area(6144, 4096).rearrange("p (k t) -> p k t", k=DK)
        hT = area(10240, 4096).rearrange("p (k t) -> p k t", k=DK)
        w3s = area(0, 2048)[0:HY_H, :]
        decay = area(2048, 1024).rearrange("p (j c) -> p j c", j=2)
        fz = area(3072, 256)[0:HY_E, :]
        fw1 = area(3328, 64)[0:HY_E, :]
        fw2 = area(3392, 64)[0:HY_H, :]
        fpm = area(6144, 2048).rearrange("p (i j c) -> p i j c", i=2, j=2)
        fraw = area(8192, 2048).rearrange("p (i j c) -> p i j c", i=2, j=2)
        fabs_ = work[:, 0:1024].rearrange("p (j c) -> p j c", j=2)
        fnorm = work[:, 1024:1536]
        fhid = work[:, 1536:1536 + 3 * 256].rearrange("p (i t) -> p i t", i=3)
        fang = work[:, 2304:2304 + 2 * 256].rearrange("p (i t) -> p i t", i=2)
        mods_next = area(6400, MOD_T * 2).rearrange("p (m s) -> p m s", s=2)
        mrow = work[:, 3072:4096].rearrange("p (i c) -> p i c", i=2)
        sqb = area(18432, 1024).rearrange("p (i t) -> p i t", i=2)
        nrm = area(18432 + 1024, 2048).rearrange("p (i t) -> p i t", i=4)
        up = work[:, 0:2 * POOL_L].rearrange("p (s t) -> p s t", s=2)
        ps_a = work[:, 576:576 + 2 * POOL_L].rearrange("p (s t) -> p s t", s=2)
        ps_b = work[:, 1152:1152 + 2 * POOL_L].rearrange("p (s t) -> p s t", s=2)
        ypool = work[:, 2048:4096].rearrange("p (c t) -> p c t", c=BK)
        zt = work[:, 0:1024].rearrange("p (j c) -> p j c", j=2)
        hy_y = work[:, 1024:3072].rearrange("p (f c) -> p f c", f=4)
        hy_t = work[:, 3072:4096].rearrange("p (i c) -> p i c", i=2)
        qrot = area(14336, 1024).rearrange("p (c t) -> p c t", c=BK)
        krot = area(15360, 1024).rearrange("p (c t) -> p c t", c=BK)
        rtmp = area(16384, 512).rearrange("p (i t) -> p i t", i=2)
        rope = area(16896, 512).rearrange("p (i t) -> p i t", i=2)
        colmask = area(17408, GRID)
        wrt = area(17472, DK * E_N).rearrange("p (k e) -> p k e", k=DK)
        prob = work[:, 0:2048].rearrange("p (u t) -> p u t", u=4)
        bias = work[:, 2048:2048 + 768].rearrange("p (i s j) -> p i s j", i=2, s=6)
        pstat = work[:, 2816:2816 + 32].rearrange("p (u i) -> p u i", u=4)
        pT_s = area(10240, 3072).rearrange("p (i k t) -> p i k t", i=2, k=6)
        gate_t = work[:, 0:1024].rearrange("p (i t) -> p i t", i=2)
        mtmp = work[:, 1024:1536]
        htok = area(0, 4096).rearrange("p (j d) -> p j d", j=4)
        rt = area(4096, 2048).rearrange("p (i x) -> p i x", i=32)
        logit = area(6528, 512)[0:E_N, :]
        wide = area(6528, 512).rearrange("p (i x) -> p i x", i=2)
        ids_f = area(6144, 128)[0:64, :]
        tidx = sb("tidx", [P, 64], U32)
        didx = sb("didx", [P, 2, 4], U32)
        cnt_u = sb("cnt_u", [P, 1], U32)
        wsel = sb("wsel", [P, 2, 4])
        zero_ids = area(6272, 64)
        hg = area(8192, 2048).rearrange("p (i d) -> p i d", i=2)
        heT = area(10240, 2048).rearrange("p (i k t) -> p i k t", i=2, k=DK)
        hid = area(12288, 1024).rearrange("p (i f) -> p i f", i=2)
        thb = area(13312, 1024).rearrange("p (i f) -> p i f", i=2)
        hidT = area(14336, 1024).rearrange("p (i k t) -> p i k t", i=2, k=FK)
        yb = area(15360, 2048).rearrange("p (i d) -> p i d", i=2)
        over_w = [area(0, 4096), area(17408, 4096)]
        over_idx = sb("over_idx", [P, 1], U32)
        fa = area(0, 4096).rearrange("p (j d) -> p j d", j=4)
        fb = area(8192, 4096).rearrange("p (j d) -> p j d", j=4)

        bank = [ctx.enter_context(nc.psum_tensor(f"bank{i}", [P, 512], F32)) for i in range(8)]

        s_ld = sem("constants_loaded")
        s_ldl = sems("layer_params_loaded")
        ring_full = [sem(f"ring_full{i}") for i in range(RS)]
        ring_used = sem("ring_used")
        w_h = sem("weight_half_leading")
        w_l = sem("weight_half_split")
        w_u = sem("weight_half_used")
        h_h = sem("operand_leading")
        h_l = sem("operand_split")
        dve_c = sem("dve_chain")
        act_c = sem("act_chain")
        s_ce = sem("c_exp")
        s_cs = sem("c_silu")
        f_p = both("filter_pe")
        f_d = both("filter_dve")
        f_a = both("filter_act")
        m_ev = both("mod_rows_copied")
        m_co = both("mod_columns_ready")
        m_tk = both("mod_columns_taken")
        m_d = both("mod_ready")
        n_sq = sem("norm_squares")
        n_mm = sem("norm_sums")
        n_a = sem("norm_mean")
        n_s = sem("norm_root")
        n_x = sem("norm_scaled")
        n_h = sem("norm_modulated")
        j_pe = sems("proj_products")
        j_c = sems("conv_centre")
        j_d = sems("proj_taken_dve")
        j_a = sems("proj_taken_act")
        pw_pe = both("pool_products")
        pw_a = both("pool_scaled")
        y_tp = sems("z_transposed")
        y_zt = sems("z_rows_ready")
        y_f = sems("spectrum_ready")
        y_m = sems("spectra_multiplied")
        y_i = sems("inverse_ready")
        y_z = sems("z_updated")
        r_ld = both("rope_tables_loaded")
        r_pe = both("rope_swapped")
        r_d = both("rope_ready")
        b_ld = [sems(f"bias_loaded{l}_", 2) for l in range(DEPTH)]
        b_fix = sems("bias_masked")
        a_sc = sems("scores_ready")
        a_mx = sems("score_max_ready")
        a_ex = sems("exp_ready")
        a_nm = sems("probs_ready")
        a_tr = sems("probs_transposed")
        a_ev = sems("probsT_ready")
        a_pv = sems("attention_out")
        a_o = sems("attention_taken")
        g_pe = sems("merge_products")
        g_t = sems("gate_tanh")
        g_d = sems("merge_taken")
        o_pe = sems("out_products")
        o_d = sems("residual_added")
        t_pe = sems("rows_transposed")
        t_ev = sems("rows_copied")
        t_st = sems("rows_stored")
        q_z = both("zeros_ready")
        q_zd = both("slot_table_cleared")
        q_lg = both("logits_ready")
        q_ex = both("logits_exp")
        q_m = both("experts_chosen")
        q_rk = both("ranks_ready")
        q_ix = both("slots_ready")
        q_sc = both("slots_scattered")
        q_tb = both("slot_table_loaded")
        q_tt = both("slot_table_transposed")
        q_ti = both("token_index_ready")
        x_g = [sems(f"rows_gathered{l}_", 2) for l in range(DEPTH)]
        x_tr = both("expert_rows_transposed")
        x_ha = both("expert_in_act")
        x_hd = both("expert_in_dve")
        x_gu = both("gate_up_ready")
        x_th = both("expert_tanh")
        x_th2 = both("gate_silu_ready")
        x_hid = both("hidden_ready")
        x_ht = both("hidden_transposed")
        x_hte = both("hiddenT_ready")
        x_y = both("expert_out_ready")
        x_ya = both("expert_out_act")
        x_yd = both("expert_out_dve")
        x_st = [sems(f"expert_out_stored{l}_", 2) for l in range(DEPTH)]
        v_w = sems("over_gate_up_loaded")
        v_wd = sems("over_down_loaded")
        v_g = sems("over_gathered")
        v_pe = sems("over_products")
        v_a = sems("over_tanh")
        v_d = sems("over_vector")
        v_s = sems("over_stored")
        v_done = sems("over_areas_free")
        v_t = sems("over_wait_taken")
        z_g = [sem(f"combine_gathered_tile{j}") for j in range(NT // P)]
        z_s = both("combine_scaled")
        z_f = sems("combined")
        z_t = sems("combined_transposed")
        z_x = sems("moe_added")
        e_t = sem("final_transposed")
        e_c = sem("final_copied")
        e_s = sem("output_stored")

        def mbank(l, g):
            return bank[(4 if l and g < MOD_EARLY else 5) + g % 2]

        fbank = [bank[i] for i in (2, 3, 4, 7)]

        deep = [1, 2]
        units_of = [[(x, s) for s in range(streams(l)) for x in range(2)] for l in range(DEPTH)]

        def win(l, c):
            return a["w_in"][l].rearrange("(k p) n -> p k n", p=P)[:, :, c * 256:(c + 1) * 256]

        def chunk_src(l, i):
            if i < IN_C:
                return win(l, IN_ORDER[i]), 8
            i -= IN_C
            if i < MERGE_C:
                n, r = divmod(i, 6)
                h, r = divmod(r, 3)
                if r == 1:
                    v = a["w_branch"][l, n].rearrange("(k p) n -> p k n", p=P)
                    return v[:, :, h * 512:(h + 1) * 512], 4
                return win(l, GATE_C0 + n * 4 + 2 * h + r // 2), 8
            i -= MERGE_C
            return a["w_out"][l].rearrange("(k p) n -> p k n", p=P)[:, :, i * 256:(i + 1) * 256], 8

        def rview(slot, k):
            return ring[:, slot, :].rearrange("p (k n) -> p k n", k=k)

        def merge_chunk(m):
            n, r = divmod(m, DK)
            return 6 * n + 3 * (r // 4) + 2 * (r % 4 // 2)

        def mod_after(l):
            return MOD_AFTER_0 if l == 0 else MOD_AFTER_1

        order = [("mod", 0, 2 * g + h) for g in range(MOD_FIRST) for h in range(2)]
        for l in range(DEPTH):
            if l == 0:
                order.append(("in", l, 0))
            for g in range(2 * IN_C - AHEAD):
                if g % 2 == 0:
                    order.append(("in", l, (g + AHEAD) // 2))
                if g in mod_after(l):
                    order += [("mod", l, 2 * mod_after(l)[g] + h) for h in range(2)]
            order += [("merge", l, i) for i in range(MERGE_C)] + [("out", l, i) for i in range(OUT_C)]
            if l + 1 < DEPTH:
                order += [("mod", l + 1, i) for i in range(2 * MOD_EARLY)]
            order += [("exp", l, i) for i in range(EXP_C)]
            if l + 1 < DEPTH:
                order += [("mod", l + 1, i) for i in range(2 * MOD_EARLY, 2 * MOD_MID)] + [("in", l + 1, 0)]
                order += [("mod", l + 1, i) for i in range(2 * MOD_MID, 2 * MOD_LATE)]
        assert len(order) == DEPTH * (MOD_C + IN_C + MERGE_C + OUT_C + EXP_C)
        at_of = {c: p for p, c in enumerate(order)}

        split_c = [kind in ("in", "out") or kind == "merge" and i % 3 != 1 for kind, _, i in order]

        def half_at(l, q):
            return at_of[("in", l, q // 2)] if q < 2 * IN_C else at_of[("merge", l, 0)]

        def fill(l, where):
            k = 2 // streams(l)
            return (k, 2 * k, k)[where]

        halves_to = [2 * sum(split_c[:i + 1]) for i in range(len(order))]
        direct_to = [i + 1 - sum(split_c[:i + 1]) for i in range(len(order))]

        def full_at(idx):
            return 16 * (idx // RS + 1)

        block = ctx.enter_context(nc.Block())

        @block.sync
        def _(sp):
            for dst, name in ((cc[:, 0, :], "c_cols"), (square[:], "square"), (sel2[:], "sel2"), (par[0][:], "par0"),
                              (xT[:], "x_cols")):
                sp.dma_start(dst, a[name]).then_inc(s_ld, 16)

            def slot_free(at):
                if at >= RS and split_c[at - RS]:
                    sp.wait_ge(w_l, halves_to[at - RS])
                elif at >= RS:
                    sp.wait_ge(ring_used, direct_to[at - RS])

            def tables(l):
                if l == 0:
                    for dst, name in ((dft_f[:], "dft_f"), (dft_i[:], "dft_i"), (edge[:], "edge"), (earlier[:], "earlier"),
                                      (nyq[:], "nyq"), (slot0[:], "slot0"), (tok_id[:], "tok_id"),
                                      (par[1][:], "par1"), (fin_g[:], "fin_g"), (rbias[:], "router_bias")):
                        sp.dma_start(dst, a[name]).then_inc(s_ldl[l], 16)
                else:
                    sp.wait_ge(z_x[l - 1], 16)
                for dst, src in ((w3s, a["hy_w3"][l]), (decay, a["decay"]), (fz, a["filter_in"]),
                                 (fw1, a["hy_w1"][l]), (fw2, a["hy_w2"][l]),
                                 (poolw[:], a["pool_w"][l].rearrange("g c d -> c g d"))):
                    sp.dma_start(dst, src).then_inc(s_ldl[l], 16)

            for l in range(DEPTH):
                lo = at_of[("exp", l - 1, EXP_C - 1)] + 1 if l else 0
                xb = at_of[("exp", l, 0)]
                for at in range(lo, xb):
                    kind, ll, i = order[at]
                    if at == (at_of[("mod", l, 2 * MOD_LATE - 2)] if l else RS):
                        tables(l)
                    if kind == "mod":
                        k = 4
                        src = a["w_mod"][ll].rearrange("(h k p) (g n) -> p h k g n", p=P, h=2, n=512
                                                       )[:, i % 2, :, i // 2, :]
                    else:
                        src, k = chunk_src(l, i + {"in": 0, "merge": IN_C, "out": IN_C + MERGE_C}[kind])
                    slot_free(at)
                    sp.dma_start(rview(at % RS, k), src).then_inc(ring_full[at % RS], 16)
                wg = a["w_gate_e"][l].rearrange("e (h k p) n -> p e h k n", p=P, h=2)
                wu = a["w_up_e"][l].rearrange("e (h k p) n -> p e h k n", p=P, h=2)
                wd = a["w_down_e"][l].rearrange("e (h k p) n -> p e h k n", p=P, h=2)

                xd = direct_to[xb - 1]

                def put(c, slot, w, e, h, k):
                    if isinstance(c, int) and c < RS:
                        slot_free(xb + c)
                    else:
                        sp.wait_ge(ring_used, c + (xd - RS + 1))
                    sp.dma_start(rview((xb + slot) % RS, k), w[:, bass.ds(e, 1), h].rearrange("p e k n -> p (e k) n")
                                 ).then_inc(ring_full[(xb + slot) % RS], 16)

                for h in range(2):
                    put(h, h, wg, 0, h, 4)
                for h in range(2):
                    put(2 + h, 2 + h, wu, 0, h, 4)

                def step(s):
                    at = s * 6 - 2
                    for h in range(2):
                        put(at + h, 4 + h, wg, s, h, 4)
                    for h in range(2):
                        put(at + 2 + h, h, wu, s, h, 4)
                    for h in range(2):
                        put(at + 4 + h, 2 + h, wd, s - 1, h, 2)

                with sp.Fori(0, 7) as i:
                    step(2 * i + 1)
                    step(2 * i + 2)
                step(15)
                for h in range(2):
                    put(EXP_C - 2 + h, 4 + h, wd, E_N - 1, h, 2)
                sp.wait_ge(q_ix[l], l + 1)
                most = sp.value_load(cnt_u[0:1, 0:1], min_val=0, max_val=NT)
                sp.wait_ge(x_hd[l], 16 * l + 1)
                with sp.If(most > P):
                    with sp.Fori(0, tcols(l) // P - 1) as r:
                        with sp.Fori(0, E_N) as e:
                            b = r * E_N + e
                            gu = [a[n][l].rearrange("e (k p) n -> p e k n", p=P) for n in ("w_gate_e", "w_up_e")]
                            dn = a["w_down_e"][l].rearrange("e (k p) n -> p e k n", p=P)
                            sp.wait_ge(x_y[l], 16 * l + 16)
                            sp.wait_ge(v_done[l], b + 1)
                            for i in range(2):
                                sp.dma_start(over_w[i].rearrange("p (k n) -> p k n", k=8),
                                             gu[i][:, bass.ds(e, 1)].rearrange("p e k n -> p (e k) n")
                                             ).then_inc(v_w[l], 16)
                            sp.wait_ge(v_pe[l], b * 4 + 2)
                            sp.dma_start(over_w[0].rearrange("p (k n) -> p k n", k=4),
                                         dn[:, bass.ds(e, 1)].rearrange("p e k n -> p (e k) n")).then_inc(v_wd[l], 16)
            sp.wait_ge(e_c, 2)
            sp.dma_start(out[0, 0:P, :], htok[:, 0, :]).then_inc(e_s, 16)
            sp.wait_ge(e_c, 4)
            sp.dma_start(out[0, P:2 * P, :], htok[:, 1, :]).then_inc(e_s, 16)
            sp.wait_ge(e_s, 32)

        @block.gpsimd
        def _(pool):
            for l in range(DEPTH):
                T = tcols(l)
                nt = T // P

                def trail(q, slot, x, raw):
                    pool.wait_ge(w_h, q + 1)
                    pool.tensor_tensor(w_lo[:, slot], rview(raw, 8)[:, :, x * P:(x + 1) * P],
                                       w_hi[:, slot].bitcast(F32), ALU.subtract).then_inc(w_l, 1)

                q0 = l * HALVES
                for q in range(2 * IN_C + AHEAD):
                    trail(q0 + q, q % WS, q % 2, half_at(l, q) % RS)
                pool.wait_ge(y_m[l], 4 * streams(l))
                pool.dma_start(rope, a["rope"]).then_inc(r_ld[l], 16)
                pool.dma_start(colmask, a["colmask"]).then_inc(r_ld[l], 16)
                pool.dma_start(wrt, a["w_router"]).then_inc(r_ld[l], 16)
                for h in range(HEADS):
                    if h >= 2:
                        pool.wait_ge(a_mx[l], len(units_of[l]) * (h - 1))
                    else:
                        pool.wait_ge(y_z[l], 2 * streams(l) * BK)
                    pool.dma_start(bias[:, h % 2], a["rpb_win"][l, h]).then_inc(b_ld[l][h % 2], 16)
                m0 = 2 * IN_C
                with pool.Fori(0, 3) as n:
                    for m in range(AHEAD, DK + AHEAD):
                        trail(n * DK + (q0 + m0 + m), m % WS, m % 2, (at_of[("merge", l, 0)] + merge_chunk(m)) % RS)
                for m in range(AHEAD, DK):
                    trail(q0 + m0 + 3 * DK + m, m % WS, m % 2, at_of[("out", l, m // 2)] % RS)
                pool.wait_ge(o_d[l], 8 * streams(l))
                pool.memset(zero_ids, 0.0).then_inc(q_z[l], 1)
                pool.wait_ge(q_z[l], l + 1)
                pool.dma_start(slot_tok[l].rearrange("(p x) o -> p (x o)", p=P), zero_ids).then_inc(q_zd[l], 16)
                pool.wait_ge(q_zd[l], 16 * (l + 1))
                for j in range(nt):
                    pool.wait_ge(t_ev[l], 2 * (j + 1))
                    pool.dma_start(h_rows[l][j * P:(j + 1) * P, :], htok[:, j, :]).then_inc(t_st[l], 16)
                pool.wait_ge(q_ix[l], l + 1)
                for j in range(nt):
                    for i in range(2):
                        pool.indirect_dma_start(
                            out=slot_tok[l], out_offset=bass.IndirectOffsetOnAxis(ap=didx[:, i, j:j + 1], axis=0),
                            in_=tok_id[:, j:j + 1], in_offset=None).then_inc(q_sc[l], 16)
                pool.wait_ge(q_sc[l], 16 * 2 * (nt if l == 0 else nt + NT // P))
                pool.dma_start(ids_f, slot_tok[l].rearrange("(r s) o -> r (s o)", s=P)).then_inc(q_tb[l], 16)
                pool.wait_ge(q_ti[l], l + 1)
                pool.wait_ge(t_st[l], 16 * nt)

                def gather(i, e, dst, done):
                    pool.indirect_dma_start(
                        out=dst, out_offset=None, in_=h_rows[l][0:tcols(l), :],
                        in_offset=bass.IndirectOffsetOnAxis(ap=e, axis=0)).then_inc(done, 16)

                def store(s, par_):
                    pool.wait_ge(x_ya[l], 16 * l + s + 1)
                    pool.wait_ge(x_yd[l], 16 * l + s + 1)
                    pool.dma_start(y_rows[l][s * P:(s + 1) * P, :], yb[:, par_, :]).then_inc(x_st[l][par_], 16)

                for e in range(2):
                    gather(e, tidx[:, e:e + 1], hg[:, e, :], x_g[l][e])
                for s in range(E_N):
                    if s + 2 < E_N:
                        pool.wait_ge(x_tr[l], 16 * l + s + 1)
                        gather(s, tidx[:, s + 2:s + 3], hg[:, s % 2, :], x_g[l][s % 2])
                    if s >= 1:
                        store(s - 1, (s - 1) % 2)
                store(E_N - 1, 1)
                for i in range(2):
                    pool.wait_ge(x_st[l][i], 16 * E_N // 2)

                def combine(rows):
                    for j in range(nt):
                        for i in range(2):
                            pool.indirect_dma_start(
                                out=(fa if i == 0 else fb)[:, j, :], out_offset=None, in_=y_rows[l][0:rows, :],
                                in_offset=bass.IndirectOffsetOnAxis(ap=didx[:, i, j:j + 1], axis=0)
                            ).then_inc(z_g[j], 16)

                most = pool.value_load(cnt_u[0:1, 0:1], min_val=0, max_val=NT)
                with pool.If(most > P):
                    with pool.Fori(0, (nt - 1) * E_N) as b:
                        pool.wait_ge(v_d[l], b * 6 + 1)
                        pool.tensor_tensor(zero_ids[:, 1:2], zero_ids[:, 0:1], zero_ids[:, 0:1], ALU.add
                                           ).then_inc(v_t[l], 1)
                        gather(0, over_idx[:], hg[:, 0, :], v_g[l])
                        pool.wait_ge(v_d[l], b * 6 + 6)
                        pool.dma_start(y_rows[l][bass.ds(b * P + E_N * P, P), :], yb[:, 0, :]).then_inc(v_s[l], 16)
                        pool.wait_ge(v_t[l], b + 1)
                        pool.wait_ge(v_s[l], b * 16 + 16)
                    combine(E_N * T)
                with pool.Else():
                    combine(E_N * P)

        @block.tensor
        def _(pe):
            mm = nc.tensor.matmul
            tp = nc.tensor.transpose

            def norm_pe(inst, cols):
                for k in range(DK):
                    pe.wait_ge(n_sq, inst * DK + k + 1)
                    mm(bank[7][:, 0:cols], ones, sqb[:, k % 2, 0:cols], start=k == 0, stop=k == DK - 1
                       ).then_inc(n_mm, 1)

            def mm3(dst, stat, mov, start, stop):
                first = mm(dst, stat[0], mov[0], start=start, stop=False)
                mm(dst, stat[1], mov[0], start=False, stop=False)
                return first, mm(dst, stat[0], mov[1], start=False, stop=stop)

            def mod_columns(l, g):
                pe.wait_ge(m_ev[l], 12 * l + g + 1)
                for c in range(4):
                    last = mm(mbank(l, g)[:, 2 * c:2 * c + 2], mrow[:, g % 2, c * P:(c + 1) * P], sel2[:],
                              start=True, stop=True)
                last.then_inc(m_co[l], 1)

            def mod(l, g):
                if g >= 2:
                    pe.wait_ge(m_tk[l], 12 * l + g - 1)
                for h in range(2):
                    at = at_of[("mod", l, 2 * g + h)]
                    pe.wait_ge(ring_full[at % RS], full_at(at))
                    for k in range(4):
                        last = mm(mbank(l, g)[32 * k:32 * k + 32, :], csil[:, 4 * h + k, :],
                                  rview(at % RS, 4)[:, k, :], start=h == 0, stop=h == 1)
                    last.then_inc(ring_used, 1)
                ends = [e - 1 for e in ((MOD_FIRST, MOD_G) if l == 0 else (MOD_EARLY, MOD_MID, MOD_LATE, MOD_G))]
                if g and g - 1 not in ends:
                    mod_columns(l, g - 1)
                if g in ends:
                    mod_columns(l, g)

            pe.wait_ge(s_ld, 16 * 5)
            norm_pe(0, NT)
            pe.wait_ge(s_cs, 1)
            for g in range(MOD_FIRST):
                mod(0, g)
            for l in range(DEPTH):
                T = tcols(l)
                S = streams(l)
                q0 = l * HALVES

                def w_part(slot, k):
                    return w_hi[:, slot, k, :], w_lo[:, slot, k, :]

                def h_part(k, c0, c1):
                    return h_hi[:, k, c0:c1], h_lo[:, k, c0:c1]

                def filters(o):
                    if o:
                        pe.wait_ge(f_d[l], 8 * l + 5)
                    for i in range(2):
                        for j in range(2):
                            last = mm(fbank[2 * i + j][:], fhid[0:HY_H, 2, j * P:(j + 1) * P],
                                      w3s[:, (2 * o + i) * BW:(2 * o + i + 1) * BW], start=True, stop=True)
                    last.then_inc(f_p[l], 1)

                def spectra_a(o):
                    pe.wait_ge(f_d[l], 8 * l + 3 + 3 * o)
                    for j in range(2):
                        mm(bank[7][:], ones, fabs_[:, j, :], start=j == 0, stop=j == 1)
                    for f in range(2):
                        for j in range(2):
                            mm(bank[2 + f][:], dft_f[:, j, f * P:(f + 1) * P], fpm[:, 0, j, :],
                               start=j == 0, stop=j == 1)
                    for j in range(2):
                        last = mm(bank[4][0:1, :], nyq[:, j:j + 1], fpm[:, 0, j, :], start=j == 0, stop=j == 1)
                    last.then_inc(f_p[l], 1)

                def spectra_b(o):
                    pe.wait_ge(f_d[l], 8 * l + 4 + 3 * o)
                    for f in range(2):
                        for j in range(2):
                            last = mm(bank[2 + f][:], dft_f[:, j, (2 + f) * P:(3 + f) * P], fpm[:, 1, j, :],
                                      start=j == 0, stop=j == 1)
                    last.then_inc(f_p[l], 1)

                def filter_part(g):
                    if g == 0:
                        pe.wait_ge(s_ldl[l], 16 * (16 if l == 0 else 6))
                        mm(bank[2][0:HY_H, 0:SEQ], fw1, fz, start=True, stop=True).then_inc(f_p[l], 1)
                    elif g == 2:
                        pe.wait_ge(f_a[l], 2 * l + 1)
                        mm(bank[3][0:HY_H, 0:SEQ], fw2, fhid[0:HY_H, 1, :], start=True, stop=True
                           ).then_inc(f_p[l], 1)
                    elif g == 3:
                        pe.wait_ge(f_a[l], 2 * l + 2)
                        filters(0)
                    elif g == 7:
                        filters(1)
                    elif g in (5, 9):
                        spectra_a(g // 9)
                    elif g in (6, 10):
                        spectra_b(g // 10)

                if l:
                    norm_pe(2 * l, NT)
                    for g in range(MOD_MID, MOD_LATE):
                        mod(l, g)
                def proj_tile(g):
                    cols = NT if g >= 20 else T
                    b = bank[g % 2 if g < 12 else g % 4 if g < 16 else 6 + g % 2]
                    pe.wait_ge(w_l, q0 + g + 1)
                    for k in range(DK):
                        if g == 0:
                            pe.wait_ge(h_l, 2 * DK * l + k + 1)
                        first, last = mm3(b[:, 0:cols], w_part(g % WS, k), h_part(k, 0, cols), k == 0, k == DK - 1)
                        if g and k == 0:
                            first.then_inc(w_u, 1)
                    last.then_inc(j_pe[l], 1)

                def value_tile(i, j):
                    pe.wait_ge(w_l, q0 + 24 + 2 * i + 2)
                    for k in range(DK):
                        w = [v[:, 2 * i:2 * i + 2, k, :] for v in (w_hi, w_lo)]
                        first, last = mm3(bank[6 + j % 2][:, 0:256].rearrange("p (x n) -> p x n", x=2),
                                          h_part(k, j * P, (j + 1) * P), w, k == 0, k == DK - 1)
                        if j + k == 0:
                            first.then_inc(w_u, 2 if i else 1)
                    last.then_inc(j_pe[l], 1)

                done = [0]

                def fill_tiles(n):
                    for u in range(done[0], done[0] + n):
                        if u >= 2:
                            pe.wait_ge(j_a[l], u - 1)
                        if u < 8:
                            proj_tile(16 + u)
                        else:
                            value_tile((u - 8) // 4, u % 4)
                    done[0] += n

                for g in range(16):
                    if g in (14, 15):
                        pe.wait_ge(f_d[l], 8 * l + 8)
                    elif g >= 2:
                        pe.wait_ge(j_d[l], g - 1)
                    proj_tile(g)
                    filter_part(g)
                    if g in mod_after(l):
                        mod(l, mod_after(l)[g])
                pe.wait_ge(j_d[l], 16)
                for c in range(BK):
                    mm(bank[4 + c][:, 0:T], poolw[:, c, :], ypool[:, c, 0:T], start=True, stop=True
                       ).then_inc(pw_pe[l], 1)
                pe.wait_ge(pw_a[l], 4 * l + BK)
                n = 0
                for o in range(HY_O):
                    for s in range(S):
                        if n:
                            pe.wait_ge(y_z[l], BK * n)
                        for j in range(2):
                            for c in range(BK):
                                last = tp(bank[4 + j][:, c * P:(c + 1) * P],
                                          hv[:, c, s * SEQ + j * P:s * SEQ + (j + 1) * P], ident)
                            last.then_inc(y_tp[l], 1)
                        fill_tiles(fill(l, 0))
                        pe.wait_ge(y_zt[l], 2 * n + 2)
                        for f in (0, 2, 1, 3):
                            for j in range(2):
                                last = mm(bank[f][:], dft_f[:, j, f * P:(f + 1) * P], zt[:, j, :],
                                          start=j == 0, stop=j == 1)
                            last.then_inc(y_f[l], 1)
                        fill_tiles(fill(l, 1))
                        pe.wait_ge(y_m[l], 2 * n + 2)
                        for c in range(BK):
                            for f in range(4):
                                last = mm(bank[4 + c // 2][:, c % 2 * SEQ:(c % 2 + 1) * SEQ],
                                          hy_y[:, f, c * P:(c + 1) * P], dft_i[:, f, :], start=f == 0, stop=f == 3)
                            last.then_inc(y_i[l], 1)
                        fill_tiles(fill(l, 2))
                        n += 1
                pe.wait_ge(j_pe[l], 32)
                pe.nop().then_inc(w_u, 2)
                for i, src in enumerate((qT, kT)):
                    for c in range(BK):
                        u = i * BK + c
                        if u >= 2:
                            pe.wait_ge(r_d[l], 8 * l + u - 1)
                        elif u == 0:
                            pe.wait_ge(y_z[l], 2 * S * BK)
                            pe.wait_ge(j_a[l], 16)
                        mm(bank[6 + u % 2][:, 0:SEQ], perm, src[:, c, 0:SEQ], start=True, stop=True
                           ).then_inc(r_pe[l], 1)
                pe.wait_ge(r_d[l], 8 * l + 8)
                units = units_of[l]
                U = len(units)

                def scores(h):
                    c, p0 = h // 2, (h % 2) * DH
                    rows = slice(p0, p0 + DH)
                    for i, (x, s) in enumerate(units):
                        u = h * U + i
                        if h >= deep[l]:
                            pe.wait_ge(a_ex[l], u - deep[l] * U + 1)
                        b = bank[h % deep[l] * U + i]
                        if s == 0:
                            mm(b[:, 0:SEQ], qrot[rows, c, x * P:(x + 1) * P], krot[rows, c, :], start=True, stop=True)
                            last = mm(b[:, SEQ:NT], qT[rows, c, x * P:(x + 1) * P], kT[rows, c, SEQ:NT],
                                      start=True, stop=True)
                        else:
                            last = mm(b[:, 0:SEQ], qT[rows, c, SEQ + x * P:SEQ + (x + 1) * P], kT[rows, c, SEQ:NT],
                                      start=True, stop=True)
                        last.then_inc(a_sc[l], 1)

                def transposes(h):
                    if h:
                        pe.wait_ge(a_ev[l], (U // 2 + 1) * h)
                    for i, (x, s) in enumerate(units):
                        pe.wait_ge(a_nm[l], h * U + i + 1)
                        for k in range(4 if s == 0 else 2):
                            b = bank[4 + (k // 2 if s == 0 else 2)]
                            col = (k % 2) * SEQ + x * P
                            last = tp(b[:, col:col + P], prob[:, h % deep[l] * U + i, k * P:(k + 1) * P], ident)
                        if x == 1:
                            last.then_inc(a_tr[l], 1)

                def values(h):
                    c, p0 = h // 2, (h % 2) * DH
                    if h:
                        pe.wait_ge(a_o[l], h)
                    pe.wait_ge(a_ev[l], (U // 2 + 1) * (h + 1))
                    o = bank[7][p0:p0 + DH, :]
                    for k in range(4):
                        last = mm(o[:, 0:SEQ], vtok[:, k, h * DH:(h + 1) * DH], pT_s[:, h % 2, k, :],
                                  start=k == 0, stop=k == 3)
                    if S == 2:
                        for k in range(2):
                            last = mm(o[:, SEQ:NT], vtok[:, 2 + k, h * DH:(h + 1) * DH], pT_s[:, h % 2, 4 + k, :],
                                      start=k == 0, stop=k == 1)
                    last.then_inc(a_pv[l], 1)

                for h in range(deep[l]):
                    scores(h)
                for h in range(HEADS):
                    if h + deep[l] < HEADS:
                        scores(h + deep[l])
                    transposes(h)
                    values(h)
                pe.wait_ge(a_o[l], HEADS)
                with pe.Fori(0, 3) as n:
                    for m in range(DK):
                        h, r = divmod(m, 4)
                        b_at = at_of[("merge", l, 3 * h + 1)]
                        bslot = b_at % RS
                        pe.wait_ge(w_l, n * DK + (q0 + 2 * IN_C + m + 1))
                        pe.wait_ge(g_d[l], n * DK + (m + 1))
                        def gate(carry):
                            for k in range(DK):
                                first, last = mm3(bank[m % 2][:, 0:T], w_part(m % WS, k), h_part(k, 0, T),
                                                  k == 0, k == DK - 1)
                                if k == 0 and carry is not None:
                                    first.then_inc(carry, 1)
                            last.then_inc(g_pe[l], 1)

                        def branch(carry):
                            for k in range(BK):
                                last = mm(bank[2 + m % 2][:, 0:T], rview(bslot, 4)[:, k, r * P:(r + 1) * P],
                                          ys[:, bass.ds(n, 1), k, 0:T], start=k == 0, stop=k == BK - 1)
                                if k == 0 and carry is not None:
                                    last.then_inc(carry, 1)
                            last.then_inc(g_pe[l], 1)

                        if r < 3:
                            gate(w_u if m == 4 else None)
                            if r == 0:
                                pe.wait_ge(ring_full[bslot], n * (16 * 6 // RS) + full_at(b_at))
                            branch(w_u)
                        else:
                            branch(None)
                            gate(ring_used)
                    pe.wait_ge(g_pe[l], n * (2 * DK) + (2 * DK))
                    pe.nop().then_inc(w_u, 1)
                for m in range(DK):
                    pe.wait_ge(w_l, q0 + 2 * IN_C + 3 * DK + m + 1)
                    if m >= 2:
                        pe.wait_ge(o_d[l], S * (m - 1))
                    for k in range(DK):
                        if m == 0:
                            pe.wait_ge(h_l, 2 * DK * l + DK + k + 1)
                        first, last = mm3(bank[m % 2][:, 0:T], w_part(m % WS, k), h_part(k, 0, T),
                                          k == 0, k == DK - 1)
                        if k == 0 and m:
                            first.then_inc(w_u, 1)
                    last.then_inc(o_pe[l], 1)
                pe.wait_ge(o_pe[l], DK)
                pe.nop().then_inc(w_u, 1)
                norm_pe(2 * l + 1, T)

                def next_mod(g0, g1):
                    if l + 1 < DEPTH:
                        for g in range(g0, g1):
                            mod(l + 1, g)

                next_mod(0, 1)
                nt = T // P
                for k in range(DK):
                    pe.wait_ge(n_h, (2 * l + 1) * DK + k + 1)
                    last = mm(bank[7][0:E_N, 0:T], wrt[:, k, :], hT[:, k, 0:T], start=k == 0, stop=k == DK - 1)
                last.then_inc(q_lg[l], 1)
                pe.wait_ge(q_ex[l], 2 * l + 1)
                for j in range(nt):
                    last = tp(bank[6][:, j * E_N:(j + 1) * E_N], logit[:, j * P:(j + 1) * P], ident[0:E_N, 0:E_N])
                last.then_inc(q_lg[l], 1)
                for j in range(nt):
                    if j >= 2:
                        pe.wait_ge(t_ev[l], 2 * (j - 1))
                    for i in range(2):
                        for k in range(4):
                            last = tp(bank[2 * (j % 2) + i][:, k * P:(k + 1) * P],
                                      hT[:, 4 * i + k, j * P:(j + 1) * P], ident)
                        last.then_inc(t_pe[l], 1)
                pe.wait_ge(q_m[l], l + 1)
                msk = rt[:, 0, :].rearrange("p (j e) -> p j e", e=E_N)
                for j in range(nt):
                    for i in range(j + 1):
                        mm(bank[7][:, j * E_N:(j + 1) * E_N], tri if i == j else ones, msk[:, i, :],
                           start=i == 0, stop=i == j)
                for i in range(nt):
                    last = mm(bank[7][:, 64:64 + E_N], ones, msk[:, i, :], start=i == 0, stop=i == nt - 1)
                last.then_inc(q_rk[l], 1)
                next_mod(1, 4)
                pe.wait_ge(q_tb[l], 16 * (l + 1))
                tp(bank[6][:, 64:128], ids_f, ident[0:64, 0:64]).then_inc(q_tt[l], 1)
                next_mod(4, 5)
                if l + 1 < DEPTH:
                    pe.wait_ge(m_tk[l + 1], MOD_G * (l + 1) + MOD_EARLY)
                xb = at_of[("exp", l, 0)]
                pe.wait_ge(t_ev[l], 2 * nt)

                def rows_t(par_, e, owed):
                    for i in range(2):
                        for k in range(4):
                            last = tp(bank[i][:, k * P:(k + 1) * P], hg[:, par_, (4 * i + k) * P:(4 * i + k + 1) * P],
                                      ident)
                            if owed and i + k == 0:
                                last.then_inc(ring_used, 1)
                    last.then_inc(x_tr[l], 1)

                def gate_up(par_, s, idx, slots):
                    pe.wait_ge(x_ha[l], 16 * l + s + 1)
                    pe.wait_ge(x_hd[l], 16 * l + s + 1)
                    for w in range(2):
                        for h in range(2):
                            c = 2 * w + h
                            pe.wait_ge(ring_full[(xb + slots[c]) % RS], idx[c])
                            for k in range(4):
                                last = mm(bank[2 + w][:], heT[:, par_, 4 * h + k, :], rview((xb + slots[c]) % RS, 4)[:, k, :],
                                          start=h + k == 0, stop=h == 1 and k == 3)
                            last.then_inc(ring_used if c < 3 else x_gu[l], 1)

                def hidden_t(par_, s, owed):
                    pe.wait_ge(x_hid[l], 16 * l + s + 1)
                    for k in range(FK):
                        last = tp(bank[4][:, k * P:(k + 1) * P], hid[:, par_, k * P:(k + 1) * P], ident)
                        if owed and k == 0:
                            last.then_inc(ring_used, 1)
                    last.then_inc(x_ht[l], 1)

                def down(par_, s, idx, slots, owed):
                    pe.wait_ge(x_hte[l], 16 * l + s + 1)
                    for h in range(2):
                        pe.wait_ge(ring_full[(xb + slots[h]) % RS], idx[h])
                        for k in range(2):
                            for x in range(2):
                                last = mm(bank[5 + x][:], hidT[:, par_, 2 * h + k, :],
                                          rview((xb + slots[h]) % RS, 2)[:, k, x * 512:(x + 1) * 512],
                                          start=h + k == 0, stop=h + k == 2)
                                if owed and h + k + x == 0:
                                    last.then_inc(ring_used, 1)
                        last.then_inc(x_y[l] if h else ring_used, 1)

                def fulls(off):
                    return [full_at(xb + off + i) for i in range(6)]

                for e in range(2):
                    pe.wait_ge(x_g[l][e], 16)
                    if e:
                        pe.wait_ge(x_ha[l], 16 * l + 1)
                        pe.wait_ge(x_hd[l], 16 * l + 1)
                    rows_t(e, e, e == 1)
                    if e == 0:
                        gate_up(0, 0, fulls(0)[0:4], (0, 1, 2, 3))
                        pe.wait_ge(x_gu[l], 16 * l + 1)

                def step(par_, s, i, off, more):
                    f = [i * (16 * 12 // RS) + v for v in fulls(off)]
                    hidden_t(1 - par_, s - 1, False)
                    gate_up(par_, s, f[0:4], (4, 5, 0, 1))
                    down(1 - par_, s - 1, f[4:6], (2, 3), True)
                    if more:
                        pe.wait_ge(x_g[l][1 - par_], 16 * ((s + 1) // 2 + 1) if isinstance(s, int) else
                                   (i * 16 + 32))
                        pe.wait_ge(x_ha[l], 16 * l + s + 1)
                        pe.wait_ge(x_hd[l], 16 * l + s + 1)
                        rows_t(1 - par_, s + 1, True)

                with pe.Fori(0, 7) as i:
                    step(1, 2 * i + 1, i, 4, True)
                    step(0, 2 * i + 2, i, 10, True)
                step(1, 15, 7, 4, False)
                hidden_t(1, 15, True)
                pe.wait_ge(x_ya[l], 16 * l + 15)
                pe.wait_ge(x_yd[l], 16 * l + 15)
                down(1, 15, [full_at(xb + EXP_C - 2), full_at(xb + EXP_C - 1)], (4, 5), False)
                pe.wait_ge(x_y[l], 16 * l + 16)
                pe.nop().then_inc(ring_used, 1)
                pe.wait_ge(q_ix[l], l + 1)
                most = pe.value_load(cnt_u[0:1, 0:1], min_val=0, max_val=NT)
                with pe.If(most > P):
                    pe.nop().then_inc(v_done[l], 1)
                    with pe.Fori(0, (nt - 1) * E_N) as b:
                        pe.wait_ge(v_g[l], b * 16 + 16)
                        for i in range(2):
                            for k in range(4):
                                last = tp(bank[i][:, k * P:(k + 1) * P], hg[:, 0, (4 * i + k) * P:(4 * i + k + 1) * P],
                                          ident)
                        last.then_inc(v_pe[l], 1)
                        pe.wait_ge(v_d[l], b * 6 + 2)
                        pe.wait_ge(v_w[l], b * 32 + 32)
                        for i in range(2):
                            for k in range(DK):
                                last = mm(bank[2 + i][:], heT[:, 0, k, :], over_w[i][:, k * FF:(k + 1) * FF],
                                          start=k == 0, stop=k == DK - 1)
                        last.then_inc(v_pe[l], 1)
                        pe.wait_ge(v_d[l], b * 6 + 4)
                        for k in range(FK):
                            last = tp(bank[4][:, k * P:(k + 1) * P], hid[:, 0, k * P:(k + 1) * P], ident)
                        last.then_inc(v_pe[l], 1)
                        pe.wait_ge(v_d[l], b * 6 + 5)
                        pe.wait_ge(v_wd[l], b * 16 + 16)
                        for i in range(2):
                            for k in range(FK):
                                last = mm(bank[5 + i][:], hidT[:, 0, k, :],
                                          over_w[0][:, k * D + i * 512:k * D + (i + 1) * 512],
                                          start=k == 0, stop=k == FK - 1)
                        last.then_inc(v_pe[l], 1)
                        pe.wait_ge(v_pe[l], b * 4 + 4)
                        pe.nop().then_inc(v_done[l], 1)
                    pe.wait_ge(v_d[l], (nt - 1) * E_N * 6)
                with pe.Else():
                    pe.nop()
                if l + 1 < DEPTH:
                    pe.wait_ge(x_ya[l], 16 * l + E_N)
                    pe.wait_ge(x_yd[l], 16 * l + E_N)
                    for g in range(MOD_EARLY, MOD_MID):
                        mod(l + 1, g)
                    pe.wait_ge(m_tk[l + 1], MOD_G * (l + 1) + MOD_MID)
                pe.wait_ge(z_f[l], nt)
                pe.wait_ge(x_ya[l], 16 * l + E_N)
                pe.wait_ge(x_yd[l], 16 * l + E_N)
                for k in range(DK):
                    for j in range(nt):
                        last = tp(bank[k][:, j * P:(j + 1) * P], fa[:, j, k * P:(k + 1) * P], ident)
                    last.then_inc(z_t[l], 1)
                pe.wait_ge(z_x[l], 16)
            norm_pe(4, SEQ)
            pe.wait_ge(n_h, 5 * DK)
            for j in range(2):
                for i in range(2):
                    for k in range(4):
                        last = tp(bank[2 * j + i][:, k * P:(k + 1) * P], hT[:, 4 * i + k, j * P:(j + 1) * P], ident)
                    last.then_inc(e_t, 1)

        @block.scalar
        def _(act):
            A = nc.scalar.activation

            def norm_act_root(inst, cols, nstream):
                if inst:
                    l = (inst - 1) // 2
                    act.wait_ge(o_d[l] if inst % 2 else z_x[l], 8 * nstream if inst % 2 else 16)
                for k in range(DK):
                    if k >= 2:
                        act.wait_ge(n_mm, inst * DK + k - 1)
                    A(sqb[:, k % 2, 0:cols], xT[:, k, 0:cols], ACT.Square).then_inc(n_sq, 1)
                act.wait_ge(n_a, inst + 1)
                A(nrm[:, 1, 0:cols], nrm[:, 0, 0:cols], ACT.Sqrt).then_inc(n_s, 1)

            def norm_act_scale(inst, cols, nstream):
                for k in range(DK):
                    act.wait_ge(n_x, inst * DK + k + 1)
                    if inst == 4:
                        A(hT[:, k, 0:cols], hT[:, k, 0:cols], ACT.Identity, scale=fin_g[:, k:k + 1]).then_inc(n_h, 1)
                        continue
                    w = inst % 2
                    for s in range(nstream):
                        v = hT[:, k, s * SEQ:(s + 1) * SEQ]
                        last = A(v, v, ACT.Identity, scale=gs[:, w, k, s:s + 1],
                                 bias=mods[:, 3 * w * DK + k, s:s + 1])
                    last.then_inc(n_h, 1)
                    if w == 0:
                        act.wait_ge(n_h, inst * DK + k + 1)
                        A(h_hi[:, k, :], hT[:, k, :], ACT.Copy).then_inc(h_h, 1)

            def norm_act(inst, cols, nstream):
                norm_act_root(inst, cols, nstream)
                norm_act_scale(inst, cols, nstream)

            def mod_rows(l, g):
                act.wait_ge(ring_used, direct_to[at_of[("mod", l, 2 * g + 1)]])
                if g >= 2:
                    act.wait_ge(m_co[l], 12 * l + g - 1)
                A(mrow[:, g % 2, :], mbank(l, g)[:, :], ACT.Copy).then_inc(m_ev[l], 1)

            def mod_take(l, g):
                act.wait_ge(m_co[l], 12 * l + g + 1)
                dst = mods_next if g < MOD_MID else mods
                for m in range(4):
                    last = A(dst[:, 4 * g + m, :], mbank(l, g)[:, 2 * m:2 * m + 2], ACT.Identity,
                             bias=par[l][:, C_BMOD + 4 * g + m:C_BMOD + 4 * g + m + 1])
                last.then_inc(m_tk[l], 1)

            def mod_next(l, g0, g1):
                if l >= DEPTH:
                    return
                for g in range(g0, g1):
                    mod_rows(l, g)
                    if g not in (0, MOD_EARLY, MOD_MID, MOD_LATE):
                        mod_take(l, g - 1)
                    if g + 1 in (MOD_EARLY, MOD_MID, MOD_LATE, MOD_G):
                        mod_take(l, g)

            act.wait_ge(s_ld, 16 * 5)
            A(cc[:, 1, :], cc[:, 0, :], ACT.Exp, scale=-1.0).then_inc(s_ce, 1)
            norm_act_root(0, NT, 2)
            for g in range(MOD_FIRST):
                mod_rows(0, g)
            for l in range(DEPTH):
                T = tcols(l)
                S = streams(l)
                pc = par[l]
                q0 = l * HALVES

                def lead(q, slot, x, raw, full):
                    act.wait_ge(ring_full[raw], full)
                    if not isinstance(q, int) or q >= WS:
                        act.wait_ge(w_u, q - (WS - 1))
                    A(w_hi[:, slot], rview(raw, 8)[:, :, x * P:(x + 1) * P], ACT.Copy).then_inc(w_h, 1)

                def lead_in(q):
                    at = half_at(l, q)
                    lead(q0 + q, q % WS, q % 2, at % RS, full_at(at))

                for q in range(AHEAD):
                    lead_in(q)
                if l:
                    norm_act_root(2 * l, NT, 2)
                    mod_next(l, MOD_MID, MOD_LATE)
                act.wait_ge(m_d[l], 2 * l + 1)
                norm_act_scale(2 * l, NT, 2)
                for g in range(12):
                    lead_in(g + AHEAD)
                    act.wait_ge(j_pe[l], g + 1)
                    dst = hv[:, g, 0:T] if g < 4 else hx[:, (g - 4) // 4, g % 4, 0:T]
                    A(dst, bank[g % 2][:, 0:T], ACT.Identity, scale=pc[:, C_TAP + 12 + g:C_TAP + 13 + g],
                      bias=pc[:, C_SB + g:C_SB + g + 1]).then_inc(j_c[l], 1)
                    if g in (0, 2):
                        act.wait_ge(f_d[l], 8 * l + 1 + g // 2)
                        A(fhid[0:HY_H, 1 + g // 2, :], fhid[0:HY_H, 0, :], ACT.Sin).then_inc(f_a[l], 1)
                    if g in mod_after(l):
                        if l == 0:
                            mod_rows(l, mod_after(l)[g])
                        else:
                            mod_next(l, mod_after(l)[g], mod_after(l)[g] + 1)
                for g in range(12, 16):
                    lead_in(g + AHEAD)
                for c in range(BK):
                    act.wait_ge(pw_pe[l], 4 * l + c + 1)
                    A(ys_pool[:, c, 0:T], bank[4 + c][:, 0:T], ACT.Copy, scale=pc[:, C_PS + c:C_PS + c + 1]
                      ).then_inc(pw_a[l], 1)
                done = [16]

                def take_tiles(n):
                    for g in range(done[0], done[0] + n):
                        if g < 24:
                            lead_in(g + AHEAD)
                        elif g % 4 == 0:
                            for x in range(2):
                                lead_in(26 + (g - 24) // 2 + x)
                        act.wait_ge(j_pe[l], g + 1)
                        b = bank[6 + g % 2]
                        if g < 20:
                            A(qT[:, g - 16, 0:T], b[:, 0:T], ACT.Copy, scale=DH ** -0.5).then_inc(j_a[l], 1)
                        elif g < 24:
                            A(kT[:, g - 20, :], b[:, :], ACT.Copy).then_inc(j_a[l], 1)
                        else:
                            h, j = divmod(g - 24, 4)
                            A(vtok[:, j, h * 256:(h + 1) * 256], b[:, 0:256], ACT.Copy).then_inc(j_a[l], 1)
                    done[0] += n

                for n in range(2 * S):
                    if n:
                        act.wait_ge(y_f[l], 4 * n)
                    for j in range(2):
                        act.wait_ge(y_tp[l], 2 * n + j + 1)
                        A(zt[:, j, :], bank[4 + j][:, :], ACT.Copy).then_inc(y_zt[l], 1)
                    take_tiles(sum(fill(l, w) for w in range(3)))
                units = units_of[l]
                U = len(units)

                def exps(h):
                    for i, (x, s) in enumerate(units):
                        act.wait_ge(a_mx[l], h * U + i + 1)
                        if h >= deep[l]:
                            act.wait_ge(a_tr[l], (U // 2) * (h - deep[l]) + s + 1)
                        w = NT if s == 0 else SEQ
                        v = h % deep[l] * U + i
                        A(prob[:, v, 0:w], bank[v][:, 0:w], ACT.Exp, bias=pstat[:, v, 0:1],
                          accum_out=pstat[:, v, 1:2]).then_inc(a_ex[l], 1)

                def evac(h):
                    act.wait_ge(a_tr[l], (U // 2) * h + 1)
                    if h >= 2:
                        act.wait_ge(a_pv[l], h - 1)
                    A(pT_s[:, h % 2, 0:2, :], bank[4][:, :].rearrange("p (k t) -> p k t", k=2), ACT.Copy
                      ).then_inc(a_ev[l], 1)
                    A(pT_s[:, h % 2, 2:4, :], bank[5][:, :].rearrange("p (k t) -> p k t", k=2), ACT.Copy
                      ).then_inc(a_ev[l], 1)
                    if S == 2:
                        act.wait_ge(a_tr[l], 2 * h + 2)
                        A(pT_s[:, h % 2, 4:6, :], bank[6][:, :].rearrange("p (k t) -> p k t", k=2), ACT.Copy
                          ).then_inc(a_ev[l], 1)

                def attended(h):
                    act.wait_ge(a_pv[l], h + 1)
                    c, p0 = h // 2, (h % 2) * DH
                    A(qT[p0:p0 + DH, c, 0:T], bank[7][p0:p0 + DH, 0:T], ACT.Copy).then_inc(a_o[l], 1)

                act.wait_ge(y_z[l], 2 * S * BK)
                exps(0)
                for h in range(HEADS):
                    if deep[l] == 1:
                        evac(h)
                    if h + 1 < HEADS:
                        exps(h + 1)
                    if deep[l] == 2:
                        evac(h)
                    attended(h)
                act.wait_ge(a_tr[l], HEADS * (U // 2))
                at0 = at_of[("merge", l, 0)]
                with act.Fori(0, 3) as n:
                    for m in range(DK):
                        q = m + AHEAD
                        at = at0 + merge_chunk(q)
                        lead(n * DK + (q0 + 2 * IN_C + q), q % WS, q % 2, at % RS, n * (16 * 6 // RS) + full_at(at))
                        act.wait_ge(g_pe[l], n * (2 * DK) + (2 * m + (2 if m % 4 == 3 else 1)))
                        act.wait_ge(g_d[l], n * DK + (m + 1))
                        A(gate_t[:, m % 2, 0:T], bank[m % 2][:, 0:T], ACT.Tanh, scale=0.5).then_inc(g_t[l], 1)
                act.wait_ge(g_pe[l], 3 * 2 * DK)
                for k in range(DK):
                    act.wait_ge(g_d[l], 2 + 2 * DK + k + 1)
                    A(h_hi[:, k, 0:T], merged[:, k, 0:T], ACT.Copy).then_inc(h_h, 1)
                for m in range(AHEAD, DK):
                    at = at_of[("out", l, m // 2)]
                    lead(q0 + 2 * IN_C + 3 * DK + m, m % WS, m % 2, at % RS, full_at(at))
                norm_act_root(2 * l + 1, T, S)
                mod_next(l + 1, 0, 1)
                act.wait_ge(m_d[l], 2 * l + 2)
                norm_act_scale(2 * l + 1, T, S)
                nt = T // P
                act.wait_ge(q_lg[l], 2 * l + 1)
                A(logit[:, 0:T], bank[7][0:E_N, 0:T], ACT.Copy).then_inc(q_ex[l], 1)
                act.wait_ge(q_lg[l], 2 * l + 2)
                A(rt[:, 1, 0:nt * E_N], bank[6][:, 0:nt * E_N], ACT.Exp, scale=-1.0).then_inc(q_ex[l], 1)
                for j in range(nt):
                    for i in range(2):
                        act.wait_ge(t_pe[l], 2 * j + i + 1)
                        A(htok[:, j, i * 512:(i + 1) * 512], bank[2 * (j % 2) + i][:, :], ACT.Copy
                          ).then_inc(t_ev[l], 1)
                mod_next(l + 1, 1, MOD_EARLY)

                def rows_in(par_, e):
                    act.wait_ge(x_tr[l], 16 * l + e + 1)
                    A(heT[:, par_, 0:4, :], bank[0][:, :].rearrange("p (k t) -> p k t", k=4), ACT.Copy
                      ).then_inc(x_ha[l], 1)

                def tanh(par_, s):
                    act.wait_ge(x_gu[l], 16 * l + s + 1)
                    A(thb[:, par_, :], bank[2][:, :], ACT.Tanh, scale=0.5).then_inc(x_th[l], 1)

                def hid_in(par_, s):
                    act.wait_ge(x_ht[l], 16 * l + s + 1)
                    A(hidT[:, par_, :, :], bank[4][:, :].rearrange("p (k t) -> p k t", k=4), ACT.Copy
                      ).then_inc(x_hte[l], 1)

                def y_out(par_, s, free):
                    act.wait_ge(x_y[l], 16 * l + s + 1)
                    if free is not None:
                        act.wait_ge(x_st[l][par_], free)
                    A(yb[:, par_, 0:512], bank[5][:, :], ACT.Copy).then_inc(x_ya[l], 1)

                rows_in(0, 0)
                tanh(0, 0)
                rows_in(1, 1)
                for s in (1, 2):
                    hid_in((s - 1) % 2, s - 1)
                    tanh(s % 2, s)
                    y_out((s - 1) % 2, s - 1, None)
                    rows_in((s + 1) % 2, s + 1)
                with act.Fori(1, 7) as i:
                    hid_in(0, 2 * i)
                    tanh(1, 2 * i + 1)
                    y_out(0, 2 * i, i * 16)
                    rows_in(0, 2 * i + 2)
                    hid_in(1, 2 * i + 1)
                    tanh(0, 2 * i + 2)
                    y_out(1, 2 * i + 1, i * 16)
                    rows_in(1, 2 * i + 3)
                hid_in(0, 14)
                tanh(1, 15)
                y_out(0, 14, 16 * 7)
                hid_in(1, 15)
                y_out(1, 15, 16 * 7)
                act.wait_ge(q_ix[l], l + 1)
                most = act.value_load(cnt_u[0:1, 0:1], min_val=0, max_val=NT)
                with act.If(most > P):
                    with act.Fori(0, (nt - 1) * E_N) as b:
                        act.wait_ge(v_pe[l], b * 4 + 2)
                        A(thb[:, 0, :], bank[2][:, :], ACT.Tanh, scale=0.5).then_inc(v_a[l], 1)
                with act.Else():
                    act.nop()
                mod_next(l + 1, MOD_EARLY, MOD_MID)
                for j in range(nt):
                    act.wait_ge(z_g[j], 32 * (l + 1))
                    A(fa[:, j, :], fa[:, j, :], ACT.Copy, scale=wsel[:, 0, j:j + 1]).then_inc(z_s[l], 1)
            norm_act(4, SEQ, 1)
            for j in range(2):
                for i in range(2):
                    act.wait_ge(e_t, 2 * j + i + 1)
                    A(htok[:, j, i * 512:(i + 1) * 512], bank[2 * j + i][:, :], ACT.Copy).then_inc(e_c, 1)

        @block.vector
        def _(dve):
            V = nc.vector
            chain = [0]

            def link(ins, n=1):
                chain[0] += n
                ins.then_inc(dve_c, 1)
                dve.wait_ge(dve_c, chain[0])

            def norm_dve(inst, cols):
                norm_dve_root(inst, cols)
                norm_dve_scale(inst, cols)

            def norm_dve_root(inst, cols):
                dve.wait_ge(n_mm, (inst + 1) * DK)
                V.tensor_scalar(nrm[:, 0, 0:cols], bank[7][:, 0:cols], 1.0 / D, EPS, ALU.mult, ALU.add).then_inc(n_a, 1)
                dve.wait_ge(n_s, inst + 1)
                link(V.reciprocal(nrm[:, 2, 0:cols], nrm[:, 1, 0:cols]))
                link(V.tensor_tensor(nrm[:, 3, 0:cols], nrm[:, 2, 0:cols], nrm[:, 2, 0:cols], ALU.mult))
                link(V.scalar_tensor_tensor(nrm[:, 3, 0:cols], nrm[:, 0, 0:cols], -0.5, nrm[:, 3, 0:cols],
                                            ALU.mult, ALU.mult))
                link(V.scalar_tensor_tensor(nrm[:, 1, 0:cols], nrm[:, 3, 0:cols], 1.5, nrm[:, 2, 0:cols],
                                            ALU.add, ALU.mult))

            def norm_dve_scale(inst, cols):
                lag = 2 if inst in (0, 2) else 0
                for k in range(DK + lag):
                    if k < DK:
                        V.tensor_tensor(hT[:, k, 0:cols], xT[:, k, 0:cols], nrm[:, 1, 0:cols], ALU.mult
                                        ).then_inc(n_x, 1)
                    if lag and k >= lag:
                        trail_h(k - lag, 8 * inst, hT, cols)

            def trail_h(k, before, src, cols):
                dve.wait_ge(h_h, before + k + 1)
                V.tensor_tensor(h_lo[:, k, 0:cols], src[:, k, 0:cols], h_hi[:, k, 0:cols].bitcast(F32), ALU.subtract
                                ).then_inc(h_l, 1)

            def mod_take(l, g):
                dve.wait_ge(m_co[l], 12 * l + g + 1)
                V.tensor_tensor(mods[:, 4 * g:4 * g + 4, :],
                                bank[5 + g % 2][:, 0:8].rearrange("p (m s) -> p m s", s=2),
                                par[l][:, C_BMOD + 4 * g:C_BMOD + 4 * g + 4].unsqueeze(2).to_broadcast([P, 4, 2]),
                                ALU.add).then_inc(m_tk[l], 1)

            def gains(l, w):
                for s in range(2):
                    last = V.scalar_tensor_tensor(gs[:, w, :, s], mods[:, (3 * w + 1) * DK:(3 * w + 2) * DK, s], 1.0,
                                                  par[l][:, C_G1 + 8 * w:C_G1 + 8 * w + 8], ALU.add, ALU.mult)
                return last

            def mod_first(l):
                for g in range(MOD_FIRST):
                    mod_take(l, g)
                dve.wait_ge(m_tk[l], 12 * l + MOD_FIRST)
                gains(l, 0).then_inc(m_d[l], 1)

            dve.wait_ge(s_ce, 1)
            link(V.tensor_scalar(cc[:, 2, :], cc[:, 1, :], 1.0, None, ALU.add))
            link(V.reciprocal(cc[:, 1, :], cc[:, 2, :]))
            link(V.memset(csil[:], 0.0))
            V.tensor_tensor(csil[:, :, 0:2], cc[:, 0, :].rearrange("p (k s) -> p k s", s=2),
                            cc[:, 1, :].rearrange("p (k s) -> p k s", s=2), ALU.mult).then_inc(s_cs, 1)
            norm_dve_root(0, NT)
            mod_first(0)
            for l in range(DEPTH):
                T = tcols(l)
                S = streams(l)
                pc = par[l]
                fc = [pc[0:HY_H, C_FILT + i:C_FILT + i + 1] for i in range(3)]

                def angle(i):
                    dve.wait_ge(f_p[l], 8 * l + i + 1)
                    x0, x1 = fhid[0:HY_H, 0, :], fang[0:HY_H, 0, :]
                    if i:
                        dve.wait_ge(f_a[l], 2 * l + 1)
                    link(V.tensor_scalar(x1, bank[2 + i][0:HY_H, 0:SEQ], fc[2 * i], fc[1], ALU.add, ALU.mult))
                    x2 = fang[0:HY_H, 1, :]
                    link(V.tensor_scalar(x2, x1, 1.0 / TWO_PI, 12582912.0, ALU.mult, ALU.add))
                    link(V.tensor_scalar(x2, x2, -12582912.0, None, ALU.add))
                    link(V.scalar_tensor_tensor(x1, x2, -6.28125, x1, ALU.mult, ALU.add))
                    link(V.scalar_tensor_tensor(x1, x2, -0.0019350051879882812, x1, ALU.mult, ALU.add))
                    link(V.scalar_tensor_tensor(x1, x2, -3.0199157663445e-07, x1, ALU.mult, ALU.add))
                    V.tensor_scalar(x0, x1, 3.1415925, -3.1415925, ALU.min, ALU.max).then_inc(f_d[l], 1)

                def taps(o):
                    dve.wait_ge(f_p[l], 8 * l + 3 + 3 * o)
                    for i in range(2):
                        for j in range(2):
                            V.tensor_tensor(fraw[:, i, j, :], fbank[2 * i + j][:, :], decay[:, j, :], ALU.mult
                                            ).then_inc(dve_c, 1)
                    chain[0] += 4
                    dve.wait_ge(dve_c, chain[0])
                    link(V.memset(fraw[0:1, 1, 0, :], 0.0))
                    V.tensor_tensor(fpm[:, 0], fraw[:, 0], fraw[:, 1], ALU.add)
                    link(V.tensor_tensor(fpm[:, 1], fraw[:, 0], fraw[:, 1], ALU.subtract))
                    link(V.scalar_tensor_tensor(fraw[:, 0], fraw[:, 0], -1.0, fraw[:, 0], ALU.mult, ALU.max))
                    link(V.scalar_tensor_tensor(fraw[:, 1], fraw[:, 1], -1.0, fraw[:, 1], ALU.mult, ALU.max))
                    V.tensor_tensor(fabs_, fraw[:, 0], fraw[:, 1], ALU.add).then_inc(f_d[l], 1)

                def normed_a(o):
                    dve.wait_ge(f_p[l], 8 * l + 4 + 3 * o)
                    link(V.reciprocal(fnorm, bank[7][:, :]))
                    V.tensor_tensor(spec[:, o, 0, :], bank[2][:, :], fnorm, ALU.mult)
                    V.tensor_tensor(spec[:, o, 1, :], bank[3][:, :], fnorm, ALU.mult).then_inc(f_d[l], 1)

                def normed_b(o):
                    dve.wait_ge(f_p[l], 8 * l + 5 + 3 * o)
                    V.tensor_tensor(spec[:, o, 2, :], bank[2][:, :], fnorm, ALU.mult)
                    link(V.tensor_tensor(spec[:, o, 3, :], bank[3][:, :], fnorm, ALU.mult))
                    V.tensor_tensor(spec[0:1, o, 2, :], bank[4][0:1, :], fnorm[0:1, :], ALU.mult).then_inc(f_d[l], 1)

                def filter_part(g):
                    if g in (0, 2):
                        angle(g // 2)
                    elif g in (3, 7):
                        taps(g // 7)
                    elif g in (5, 9):
                        normed_a(g // 9)
                    elif g in (6, 10):
                        normed_b(g // 10)

                if l:
                    norm_dve_root(2 * l, NT)
                norm_dve_scale(2 * l, NT)
                for g in range(12):
                    dve.wait_ge(j_c[l], g + 1)
                    dst = hv[:, g, 0:T] if g < 4 else hx[:, (g - 4) // 4, g % 4, 0:T]
                    dst = dst.rearrange("p (s t) -> p s t", t=SEQ)
                    src = bank[g % 2][:, 0:T].rearrange("p (s t) -> p s t", t=SEQ)
                    link(V.scalar_tensor_tensor(dst[:, :, 1:SEQ], src[:, :, 0:SEQ - 1], pc[:, C_TAP + g:C_TAP + g + 1],
                                                dst[:, :, 1:SEQ], ALU.mult, ALU.add))
                    V.scalar_tensor_tensor(dst[:, :, 0:SEQ - 1], src[:, :, 1:SEQ],
                                           pc[:, C_TAP + 24 + g:C_TAP + 25 + g], dst[:, :, 0:SEQ - 1],
                                           ALU.mult, ALU.add).then_inc(j_d[l], 1)
                    filter_part(g)
                    if l == 0 and mod_after(l).get(g, 0) > MOD_FIRST:
                        mod_take(l, mod_after(l)[g] - 1)
                if l == 0:
                    mod_take(l, MOD_G - 1)
                dve.wait_ge(m_tk[l], MOD_G * (l + 1))
                gains(l, 1)
                V.tensor_scalar(half_gate[:], mods[:, 2 * DK:3 * DK, :], 0.5, None, ALU.mult).then_inc(m_d[l], 1)
                link(V.memset(up[:, :, 0:POOL_PAD], 0.0))
                link(V.memset(up[:, :, POOL_PAD + SEQ:POOL_L], 0.0))
                for c in range(BK):
                    dve.wait_ge(j_pe[l], 12 + c + 1)
                    link(V.tensor_copy(up[:, 0:S, POOL_PAD:POOL_PAD + SEQ],
                                       bank[(12 + c) % 4][:, 0:T].rearrange("p (s t) -> p s t", t=SEQ)))
                    lo, hi = 1, POOL_L
                    link(V.tensor_tensor(ps_a[:, 0:S, lo:hi], up[:, 0:S, lo - 1:hi - 1], up[:, 0:S, lo:hi], ALU.add))
                    src, dst = ps_a, ps_b
                    for i in range(c):
                        h = 1 << i
                        lo, hi = lo + h, hi - h
                        link(V.tensor_tensor(dst[:, 0:S, lo:hi], src[:, 0:S, lo - h:hi - h], src[:, 0:S, lo + h:hi + h],
                                             ALU.add))
                        src, dst = dst, src
                    for s in range(S):
                        for x, t in ((0, 0), (8, SEQ - 8)):
                            v = src[:, s, POOL_PAD + t:POOL_PAD + t + 8]
                            link(V.tensor_tensor(v, v, edge[:, c, x:x + 8], ALU.mult))
                    V.scalar_tensor_tensor(ypool[:, c, 0:T].rearrange("p (s t) -> p s t", t=SEQ),
                                           src[:, 0:S, POOL_PAD:POOL_PAD + SEQ], 1.0 / (2 << c),
                                           up[:, 0:S, POOL_PAD:POOL_PAD + SEQ], ALU.mult, ALU.subtract
                                           ).then_inc(j_d[l], 1)
                    dve.wait_ge(j_d[l], 12 + c + 1)
                dve.wait_ge(pw_a[l], 4 * l + BK)
                n = 0
                for o in range(HY_O):
                    for s in range(S):
                        if n:
                            dve.wait_ge(y_i[l], BK * n)
                        for h in range(2):
                            zr, zi = bank[h], bank[2 + h]
                            hr, hi = spec[:, o, h, :], spec[:, o, 2 + h, :]
                            dve.wait_ge(y_f[l], 4 * n + 2 * h + 2)
                            link(V.tensor_tensor(hy_t[:, 0, :], zr[:, :], hr, ALU.mult))
                            link(V.tensor_tensor(hy_t[:, 1, :], zi[:, :], hi, ALU.mult))
                            link(V.tensor_tensor(hy_y[:, h, :], hy_t[:, 0, :], hy_t[:, 1, :], ALU.subtract))
                            link(V.tensor_tensor(hy_t[:, 0, :], zr[:, :], hi, ALU.mult))
                            link(V.tensor_tensor(hy_t[:, 1, :], zi[:, :], hr, ALU.mult))
                            last = V.tensor_tensor(hy_y[:, 2 + h, :], hy_t[:, 0, :], hy_t[:, 1, :], ALU.add)
                            if h == 0:
                                link(last)
                                link(V.tensor_tensor(hy_y[0:1, 0, :], zr[0:1, :], hr[0:1, :], ALU.mult))
                                last = V.tensor_tensor(hy_y[0:1, 2, :], zi[0:1, :], hi[0:1, :], ALU.mult)
                            last.then_inc(y_m[l], 1)
                            dve.wait_ge(y_m[l], 2 * n + h + 1)
                        for c in range(BK):
                            dve.wait_ge(y_i[l], BK * n + c // 2 * 2 + 2)
                            z = hv[:, c, s * SEQ:(s + 1) * SEQ]
                            sk = C_SKIP + o * BK + c
                            link(V.scalar_tensor_tensor(hy_t[:, 0, 0:SEQ], z, pc[:, sk:sk + 1],
                                                        bank[4 + c // 2][:, c % 2 * SEQ:(c % 2 + 1) * SEQ],
                                                        ALU.mult, ALU.add))
                            V.tensor_tensor(z, hy_t[:, 0, 0:SEQ], hx[:, o, c, s * SEQ:(s + 1) * SEQ], ALU.mult
                                            ).then_inc(y_z[l], 1)
                            dve.wait_ge(y_z[l], BK * n + c + 1)
                        n += 1
                dve.wait_ge(r_ld[l], 48 * (l + 1))
                for i, (src, dst) in enumerate(((qT, qrot), (kT, krot))):
                    for c in range(BK):
                        u = i * BK + c
                        dve.wait_ge(r_pe[l], 8 * l + u + 1)
                        link(V.tensor_tensor(rtmp[:, 0, :], bank[6 + u % 2][:, 0:SEQ], rope[:, 1, :], ALU.mult))
                        link(V.tensor_tensor(rtmp[:, 1, :], src[:, c, 0:SEQ], rope[:, 0, :], ALU.mult))
                        V.tensor_tensor(dst[:, c, :], rtmp[:, 0, :], rtmp[:, 1, :], ALU.add).then_inc(r_d[l], 1)
                        dve.wait_ge(r_d[l], 8 * l + u + 1)
                units = units_of[l]
                U = len(units)

                def maxes(h):
                    dve.wait_ge(b_ld[l][h % 2], 16 * (h // 2 + 1))
                    v = bias[:, h % 2]
                    V.tensor_tensor(v, v, colmask.unsqueeze(1).to_broadcast([P, 6, GRID]), ALU.add
                                    ).then_inc(b_fix[l], 1)
                    dve.wait_ge(b_fix[l], h + 1)
                    for i, (x, s) in enumerate(units):
                        dve.wait_ge(a_sc[l], h * U + i + 1)
                        k = h % deep[l] * U + i
                        b = bank[k]
                        w = NT if s == 0 else SEQ
                        if s == 0:
                            k0 = 2 - 2 * x
                            link(V.tensor_tensor(b[:, 0:SEQ].rearrange("p (s j) -> p s j", s=4),
                                                 b[:, 0:SEQ].rearrange("p (s j) -> p s j", s=4),
                                                 v[:, k0:k0 + 4, :], ALU.add))
                        if h >= deep[l]:
                            dve.wait_ge(a_nm[l], (h - deep[l]) * U + i + 1)
                        V.tensor_reduce(pstat[:, k, 0:1], b[:, 0:w], AX.X, ALU.max, negate=True).then_inc(a_mx[l], 1)

                def probs(h):
                    for i, (x, s) in enumerate(units):
                        dve.wait_ge(a_ex[l], h * U + i + 1)
                        w = NT if s == 0 else SEQ
                        k = h % deep[l] * U + i
                        link(V.reciprocal(pstat[:, k, 2:3], pstat[:, k, 1:2]))
                        V.tensor_scalar(prob[:, k, 0:w], prob[:, k, 0:w], pstat[:, k, 2:3], None, ALU.mult
                                        ).then_inc(a_nm[l], 1)

                maxes(0)
                for h in range(HEADS):
                    if deep[l] == 1:
                        probs(h)
                    if h + 1 < HEADS:
                        maxes(h + 1)
                    if deep[l] == 2:
                        probs(h)
                dve.wait_ge(a_o[l], HEADS)
                V.memset(merged, 0.0).then_inc(g_d[l], 2)
                dve.wait_ge(g_d[l], 2)
                with dve.Fori(0, 3) as n:
                    for m in range(DK):
                        dve.wait_ge(g_t[l], n * DK + (m + 1))
                        dve.wait_ge(g_pe[l], n * (2 * DK) + (2 * m + 2))
                        dve.wait_ge(g_d[l], n * DK + (m + 2))
                        V.scalar_tensor_tensor(mtmp[:, 0:T], gate_t[:, m % 2, 0:T], 1.0, bank[2 + m % 2][:, 0:T],
                                               ALU.add, ALU.mult).then_inc(dve_c, 1)
                        dve.wait_ge(dve_c, n * DK + (chain[0] + m + 1))
                        V.tensor_tensor(merged[:, m, 0:T], merged[:, m, 0:T], mtmp[:, 0:T], ALU.add
                                        ).then_inc(g_d[l], 1)
                chain[0] += 3 * DK
                for k in range(DK):
                    trail_h(k, 2 * DK * l + DK, merged, T)
                for m in range(DK):
                    dve.wait_ge(o_pe[l], m + 1)
                    for s in range(S):
                        v = xT[:, m, s * SEQ:(s + 1) * SEQ]
                        V.scalar_tensor_tensor(v, bank[m % 2][:, s * SEQ:(s + 1) * SEQ], half_gate[:, m, s:s + 1], v,
                                               ALU.mult, ALU.add).then_inc(o_d[l], 1)
                dve.wait_ge(o_d[l], 8 * S)
                norm_dve(2 * l + 1, T)
                nt = T // P
                NE = nt * E_N
                G4 = nt * 4

                def r16(i):
                    return rt[:, i, 0:NE]

                def r4(i):
                    return rt[:, i, 0:NE].rearrange("p (g k) -> p g k", k=4)

                def r1(i):
                    return rt[:, i, 0:G4]

                def rje(i):
                    return rt[:, i, 0:NE].rearrange("p (j e) -> p j e", e=E_N)

                dve.wait_ge(q_ex[l], 2 * l + 2)
                link(V.tensor_scalar(r16(2), r16(1), 1.0, None, ALU.add))
                link(V.reciprocal(r16(1), r16(2)))
                link(V.tensor_tensor(rje(2), rje(1), rbias[:].unsqueeze(1).to_broadcast([P, nt, E_N]), ALU.add))

                def place(src, dst, view):
                    v, d = view(src), view(dst)
                    g = v.shape[1]
                    pairs = [wide[:, i, 0:g * 16].rearrange("p (g i j) -> p g i j", i=4, j=4) for i in range(2)]
                    vi = v.unsqueeze(3).to_broadcast([P, g, 4, 4])
                    vj = v.unsqueeze(2).to_broadcast([P, g, 4, 4])
                    V.tensor_tensor(pairs[0], vj, vi, ALU.is_gt).then_inc(dve_c, 1)
                    link(V.tensor_tensor(pairs[1], vj, vi, ALU.is_equal), 2)
                    link(V.tensor_tensor(pairs[1], pairs[1],
                                         earlier[:].rearrange("p (i j) -> p i j", i=4).unsqueeze(1)
                                         .to_broadcast([P, g, 4, 4]), ALU.mult))
                    link(V.tensor_tensor(pairs[0], pairs[0], pairs[1], ALU.add))
                    link(V.tensor_reduce(d, pairs[0], AX.X, ALU.add))

                place(r16(2), r16(3), lambda v: v.rearrange("p (g k) -> p g k", k=4))
                link(V.tensor_scalar(r16(4), r16(3), 1.5, None, ALU.is_lt))
                link(V.tensor_tensor(r16(5), r16(4), r16(2), ALU.mult))
                link(V.tensor_reduce(r1(6), r4(5), AX.X, ALU.add))
                place(r1(6), r1(7), lambda v: v.rearrange("p (j g) -> p j g", g=4))
                link(V.tensor_scalar(r1(8), r1(7), 0.5, None, ALU.is_lt))
                V.tensor_tensor(r4(0), r4(4), r1(8).unsqueeze(2).to_broadcast([P, G4, 4]), ALU.mult
                                ).then_inc(q_m[l], 1)
                dve.wait_ge(q_m[l], l + 1)
                link(V.tensor_tensor(r16(9), r16(0), r16(1), ALU.mult))
                link(V.tensor_reduce(rt[:, 10, 0:nt], rje(9), AX.X, ALU.add))
                link(V.reciprocal(rt[:, 11, 0:nt], rt[:, 10, 0:nt]))
                link(V.tensor_scalar(rt[:, 11, 0:nt], rt[:, 11, 0:nt], 0.5, None, ALU.mult))
                link(V.tensor_tensor(rje(9), rje(9), rt[:, 11, 0:nt].unsqueeze(2).to_broadcast([P, nt, E_N]), ALU.mult))
                dve.wait_ge(q_rk[l], l + 1)
                link(V.tensor_tensor(rje(12), bank[7][:, 0:NE].rearrange("p (j e) -> p j e", e=E_N),
                                     slot0[:].unsqueeze(1).to_broadcast([P, nt, E_N]), ALU.add))
                for i in range(1, nt):
                    link(V.tensor_scalar(rje(18), bank[7][:, 0:NE].rearrange("p (j e) -> p j e", e=E_N),
                                         float(i * P), float((E_N - 1) * P), ALU.is_ge, ALU.mult))
                    link(V.tensor_tensor(r16(12), r16(12), r16(18), ALU.add))
                link(V.scalar_tensor_tensor(r16(12), r16(12), 1.0, r16(0), ALU.add, ALU.mult))
                link(V.tensor_reduce(rt[:, 13, 0:nt], rje(12), AX.X, ALU.max))
                link(V.tensor_reduce(rt[:, 14, 0:nt], rje(12), AX.X, ALU.add))
                link(V.tensor_tensor(rt[:, 14, 0:nt], rt[:, 14, 0:nt], rt[:, 13, 0:nt], ALU.subtract))
                link(V.tensor_scalar(didx[:, 0, 0:nt], rt[:, 14, 0:nt], -1.0, None, ALU.add))
                link(V.tensor_scalar(didx[:, 1, 0:nt], rt[:, 13, 0:nt], -1.0, None, ALU.add))
                link(V.tensor_reduce(rt[:, 15, 0:1], bank[7][:, 64:64 + E_N], AX.X, ALU.max))
                V.tensor_copy(cnt_u[:], rt[:, 15, 0:1]).then_inc(q_ix[l], 1)
                link(V.tensor_tensor(rje(16), rje(12), rt[:, 13, 0:nt].unsqueeze(2).to_broadcast([P, nt, E_N]),
                                     ALU.is_equal))
                link(V.tensor_tensor(r16(16), r16(16), r16(9), ALU.mult))
                link(V.tensor_reduce(wsel[:, 1, 0:nt], rje(16), AX.X, ALU.add))
                link(V.tensor_reduce(rt[:, 17, 0:nt], rje(9), AX.X, ALU.add))
                link(V.tensor_tensor(wsel[:, 0, 0:nt], rt[:, 17, 0:nt], wsel[:, 1, 0:nt], ALU.subtract))
                dve.wait_ge(q_tt[l], l + 1)
                V.tensor_copy(tidx[:], bank[6][:, 64:128]).then_inc(q_ti[l], 1)

                def rows_in(par_, e):
                    dve.wait_ge(x_tr[l], 16 * l + e + 1)
                    V.tensor_copy(heT[:, par_, 4:8, :], bank[1][:, :].rearrange("p (k t) -> p k t", k=4)
                                  ).then_inc(x_hd[l], 1)

                def hidden(par_, s):
                    dve.wait_ge(x_th[l], 16 * l + s + 1)
                    V.scalar_tensor_tensor(thb[:, par_, :], thb[:, par_, :], 1.0, bank[2][:, :], ALU.add, ALU.mult
                                           ).then_inc(x_th2[l], 1)
                    dve.wait_ge(x_th2[l], 16 * l + s + 1)
                    V.tensor_tensor(hid[:, par_, :], thb[:, par_, :], bank[3][:, :], ALU.mult).then_inc(x_hid[l], 1)

                def y_out(par_, s, free):
                    dve.wait_ge(x_y[l], 16 * l + s + 1)
                    if free is not None:
                        dve.wait_ge(x_st[l][par_], free)
                    V.tensor_copy(yb[:, par_, 512:1024], bank[6][:, :]).then_inc(x_yd[l], 1)

                rows_in(0, 0)
                hidden(0, 0)
                rows_in(1, 1)
                for s in (1, 2):
                    hidden(s % 2, s)
                    y_out((s - 1) % 2, s - 1, None)
                    rows_in((s + 1) % 2, s + 1)
                with dve.Fori(1, 7) as i:
                    hidden(1, 2 * i + 1)
                    y_out(0, 2 * i, i * 16)
                    rows_in(0, 2 * i + 2)
                    hidden(0, 2 * i + 2)
                    y_out(1, 2 * i + 1, i * 16)
                    rows_in(1, 2 * i + 3)
                hidden(1, 15)
                y_out(0, 14, 16 * 7)
                y_out(1, 15, 16 * 7)
                most = dve.value_load(cnt_u[0:1, 0:1], min_val=0, max_val=NT)
                with dve.If(most > P):
                    for i in range(2):
                        dve.wait_ge(x_st[l][i], 16 * E_N // 2)
                    with dve.Fori(0, (nt - 1) * E_N) as b:
                        V.tensor_copy(over_idx[:], tidx[:, bass.ds(b + E_N, 1)]).then_inc(v_d[l], 1)
                        dve.wait_ge(v_pe[l], b * 4 + 1)
                        V.tensor_copy(heT[:, 0, 0:4, :], bank[0][:, :].rearrange("p (k t) -> p k t", k=4))
                        V.tensor_copy(heT[:, 0, 4:8, :], bank[1][:, :].rearrange("p (k t) -> p k t", k=4)
                                      ).then_inc(v_d[l], 1)
                        dve.wait_ge(v_a[l], b + 1)
                        V.scalar_tensor_tensor(thb[:, 0, :], thb[:, 0, :], 1.0, bank[2][:, :], ALU.add, ALU.mult
                                               ).then_inc(v_d[l], 1)
                        dve.wait_ge(v_d[l], b * 6 + 3)
                        V.tensor_tensor(hid[:, 0, :], thb[:, 0, :], bank[3][:, :], ALU.mult).then_inc(v_d[l], 1)
                        dve.wait_ge(v_pe[l], b * 4 + 3)
                        V.tensor_copy(hidT[:, 0, :, :], bank[4][:, :].rearrange("p (k t) -> p k t", k=4)
                                      ).then_inc(v_d[l], 1)
                        dve.wait_ge(v_pe[l], b * 4 + 4)
                        V.tensor_copy(yb[:, 0, 0:512], bank[5][:, :])
                        V.tensor_copy(yb[:, 0, 512:1024], bank[6][:, :]).then_inc(v_d[l], 1)
                with dve.Else():
                    dve.nop()
                for j in range(nt):
                    dve.wait_ge(z_s[l], (4 * l) + j + 1)
                    V.scalar_tensor_tensor(fa[:, j, :], fb[:, j, :], wsel[:, 1, j:j + 1], fa[:, j, :],
                                           ALU.mult, ALU.add).then_inc(z_f[l], 1)
                for k in range(DK):
                    dve.wait_ge(z_t[l], k + 1)
                    for s in range(S):
                        v = xT[:, k, s * SEQ:(s + 1) * SEQ]
                        V.scalar_tensor_tensor(v, bank[k][:, s * SEQ:(s + 1) * SEQ], mods[:, 5 * DK + k, s:s + 1], v,
                                               ALU.mult, ALU.add).then_inc(z_x[l], 2 // S)
                dve.wait_ge(z_x[l], 16)
                if l + 1 < DEPTH:
                    dve.wait_ge(m_tk[l + 1], MOD_G * (l + 1) + MOD_MID)
                    link(V.tensor_copy(mods[:, 0:4 * MOD_MID, :], mods_next[:, 0:4 * MOD_MID, :]))
                    gains(l + 1, 0).then_inc(m_d[l + 1], 1)
            norm_dve(4, SEQ)


def shape_constants():
    import numpy as np
    n = SEQ
    t = np.arange(n, dtype=np.float64)
    f = np.arange(n, dtype=np.float64)
    ang = 2 * np.pi * np.outer(t, f) / (2 * n)
    cos, sin = np.cos(ang), np.sin(ang)
    alt = (-1.0) ** t
    fwd = np.concatenate([cos, -sin], axis=1)
    fwd[:, n] = alt
    inv = np.concatenate([2 * cos.T, -2 * sin.T], axis=0) / (2 * n)
    inv[0] = 1.0 / (2 * n)
    inv[n] = alt / (2 * n)
    c = {}
    c["dft_f"] = fwd.reshape(2, P, 512).transpose(1, 0, 2)
    c["dft_i"] = inv.reshape(4, P, n).transpose(1, 0, 2)
    c["sel2"] = (np.arange(P)[:, None] % 32 == np.arange(2)[None, :])
    c["nyq"] = alt.reshape(2, P).T
    ident = np.eye(P)
    perm = np.zeros((P, P))
    for m in range(P):
        if m % 64 < 32:
            perm[m + 32, m] = -1.0
        else:
            perm[m - 32, m] = 1.0
    tri = np.triu(np.ones((P, P)), 1)
    c["square"] = np.stack([ident, perm, tri, np.ones((P, P))], axis=1)
    nf = DH // 4
    inv_f = (10000.0 ** (-np.arange(nf, dtype=np.float32) / nf)).astype(np.float32)
    row = (np.arange(n) // GRID).astype(np.float32)
    col = (np.arange(n) % GRID).astype(np.float32)
    an = np.concatenate([row[:, None] * inv_f, col[:, None] * inv_f], axis=-1)
    idx = np.arange(P) % 32
    c["rope"] = np.stack([np.cos(an)[:, idx].T, np.sin(an)[:, idx].T], axis=1)
    j = np.arange(GRID)
    st = np.clip(j - KW // 2, 0, GRID - KW)
    ok = (j[None, :] >= st[:, None]) & (j[None, :] < st[:, None] + KW)
    c["colmask"] = np.tile(np.where(ok, 0.0, -1e30), (2, 1))
    edge = np.ones((BK, 16))
    for g in range(BK):
        w = 2 << g
        for x in range(16):
            tt = x if x < 8 else n - 16 + x
            edge[g, x] = w / (min(tt + w - w // 2, n) - max(tt - w // 2, 0))
    c["edge"] = np.broadcast_to(edge, (P, BK, 16))
    c["earlier"] = np.broadcast_to(np.tril(np.ones((4, 4)), -1).reshape(16), (P, 16))
    c["slot0"] = np.broadcast_to(np.arange(E_N) * P, (P, E_N))
    c["tok_id"] = np.arange(4)[None, :] * P + np.arange(P)[:, None]
    tl = np.linspace(0.0, 1.0, n, dtype=np.float32)
    bands = (HY_E - 1) // 2
    fr = np.linspace(1e-4, bands - 1, bands, dtype=np.float32)
    an = np.float32(2.0 * np.pi / n) * np.arange(n, dtype=np.float32)
    z = np.concatenate([tl[:, None], np.cos(fr[None, :] * an[:, None]), -np.sin(fr[None, :] * an[:, None])], axis=-1)
    c["filter_in"] = z.T
    lo, hi = np.log(1e-2) / 0.3, np.log(1e-2) / 1.5
    deltas = np.abs(np.linspace(lo, hi, BW, dtype=np.float32))
    c["decay"] = np.exp(-tl[:, None] * deltas).reshape(2, P, BW).transpose(1, 0, 2)
    return {k: np.ascontiguousarray(v, dtype=np.float32) for k, v in c.items()}


def kernel(x, c, ctx, c_ctx, norm1_g, norm2_g, w_mod, b_mod, w_in, rpb, pool_w, pool_scale,
           hy_short_w, hy_short_b, hy_w1, hy_b1, hy_freq, hy_w2, hy_b2, hy_w3, hy_skip,
           w_branch, w_out, w_router, router_bias, w_gate_e, w_up_e, w_down_e, final_g):
    import numpy as np
    import concourse.bacc as bacc
    from concourse.bass_utils import run_bass_kernel_spmd

    def cols(v):
        return np.asarray(v).reshape(-1, P).T

    data = dict(shape_constants())
    tokens = np.concatenate([np.asarray(x)[0], np.asarray(ctx)[0]], axis=0)
    data["x_cols"] = tokens.T.reshape(DK, P, NT).transpose(1, 0, 2)
    data["c_cols"] = np.stack([cols(np.asarray(c)[0]), cols(c_ctx)], axis=2).reshape(P, DK * 2)
    for l in range(DEPTH):
        filt = np.zeros((P, 3), np.float32)
        filt[0:HY_H, 0] = hy_b1[l]
        filt[0:HY_H, 1] = hy_freq[l]
        filt[0:HY_H, 2] = hy_b2[l]
        data[f"par{l}"] = np.concatenate(
            [cols(norm1_g[l]), cols(norm2_g[l]), cols(b_mod[l]), cols(pool_scale[l])]
            + [cols(hy_short_w[l, i]) for i in range(NTAP)] + [cols(hy_short_b[l])]
            + [cols(hy_skip[l, i]) for i in range(HY_O)] + [filt], axis=1)
    pad = np.zeros((DEPTH, HEADS, 15, 128), np.float32)
    pad[:, :, :, 63 - (KW - 1):63 + KW] = rpb
    r, q, slot, k = np.ix_(range(2), range(GRID), range(6), range(GRID))
    data["rpb_win"] = pad[:, :, 5 - r + slot, 63 + k - q].reshape(DEPTH, HEADS, P, 6, GRID)
    data["fin_g"] = cols(final_g)
    data["w_router"] = np.asarray(w_router).reshape(DK, P, E_N).transpose(1, 0, 2)
    data["router_bias"] = np.broadcast_to(np.asarray(router_bias), (P, E_N))
    for name, v in (("w_mod", w_mod), ("w_in", w_in), ("pool_w", pool_w), ("hy_w1", hy_w1), ("hy_w2", hy_w2),
                    ("hy_w3", hy_w3), ("w_branch", w_branch), ("w_out", w_out), ("w_gate_e", w_gate_e),
                    ("w_up_e", w_up_e), ("w_down_e", w_down_e)):
        data[name] = v
    nc = bacc.Bacc("TRN2", target_bir_lowering=False, num_devices=1)
    arrays, aps = {}, {}
    for name, v in data.items():
        v = np.ascontiguousarray(v)
        arrays[f"in_{name}"] = v
        aps[name] = nc.dram_tensor(f"in_{name}", v.shape, mybir.dt.from_np(v.dtype), kind="ExternalInput").ap()
    out = nc.dram_tensor("out", (1, SEQ, D), F32, kind="ExternalOutput").ap()
    build(nc, aps, out)
    r = run_bass_kernel_spmd(nc, [arrays], core_ids=[0])
    return r.results[0]["out"]
```
